# Optimizing a Trainium2 kernel written in Bass

```python
import jax
import jax.numpy as jnp
from jax import lax
import numpy as np
import math

D_MODEL = 1024
BATCH = 1
SEQ = 256
DEPTH = 1

HEAD_DIM = 64
RWKV_HEADS = 8
RWKV_WIDTH = RWKV_HEADS * HEAD_DIM
MOBA_HEADS = 8
MOBA_WIDTH = MOBA_HEADS * HEAD_DIM
DECAY_LORA = 64
AAA_LORA = 64
GATE_LORA = 160
MOBA_BLOCK = 256
MOBA_TOPK = 3
Q_CHUNK = 64
ROT_DIM = HEAD_DIM // 4
ROPE_THETA = 500000.0
D_FF = 2816
CONV_WIDTH = 3
NORM_EPS = 1e-6
GN_EPS = 64e-5
N_BRANCH = 2
RWKV_IN = 3 * RWKV_WIDTH + DECAY_LORA + AAA_LORA + GATE_LORA
MOBA_IN = 3 * MOBA_WIDTH
GATE_IN = N_BRANCH * D_MODEL
IN_COLS = RWKV_IN + MOBA_IN + GATE_IN


def rms_norm(x, g):
    xf = x.astype(jnp.float32)
    y = xf * lax.rsqrt(jnp.mean(xf * xf, axis=-1, keepdims=True) + NORM_EPS)
    return (y * g.astype(jnp.float32)).astype(x.dtype)

def shift_right(z):
    return jnp.pad(z, ((0, 0), (1, 0), (0, 0)))[:, :-1]

def partial_rope(x, positions):
    half = ROT_DIM // 2
    inv_freq = ROPE_THETA ** (-jnp.arange(half, dtype=jnp.float32) / half)
    ang = positions.astype(jnp.float32)[..., None] * inv_freq
    cos = jnp.cos(ang)[:, :, None, :]
    sin = jnp.sin(ang)[:, :, None, :]
    xr = x[..., :ROT_DIM].astype(jnp.float32)
    x1, x2 = xr[..., :half], xr[..., half:]
    rot = jnp.concatenate([x1 * cos - x2 * sin, x2 * cos + x1 * sin], axis=-1)
    return jnp.concatenate([rot.astype(x.dtype), x[..., ROT_DIM:]], axis=-1)

def rwkv7_time_mix(z, w_decay_up, decay_bias, w_aaa_up, aaa_bias, w_gate_up,
                   k_k, k_a, r_k, ln_g, ln_b):
    B, S, _ = z.shape
    H, N, C = RWKV_HEADS, HEAD_DIM, RWKV_WIDTH
    f32 = jnp.float32
    o3 = 3 * C
    o4 = o3 + DECAY_LORA
    o5 = o4 + AAA_LORA
    r, k, v = z[..., :C], z[..., C:2 * C], z[..., 2 * C:o3]
    xw, xa, xg = z[..., o3:o4], z[..., o4:o5], z[..., o5:]
    w_log = -jax.nn.softplus(-(decay_bias + jnp.tanh(xw) @ w_decay_up)) - 0.5
    decay = jnp.exp(-jnp.exp(w_log.astype(f32)))
    a = jax.nn.sigmoid(aaa_bias + xa @ w_aaa_up)
    g = jax.nn.sigmoid(xg) @ w_gate_up
    kk = (k * k_k).astype(f32).reshape(B, S, H, N)
    kk = kk / jnp.maximum(jnp.sqrt(jnp.sum(kk * kk, axis=-1, keepdims=True)), 1e-12)
    k = k * (1.0 + (a - 1.0) * k_a)

    def time_major(t):
        return t.astype(f32).reshape(B, S, H, N).transpose(1, 0, 2, 3)

    kk_t = kk.transpose(1, 0, 2, 3)
    inputs = (time_major(r), time_major(decay), time_major(k), time_major(v),
              -kk_t, kk_t * time_major(a))

    def step(state, inp):
        r_t, w_t, k_t, v_t, a_t, b_t = inp
        sa = jnp.einsum('bhvk,bhk->bhv', state, a_t)
        state = (state * w_t[:, :, None, :] + sa[..., None] * b_t[:, :, None, :]
                 + v_t[..., None] * k_t[:, :, None, :])
        return state, jnp.einsum('bhvk,bhk->bhv', state, r_t)

    state0 = jnp.zeros((B, H, N, N), f32)
    _, y = lax.scan(step, state0, inputs)
    y = y.transpose(1, 0, 2, 3)
    mu = jnp.mean(y, axis=-1, keepdims=True)
    var = jnp.mean(jnp.square(y - mu), axis=-1, keepdims=True)
    y = ((y - mu) * lax.rsqrt(var + GN_EPS)).reshape(B, S, C)
    y = y * ln_g.astype(f32) + ln_b.astype(f32)
    rh = r.astype(f32).reshape(B, S, H, N)
    kh = k.astype(f32).reshape(B, S, H, N)
    vh = v.astype(f32).reshape(B, S, H, N)
    bonus = (jnp.sum(rh * kh * r_k.astype(f32), axis=-1, keepdims=True) * vh).reshape(B, S, C)
    return ((y + bonus) * g.astype(f32)).astype(z.dtype)

def moba_attention(q, k, v):
    B, S, H, Dh = q.shape
    f32 = jnp.float32
    n_blk = -(-S // MOBA_BLOCK)
    S_pad = n_blk * MOBA_BLOCK
    pad = ((0, 0), (0, S_pad - S), (0, 0), (0, 0))
    qt = jnp.pad(q, pad).transpose(0, 2, 1, 3)
    kt = jnp.pad(k, pad).transpose(0, 2, 1, 3)
    vt = jnp.pad(v, pad).transpose(0, 2, 1, 3)
    kb = kt.reshape(B, H, n_blk, MOBA_BLOCK, Dh)
    vb = vt.reshape(B, H, n_blk, MOBA_BLOCK, Dh)
    k_mean = jnp.mean(kb.astype(f32), axis=3)
    gate = jnp.einsum('bhsd,bhnd->bhsn', qt.astype(f32), k_mean)
    q_blk = jnp.arange(S_pad) // MOBA_BLOCK
    past = jnp.arange(n_blk)[None, :] < q_blk[:, None]
    gate = jnp.where(past, gate, -jnp.inf)
    n_sel = min(MOBA_TOPK, n_blk)
    _, sel = lax.top_k(gate, n_sel)
    slot_ok = jnp.arange(n_sel)[None, :] < q_blk[:, None]
    b_idx = jnp.arange(B)[:, None, None, None]
    h_idx = jnp.arange(H)[None, :, None, None]
    scale = Dh ** -0.5
    q_off = jnp.arange(Q_CHUNK)
    k_off = jnp.arange(MOBA_BLOCK)
    n_keys_sel = n_sel * MOBA_BLOCK

    def attend_chunk(c):
        start = c * Q_CHUNK
        blk = start // MOBA_BLOCK
        q_c = lax.dynamic_slice_in_dim(qt, start, Q_CHUNK, axis=2)
        sel_c = lax.dynamic_slice_in_dim(sel, start, Q_CHUNK, axis=2)
        ok_c = lax.dynamic_slice_in_dim(slot_ok, start, Q_CHUNK, axis=0)
        k_sel = kb[b_idx, h_idx, sel_c]
        v_sel = vb[b_idx, h_idx, sel_c]
        k_own = lax.dynamic_index_in_dim(kb, blk, axis=2, keepdims=False)
        v_own = lax.dynamic_index_in_dim(vb, blk, axis=2, keepdims=False)
        s_sel = jnp.einsum('bhqd,bhqnkd->bhqnk', q_c, k_sel, preferred_element_type=f32) * scale
        s_sel = jnp.where(ok_c[None, None, :, :, None], s_sel, -jnp.inf)
        s_own = jnp.einsum('bhqd,bhkd->bhqk', q_c, k_own, preferred_element_type=f32) * scale
        causal = (blk * MOBA_BLOCK + k_off)[None, :] <= (start + q_off)[:, None]
        s_own = jnp.where(causal, s_own, -jnp.inf)
        s_all = jnp.concatenate([s_sel.reshape(B, H, Q_CHUNK, n_keys_sel), s_own], axis=-1)
        p = jax.nn.softmax(s_all, axis=-1).astype(v.dtype)
        p_sel = p[..., :n_keys_sel].reshape(B, H, Q_CHUNK, n_sel, MOBA_BLOCK)
        p_own = p[..., n_keys_sel:]
        o = (jnp.einsum('bhqnk,bhqnkd->bhqd', p_sel, v_sel, preferred_element_type=f32)
             + jnp.einsum('bhqk,bhkd->bhqd', p_own, v_own, preferred_element_type=f32))
        return o.astype(v.dtype)

    out = lax.map(attend_chunk, jnp.arange(S_pad // Q_CHUNK))
    out = out.transpose(1, 0, 3, 2, 4).reshape(B, S_pad, H * Dh)
    return out[:, :S]

def conv_ffn(h, w_up, conv_w, conv_b, w_down):
    u = h @ w_up
    a, b = u[..., :D_FF], u[..., D_FF:]
    a = lax.conv_general_dilated(
        a, conv_w.reshape(CONV_WIDTH, 1, D_FF), window_strides=(1,),
        padding=[(CONV_WIDTH - 1, 0)], dimension_numbers=('NWC', 'WIO', 'NWC'),
        feature_group_count=D_FF) + conv_b
    return (jax.nn.gelu(a, approximate=False) * b) @ w_down

def first_inputs(seed: int = 0) -> dict:
    key = jax.random.key(seed)
    ks = iter(jax.random.split(key, 32))
    L = DEPTH
    f32 = jnp.float32

    def nrm(shape, scale):
        return jax.random.normal(next(ks), shape, f32) * scale

    def unif(shape, lo, hi):
        return jax.random.uniform(next(ks), shape, f32, lo, hi)

    x = nrm((BATCH, SEQ, D_MODEL), 1.0)
    positions = jnp.broadcast_to(jnp.arange(SEQ, dtype=jnp.int32), (BATCH, SEQ))
    return {
        'x': x,
        'positions': positions,
        'norm1_g': 1.0 + nrm((L, D_MODEL), 0.02),
        'w_in': nrm((L, D_MODEL, IN_COLS), D_MODEL ** -0.5),
        'rwkv_mu': unif((L, RWKV_IN), 0.0, 1.0),
        'w_decay_up': nrm((L, DECAY_LORA, RWKV_WIDTH), 0.5 * DECAY_LORA ** -0.5),
        'decay_bias': unif((L, RWKV_WIDTH), -6.5, -1.5),
        'w_aaa_up': nrm((L, AAA_LORA, RWKV_WIDTH), 0.5 * AAA_LORA ** -0.5),
        'aaa_bias': nrm((L, RWKV_WIDTH), 0.1),
        'w_gate_up': nrm((L, GATE_LORA, RWKV_WIDTH), GATE_LORA ** -0.5),
        'rwkv_k_k': 0.85 + nrm((L, RWKV_WIDTH), 0.05),
        'rwkv_k_a': 1.0 + nrm((L, RWKV_WIDTH), 0.05),
        'rwkv_r_k': nrm((L, RWKV_HEADS, HEAD_DIM), 0.1),
        'rwkv_ln_g': 1.0 + nrm((L, RWKV_WIDTH), 0.02),
        'rwkv_ln_b': nrm((L, RWKV_WIDTH), 0.02),
        'q_norm_g': 1.0 + nrm((L, HEAD_DIM), 0.02),
        'k_norm_g': 1.0 + nrm((L, HEAD_DIM), 0.02),
        'w_branch_a': nrm((L, RWKV_WIDTH, D_MODEL), RWKV_WIDTH ** -0.5),
        'w_branch_b': nrm((L, MOBA_WIDTH, D_MODEL), MOBA_WIDTH ** -0.5),
        'w_out': nrm((L, D_MODEL, D_MODEL), D_MODEL ** -0.5),
        'norm2_g': 1.0 + nrm((L, D_MODEL), 0.02),
        'w_ffn_up': nrm((L, D_MODEL, 2 * D_FF), D_MODEL ** -0.5),
        'ffn_conv_w': nrm((L, CONV_WIDTH, D_FF), CONV_WIDTH ** -0.5),
        'ffn_conv_b': nrm((L, D_FF), 0.02),
        'w_ffn_down': nrm((L, D_FF, D_MODEL), D_FF ** -0.5),
    }

def first_block(x, positions, norm1_g, w_in, rwkv_mu, w_decay_up, decay_bias, w_aaa_up,
              aaa_bias, w_gate_up, rwkv_k_k, rwkv_k_a, rwkv_r_k, rwkv_ln_g, rwkv_ln_b,
              q_norm_g, k_norm_g, w_branch_a, w_branch_b, w_out, norm2_g, w_ffn_up,
              ffn_conv_w, ffn_conv_b, w_ffn_down):
    B, S, _ = x.shape
    for l in range(DEPTH):
        h = rms_norm(x, norm1_g[l])
        proj = h @ w_in[l]
        z_rwkv = proj[..., :RWKV_IN]
        z_moba = proj[..., RWKV_IN:RWKV_IN + MOBA_IN]
        gate_pre = proj[..., RWKV_IN + MOBA_IN:]
        z_rwkv = z_rwkv + rwkv_mu[l] * (shift_right(z_rwkv) - z_rwkv)
        y_a = rwkv7_time_mix(z_rwkv, w_decay_up[l], decay_bias[l], w_aaa_up[l], aaa_bias[l],
                             w_gate_up[l], rwkv_k_k[l], rwkv_k_a[l], rwkv_r_k[l],
                             rwkv_ln_g[l], rwkv_ln_b[l])
        q = z_moba[..., :MOBA_WIDTH].reshape(B, S, MOBA_HEADS, HEAD_DIM)
        k = z_moba[..., MOBA_WIDTH:2 * MOBA_WIDTH].reshape(B, S, MOBA_HEADS, HEAD_DIM)
        v = z_moba[..., 2 * MOBA_WIDTH:].reshape(B, S, MOBA_HEADS, HEAD_DIM)
        q = partial_rope(rms_norm(q, q_norm_g[l]), positions)
        k = partial_rope(rms_norm(k, k_norm_g[l]), positions)
        y_b = moba_attention(q, k, v)
        u_a = y_a @ w_branch_a[l]
        u_b = y_b @ w_branch_b[l]
        g_a = jax.nn.sigmoid(gate_pre[..., :D_MODEL])
        g_b = jax.nn.sigmoid(gate_pre[..., D_MODEL:])
        x = x + (g_a * u_a + g_b * u_b) @ w_out[l]
        h2 = rms_norm(x, norm2_g[l])
        x = x + conv_ffn(h2, w_ffn_up[l], ffn_conv_w[l], ffn_conv_b[l], w_ffn_down[l])
    return x


DEPTH_2 = 2

CHUNK = 64
Q_BLOCK = 128
N_MIXERS = 2
N_HEADS = 16
D_ATT = N_HEADS * HEAD_DIM
SSM_GROUP = 16
D_SSM = D_MODEL
N_GROUPS = D_SSM // SSM_GROUP
STATE = 64
_FF_RAW = -(-8 * D_MODEL // 3)
D_FF_2 = -(-_FF_RAW // 256) * 256
N_FOX = (DEPTH_2 + 1) // 2
N_S5 = DEPTH_2 // 2
EPS = 1e-6
DT_MIN = 1e-3
DT_MAX = 1e-1


def rmsnorm(x, gain):
    xf = x.astype(jnp.float32)
    y = xf * lax.rsqrt(jnp.mean(xf * xf, axis=-1, keepdims=True) + EPS)
    return (y * gain.astype(jnp.float32)).astype(x.dtype)

def fox_mixer(h, w_in, b_f, q_gain, k_gain, w_out):
    bsz, seq_len, _ = h.shape
    proj = h @ w_in
    q = proj[..., :D_ATT]
    k = proj[..., D_ATT:2 * D_ATT]
    v = proj[..., 2 * D_ATT:3 * D_ATT]
    gate = proj[..., 3 * D_ATT:4 * D_ATT]
    f_logit = proj[..., 4 * D_ATT:]

    def heads(t):
        return t.reshape(bsz, seq_len, N_HEADS, HEAD_DIM).transpose(0, 2, 1, 3)

    q = rmsnorm(heads(q), q_gain)
    k = rmsnorm(heads(k), k_gain)
    v = heads(v)
    log_f = jax.nn.log_sigmoid(f_logit.astype(jnp.float32) + b_f.astype(jnp.float32))
    c = jnp.cumsum(log_f, axis=1).transpose(0, 2, 1)
    scale = HEAD_DIM ** -0.5

    outs = []
    for blk in range(seq_len // Q_BLOCK):
        q0 = blk * Q_BLOCK
        k_end = q0 + Q_BLOCK
        qb = q[:, :, q0:k_end]
        kb = k[:, :, :k_end]
        vb = v[:, :, :k_end]
        s = jnp.einsum('bhqd,bhkd->bhqk', qb, kb).astype(jnp.float32) * scale
        s = s + c[:, :, q0:k_end, None] - c[:, :, None, :k_end]
        q_pos = q0 + jnp.arange(Q_BLOCK)
        mask = q_pos[:, None] >= jnp.arange(k_end)[None, :]
        s = jnp.where(mask, s, -jnp.inf)
        p = jax.nn.softmax(s, axis=-1).astype(vb.dtype)
        outs.append(jnp.einsum('bhqk,bhkd->bhqd', p, vb))
    o = jnp.concatenate(outs, axis=2)
    o = o.transpose(0, 2, 1, 3).reshape(bsz, seq_len, D_ATT)
    o = o * jax.nn.sigmoid(gate)
    return o @ w_out

def _complex_linear_combine(e1, e2):
    a1r, a1i, b1r, b1i = e1
    a2r, a2i, b2r, b2i = e2
    return (a2r * a1r - a2i * a1i,
            a2r * a1i + a2i * a1r,
            a2r * b1r - a2i * b1i + b2r,
            a2r * b1i + a2i * b1r + b2i)

def s5_mixer(h, w_in, log_dt, lam_re, lam_im, b_re, b_im, c_re, c_im, d_skip, w_glu, w_out):
    f32 = jnp.float32
    bsz, seq_len, _ = h.shape
    u = (h @ w_in).astype(f32)
    lam_re = lam_re.astype(f32)
    lam_im = lam_im.astype(f32)
    dt = jnp.exp(log_dt.astype(f32))[:, None]
    mag = jnp.exp(lam_re * dt)
    a_re = mag * jnp.cos(lam_im * dt)
    a_im = mag * jnp.sin(lam_im * dt)
    den = lam_re * lam_re + lam_im * lam_im
    n_re = a_re - 1.0
    z_re = (n_re * lam_re + a_im * lam_im) / den
    z_im = (a_im * lam_re - n_re * lam_im) / den
    b_re = b_re.astype(f32)
    b_im = b_im.astype(f32)
    bb_re = z_re[..., None] * b_re - z_im[..., None] * b_im
    bb_im = z_re[..., None] * b_im + z_im[..., None] * b_re
    c_re = c_re.astype(f32)
    c_im = c_im.astype(f32)

    n_chunks = seq_len // CHUNK
    u_chunks = u.reshape(bsz, n_chunks, CHUNK, N_GROUPS, SSM_GROUP).transpose(1, 0, 2, 3, 4)

    def step(carry, u_c):
        s_re, s_im = carry
        bu_re = jnp.einsum('gpc,bkgc->bkgp', bb_re, u_c)
        bu_im = jnp.einsum('gpc,bkgc->bkgp', bb_im, u_c)
        bu_re = bu_re.at[:, 0].add(a_re * s_re - a_im * s_im)
        bu_im = bu_im.at[:, 0].add(a_re * s_im + a_im * s_re)
        a_seq_re = jnp.broadcast_to(a_re, bu_re.shape)
        a_seq_im = jnp.broadcast_to(a_im, bu_im.shape)
        _, _, x_re, x_im = lax.associative_scan(
            _complex_linear_combine, (a_seq_re, a_seq_im, bu_re, bu_im), axis=1)
        y = (jnp.einsum('gcp,bkgp->bkgc', c_re, x_re)
             - jnp.einsum('gcp,bkgp->bkgc', c_im, x_im))
        return (x_re[:, -1], x_im[:, -1]), y

    init = (jnp.zeros((bsz, N_GROUPS, STATE), f32), jnp.zeros((bsz, N_GROUPS, STATE), f32))
    _, y = lax.scan(step, init, u_chunks)
    y = y.transpose(1, 0, 2, 3, 4).reshape(bsz, seq_len, D_SSM)
    y = y + d_skip.astype(f32) * u
    y = jax.nn.gelu(y).astype(h.dtype)
    y = y * jax.nn.sigmoid(y @ w_glu)
    return y @ w_out

def swiglu(h, w_gate, w_up, w_down):
    return (jax.nn.silu(h @ w_gate) * (h @ w_up)) @ w_down

def second_inputs(seed: int = 0) -> dict:
    key = jax.random.key(seed)
    ks = jax.random.split(key, 24)
    f32 = jnp.float32

    def nrm(k, shape, scale):
        return jax.random.normal(k, shape, f32) * scale

    def gain(k, shape):
        return 1.0 + 0.02 * jax.random.normal(k, shape, f32)

    x = jax.random.normal(ks[0], (BATCH, SEQ, D_MODEL), f32)
    fox_w_in = nrm(ks[1], (N_FOX, D_MODEL, 4 * D_ATT + N_HEADS), D_MODEL ** -0.5)
    fox_b_f = jax.random.uniform(ks[2], (N_FOX, N_HEADS), f32, minval=1.0, maxval=5.0)
    fox_q_gain = gain(ks[3], (N_FOX, HEAD_DIM))
    fox_k_gain = gain(ks[4], (N_FOX, HEAD_DIM))
    fox_w_out = nrm(ks[5], (N_FOX, D_ATT, D_MODEL), D_ATT ** -0.5)
    s5_w_in = nrm(ks[6], (N_S5, D_MODEL, D_SSM), D_MODEL ** -0.5)
    s5_log_dt = jax.random.uniform(ks[7], (N_S5, N_GROUPS), f32,
                                   minval=math.log(DT_MIN), maxval=math.log(DT_MAX))
    s5_lam_re = -0.5 + 0.01 * jax.random.normal(ks[8], (N_S5, N_GROUPS, STATE), f32)
    s5_lam_im = (math.pi * jnp.arange(STATE, dtype=f32)
                 + 0.01 * jax.random.normal(ks[9], (N_S5, N_GROUPS, STATE), f32))
    s5_b_re = nrm(ks[10], (N_S5, N_GROUPS, STATE, SSM_GROUP), (2 * SSM_GROUP) ** -0.5)
    s5_b_im = nrm(ks[11], (N_S5, N_GROUPS, STATE, SSM_GROUP), (2 * SSM_GROUP) ** -0.5)
    s5_c_re = nrm(ks[12], (N_S5, N_GROUPS, SSM_GROUP, STATE), (2 * STATE) ** -0.5)
    s5_c_im = nrm(ks[13], (N_S5, N_GROUPS, SSM_GROUP, STATE), (2 * STATE) ** -0.5)
    s5_d = nrm(ks[14], (N_S5, D_SSM), 1.0)
    s5_w_glu = nrm(ks[15], (N_S5, D_SSM, D_SSM), D_SSM ** -0.5)
    s5_w_out = nrm(ks[16], (N_S5, D_SSM, D_MODEL), D_SSM ** -0.5)
    mix_pre_gain = gain(ks[17], (DEPTH_2, D_MODEL))
    mix_post_gain = gain(ks[18], (DEPTH_2, D_MODEL))
    ffn_pre_gain = gain(ks[19], (DEPTH_2, D_MODEL))
    ffn_post_gain = gain(ks[20], (DEPTH_2, D_MODEL))
    ffn_w_gate = nrm(ks[21], (DEPTH_2, D_MODEL, D_FF_2), D_MODEL ** -0.5)
    ffn_w_up = nrm(ks[22], (DEPTH_2, D_MODEL, D_FF_2), D_MODEL ** -0.5)
    ffn_w_down = nrm(ks[23], (DEPTH_2, D_FF_2, D_MODEL), D_FF_2 ** -0.5)
    return {
        'x': x,
        'fox_w_in': fox_w_in, 'fox_b_f': fox_b_f, 'fox_q_gain': fox_q_gain,
        'fox_k_gain': fox_k_gain, 'fox_w_out': fox_w_out,
        's5_w_in': s5_w_in, 's5_log_dt': s5_log_dt, 's5_lam_re': s5_lam_re,
        's5_lam_im': s5_lam_im, 's5_b_re': s5_b_re, 's5_b_im': s5_b_im,
        's5_c_re': s5_c_re, 's5_c_im': s5_c_im, 's5_d': s5_d,
        's5_w_glu': s5_w_glu, 's5_w_out': s5_w_out,
        'mix_pre_gain': mix_pre_gain, 'mix_post_gain': mix_post_gain,
        'ffn_pre_gain': ffn_pre_gain, 'ffn_post_gain': ffn_post_gain,
        'ffn_w_gate': ffn_w_gate, 'ffn_w_up': ffn_w_up, 'ffn_w_down': ffn_w_down,
    }

def second_block(x, fox_w_in, fox_b_f, fox_q_gain, fox_k_gain, fox_w_out,
              s5_w_in, s5_log_dt, s5_lam_re, s5_lam_im, s5_b_re, s5_b_im,
              s5_c_re, s5_c_im, s5_d, s5_w_glu, s5_w_out,
              mix_pre_gain, mix_post_gain, ffn_pre_gain, ffn_post_gain,
              ffn_w_gate, ffn_w_up, ffn_w_down):
    for i in range(DEPTH_2):
        j = i // N_MIXERS
        h = rmsnorm(x, mix_pre_gain[i])
        if i % N_MIXERS == 0:
            m = fox_mixer(h, fox_w_in[j], fox_b_f[j], fox_q_gain[j], fox_k_gain[j], fox_w_out[j])
        else:
            m = s5_mixer(h, s5_w_in[j], s5_log_dt[j], s5_lam_re[j], s5_lam_im[j],
                         s5_b_re[j], s5_b_im[j], s5_c_re[j], s5_c_im[j], s5_d[j],
                         s5_w_glu[j], s5_w_out[j])
        x = x + rmsnorm(m, mix_post_gain[i])
        h = rmsnorm(x, ffn_pre_gain[i])
        x = x + rmsnorm(swiglu(h, ffn_w_gate[i], ffn_w_up[i], ffn_w_down[i]), ffn_post_gain[i])
    return x


def setup_inputs(seed=0):
    out = dict(first_inputs(seed))
    for name, value in second_inputs(seed + 1).items():
        if name != "x":
            out[name + "_2"] = value
    return out


def reference(
    x, positions, norm1_g, w_in, rwkv_mu, w_decay_up, decay_bias, w_aaa_up, aaa_bias, w_gate_up,
    rwkv_k_k, rwkv_k_a, rwkv_r_k, rwkv_ln_g, rwkv_ln_b, q_norm_g, k_norm_g, w_branch_a,
    w_branch_b, w_out, norm2_g, w_ffn_up, ffn_conv_w, ffn_conv_b, w_ffn_down, fox_w_in_2,
    fox_b_f_2, fox_q_gain_2, fox_k_gain_2, fox_w_out_2, s5_w_in_2, s5_log_dt_2, s5_lam_re_2,
    s5_lam_im_2, s5_b_re_2, s5_b_im_2, s5_c_re_2, s5_c_im_2, s5_d_2, s5_w_glu_2, s5_w_out_2,
    mix_pre_gain_2, mix_post_gain_2, ffn_pre_gain_2, ffn_post_gain_2, ffn_w_gate_2, ffn_w_up_2,
    ffn_w_down_2,
):
    x = first_block(
        x, positions, norm1_g, w_in, rwkv_mu, w_decay_up, decay_bias, w_aaa_up, aaa_bias,
        w_gate_up, rwkv_k_k, rwkv_k_a, rwkv_r_k, rwkv_ln_g, rwkv_ln_b, q_norm_g, k_norm_g,
        w_branch_a, w_branch_b, w_out, norm2_g, w_ffn_up, ffn_conv_w, ffn_conv_b, w_ffn_down,
    )
    return second_block(
        x, fox_w_in_2, fox_b_f_2, fox_q_gain_2, fox_k_gain_2, fox_w_out_2, s5_w_in_2,
        s5_log_dt_2, s5_lam_re_2, s5_lam_im_2, s5_b_re_2, s5_b_im_2, s5_c_re_2, s5_c_im_2,
        s5_d_2, s5_w_glu_2, s5_w_out_2, mix_pre_gain_2, mix_post_gain_2, ffn_pre_gain_2,
        ffn_post_gain_2, ffn_w_gate_2, ffn_w_up_2, ffn_w_down_2,
    )


_drawn_inputs = setup_inputs


def setup_inputs(seed=0):
    import zlib

    import numpy as np

    out = dict(_drawn_inputs(seed))
    spreads = {}
    factors = {'w_decay_up': 5.408,
     'rwkv_ln_g': 5.681,
     'rwkv_ln_b': 4.033,
     'q_norm_g': 8.0,
     'k_norm_g': 8.0,
     'ffn_conv_b': 3.472,
     'fox_q_gain_2': 4.602,
     'fox_k_gain_2': 4.59,
     's5_lam_re_2': 8.0,
     's5_c_re_2': 2.684,
     's5_c_im_2': 2.681,
     'mix_post_gain_2': 2.981,
     'ffn_pre_gain_2': 2.71,
     'ffn_post_gain_2': 3.9}
    for name, (base, spread) in spreads.items():
        noise = np.random.default_rng([zlib.crc32(name.encode()), seed]).standard_normal(out[name].shape)
        drawn = base * np.exp(spread * noise) if base else spread * noise
        out[name] = jnp.asarray(drawn.astype(out[name].dtype))
    for name, factor in factors.items():
        out[name] = (out[name] * factor).astype(out[name].dtype)
    return out
```

```python
from contextlib import ExitStack

import numpy as np

import concourse.bass as bass
from concourse import mybir

ALU = mybir.AluOpType
ACT = mybir.ActivationFunctionType
F32 = mybir.dt.float32
F32R = mybir.dt.float32r
BF16 = mybir.dt.bfloat16
I32 = mybir.dt.int32
AX = mybir.AxisListType.X

P = 128
S = 256
D = 1024
FF = 2816
NR = 6
NS = 4
LOOK = 2
MAGIC = 12582912.0
RSQ = 0x5F3759DF - (1 << 31)
E05 = float(np.exp(np.float32(-0.5)))


def stream_plan():
    plan = [("mq", 8, 512), ("mk", 8, 512), ("mv", 8, 512)]
    plan += [("wr", 8, 512), ("wk", 8, 512), ("wv", 8, 512), ("wl", 8, 288)]
    plan += [(f"g{i}", 8, 512) for i in range(4)]
    for c in range(2):
        plan += [(f"ba{c}", 4, 512), (f"bb{c}", 4, 512)]
    plan += [("wo0", 8, 512), ("wo1", 8, 512)]
    for i in range(5):
        plan += [(f"ua{i}", 8, 512), (f"ub{i}", 8, 512)]
    plan += [("ut", 8, 512)]
    plan += [("dn0", 22, 512), ("dn1", 22, 512)]
    plan += [(f"fq{i}", 8, 512) for i in range(2)] + [(f"fk{i}", 8, 512) for i in range(2)]
    plan += [(f"fv{i}", 8, 512) for i in range(2)] + [(f"fg{i}", 8, 512) for i in range(2)]
    plan += [("fo0", 8, 512), ("fo1", 8, 512)]
    for l in range(2):
        if l == 1:
            plan += [(f"si{i}", 8, 512) for i in range(2)]
            plan += [(f"sg{i}", 8, 512) for i in range(2)]
            plan += [(f"so{i}", 8, 512) for i in range(2)]
        for i in range(5):
            plan += [(f"{l}ug{i}", 8, 512), (f"{l}uu{i}", 8, 512)]
        plan += [(f"{l}ut", 8, 512)]
        plan += [(f"{l}dn0", 22, 512), (f"{l}dn1", 22, 512)]
    return plan


VEC_TILES = [
    ("norm1_g", 8), ("rwkv_mu", 15), ("decay_bias", 4), ("aaa_bias", 4), ("k_k", 4), ("k_a", 4), ("r_k", 4),
    ("ln_g", 4), ("ln_b", 4), ("norm2_g", 8), ("conv_w0", 22), ("conv_w1", 22), ("conv_w2", 22), ("conv_b", 22),
    ("b_f", 1), ("log_dt", 32), ("lam_re", 32), ("lam_im", 32), ("d_skip", 8), ("mix_pre", 16), ("ffn_pre", 16),
]
VEC_AT = {}
_n = 0
for _name, _k in VEC_TILES:
    VEC_AT[_name] = _n
    _n += _k
NVEC = _n

CON = [("ident", 128), ("bones", 128), ("lev0", 128), ("levs", 768), ("mask4", 512), ("iota", 128), ("invf", 8)]
CON_AT = {}
_n = 0
for _name, _k in CON:
    CON_AT[_name] = _n
    _n += _k
NCON = _n


class Queue:

    def __init__(self, sem):
        self.sem, self.n, self.items = sem, 0, []

    def __call__(self, fn, *waits, sig=True):
        self.items.append((fn, list(flat(waits)), sig))
        if sig:
            self.n += 1
        return (self.sem, self.n)

    def play(self, eng):
        seen = {}
        for fn, waits, sig in self.items:
            for s, v in waits:
                if seen.get(id(s), 0) < v:
                    eng.wait_ge(s, v)
                    seen[id(s)] = v
            ins = fn()
            if sig:
                ins.then_inc(self.sem, 1)


def flat(waits):
    for w in waits:
        if w is None:
            continue
        if isinstance(w, list):
            yield from flat(w)
        else:
            yield w


class Bank:

    def __init__(self, t):
        self.t, self.free, self.held = t, [], False


class Acts:

    def __init__(self, hi, lo):
        self.hi, self.lo, self.tok = hi, lo, {}


def program(nc, A, out):
    ctx = ExitStack()
    with ctx:
        def sem(name):
            return ctx.enter_context(nc.semaphore(name))

        def sb(name, shape, dt=F32, stack=None):
            return (stack or ctx).enter_context(nc.sbuf_tensor(name, shape, dt))

        pe, act, dve, pool = (Queue(sem("s_" + n)) for n in ("pe", "act", "dve", "pool"))
        sp_items = []
        dma_sems = {}

        def dma(dst, src, s, *waits):
            dma_sems[s] = dma_sems.get(s, 0) + 16
            sp_items.append((lambda: nc.sync.dma_start(dst, src), list(flat(waits)), s))
            return (s, dma_sems[s])

        V, G, T = nc.vector, nc.gpsimd, nc.tensor

        raw = [sb(f"raw{i}", [P, 1024]) for i in range(NR)]
        whi = [sb(f"whi{i}", [P, 1024], F32R) for i in range(NS)]
        wlo = [sb(f"wlo{i}", [P, 1024], F32R) for i in range(NS)]
        x = sb("x", [P, 2, D])
        h = sb("h", [P, 2, D])
        a_hi = sb("a_hi", [P, 8, S], F32R)
        a_lo = sb("a_lo", [P, 8, S], F32R)
        vec = sb("vec", [P, NVEC])
        con = sb("con", [P, NCON])
        maskw = sb("maskw", [P, 3 * P], mybir.dt.int16)
        maskb = maskw[:, :].bitcast(BF16).rearrange("p (a s) -> p a s", a=3)
        eps = sb("eps", [P, 4])
        st = sb("st", [P, 64])
        nt = sb("nt", [P, 4, 64])
        wps = [Bank(ctx.enter_context(nc.psum_tensor(f"wps{i}", [P, 512], F32))) for i in range(4)]
        tps = [Bank(ctx.enter_context(nc.psum_tensor(f"tps{i}", [P, 512], F32))) for i in range(4)]

        s_raw = [sem(f"s_raw{i}") for i in range(NR)]
        s_x, s_con, s_misc = sem("s_x"), sem("s_con"), sem("s_misc")
        s_gain = [sem("s_gain0"), sem("s_gain1")]
        s_out = sem("s_out")

        def vcol(name, i=0, rows=P):
            return vec[0:rows, VEC_AT[name] + i:VEC_AT[name] + i + 1]

        def vcols(name, n):
            return vec[:, VEC_AT[name]:VEC_AT[name] + n]

        def const(name, n):
            return con[:, CON_AT[name]:CON_AT[name] + n]

        ident = const("ident", P)
        bones = const("bones", P)

        q_x = [dma(x[:, j, :], A["x"][j * P:(j + 1) * P, :], s_x) for j in range(2)][-1]
        q_con = dma(con[:, :], A["con"], s_con)
        q_con = dma(vec[:, :], A["vec"], s_con)
        q_con = dma(maskw[:, :], A["mask"], s_con)
        q_eps = [pool(lambda i=i, v=v: G.memset(eps[:, i:i + 1], v)) for i, v in enumerate((1e-6, 64e-5, 1.0, 0.0))]

        plan = stream_plan()
        slabs = []
        for name, nk, w in plan:
            for kp in range(nk // 2):
                slabs.append((name, kp, w))
        load_tok, split_tok, used_tok = {}, {}, {}
        at = {"load": 0, "split": 0, "use": 0}

        def load_next():
            n = at["load"]
            if n >= len(slabs):
                return
            at["load"] += 1
            name, kp, w = slabs[n]
            load_tok[n] = dma(raw[n % NR][:, 0:2 * w], A["w_" + name][kp], s_raw[n % NR], split_tok.get(n - NR))

        def split_next():
            n = at["split"]
            if n >= len(slabs):
                return
            at["split"] += 1
            w = 2 * slabs[n][2]
            r, hi, lo = raw[n % NR][:, 0:w], whi[n % NS][:, 0:w], wlo[n % NS][:, 0:w]
            q = act(lambda: nc.scalar.activation(hi, r, ACT.Copy), load_tok[n], used_tok.get(n - NS))
            split_tok[n] = dve(lambda: V.tensor_tensor(lo, r, hi.bitcast(F32), ALU.subtract), q)
            load_next()

        for _ in range(NR):
            load_next()

        wpair = [0]
        pending = []

        def stream(name, nk, acts):
            i = wpair[0]
            wpair[0] ^= 1
            banks = wps[2 * i:2 * i + 2]
            toks = [None, None]
            for kp in range(nk // 2):
                n = at["use"]
                nm, kk, w = slabs[n]
                assert (nm, kk) == (name, kp), (nm, kk, name, kp)
                while at["split"] <= min(n + LOOK, len(slabs) - 1):
                    split_next()
                hi, lo = whi[n % NS], wlo[n % NS]
                for sub in range(2):
                    k = 2 * kp + sub
                    wh, wl = hi[:, sub * w:(sub + 1) * w], lo[:, sub * w:(sub + 1) * w]
                    for j in range(2):
                        o = banks[j].t[:, 0:w]
                        xh, xl = acts.hi[:, k, j * P:(j + 1) * P], acts.lo[:, k, j * P:(j + 1) * P]
                        first, last = k == 0, k == nk - 1
                        dep = (split_tok[n], acts.tok[k]) + ((banks[j].free,) if first else ())
                        pe(lambda o=o, xh=xh, wh=wh, f=first: T.matmul(o, xh, wh, start=f, stop=False), *dep, sig=False)
                        pe(lambda o=o, xl=xl, wh=wh: T.matmul(o, xl, wh, start=False, stop=False), sig=False)
                        done = last or (sub == 1 and j == 1)
                        t = pe(lambda o=o, xh=xh, wl=wl, l=last: T.matmul(o, xh, wl, start=False, stop=l), sig=done)
                        if last:
                            toks[j] = t
                used_tok[n] = t
                at["use"] += 1
                if kp == min(1, nk // 2 - 1):
                    while pending:
                        pending.pop(0)()
                yield
            return banks, toks

        def whole(gen):
            while True:
                try:
                    next(gen)
                except StopIteration as e:
                    return e.value

        fillers = []

        def fill(n=1):
            for _ in range(n):
                while fillers:
                    try:
                        next(fillers[0])
                        break
                    except StopIteration:
                        fillers.pop(0)

        def finish():
            while fillers:
                fill()

        def bank():
            for _ in range(4):
                b = tps.pop(0)
                tps.append(b)
                if not b.held:
                    return b
            raise ValueError("no bank")

        def transpose(o, i, n, *waits, sig=False):
            return pe(lambda: T.transpose(o, i, ident[0:n, 0:n]), *waits, sig=sig)

        def rsqrt(dst, src, n, scale, add, *waits):
            m, xh, t = nt[:, 0, 0:n], nt[:, 1, 0:n], nt[:, 2, 0:n]
            y = nt[:, 3, 0:n]
            q = dve(lambda: V.tensor_scalar(m, src, scale, add, ALU.mult, ALU.add), *waits)
            q2 = dve(lambda: V.tensor_scalar(xh, src, scale * 0.5, add * 0.5, ALU.mult, ALU.add), *waits)
            q = dve(lambda: V.tensor_scalar(t.bitcast(I32), m.bitcast(I32), 1, None, ALU.logical_shift_right), q)
            q = dve(lambda: V.tensor_scalar(y.bitcast(I32), t.bitcast(I32), -1.0, float(RSQ), ALU.mult, ALU.add), q)
            for s in range(3):
                o = dst if s == 2 else y
                q = dve(lambda: V.tensor_tensor(t, y, y, ALU.mult), q)
                q = dve(lambda: V.tensor_tensor(t, t, xh, ALU.mult), q, q2)
                q = dve(lambda o=o: V.scalar_tensor_tensor(o, t, 1.5, y, ALU.subtract, ALU.mult), q)
            return q

        def to_acts(src, ready, acts, nk, gain=None, k0=0, wait_free=()):
            for kb in range(nk // 2):
                b = bank()
                for sub in range(2):
                    for j in range(2):
                        o = b.t[:, sub * S + j * P:sub * S + (j + 1) * P]
                        i = src[:, j, (2 * kb + sub) * P:(2 * kb + sub + 1) * P]
                        q = transpose(o, i, P, ready[j], b.free, q_con, sig=(sub == 1 and j == 1))
                k = k0 + 2 * kb
                if gain is None:
                    o3 = b.t[:, :].rearrange("p (k s) -> p k s", k=2)
                    hi, lo = acts.hi[:, k:k + 2, :], acts.lo[:, k:k + 2, :]
                    qh = act(lambda hi=hi, o3=o3: nc.scalar.activation(hi, o3, ACT.Copy), q, *wait_free)
                    ql = dve(lambda hi=hi, lo=lo, o3=o3: V.tensor_tensor(lo, o3, hi.bitcast(F32), ALU.subtract), qh)
                    acts.tok[k] = acts.tok[k + 1] = ql
                else:
                    for sub in range(2):
                        o = b.t[:, sub * S:(sub + 1) * S]
                        hi, lo, g = acts.hi[:, k + sub, :], acts.lo[:, k + sub, :], gain(k + sub)
                        qh = act(lambda hi=hi, o=o, g=g: nc.scalar.activation(hi, o, ACT.Copy, scale=g), q, *wait_free)
                        if sub == 1:
                            pass
                        acts.tok[k + sub] = qh
                    for sub in range(2):
                        o = b.t[:, sub * S:(sub + 1) * S]
                        hi, lo, g = acts.hi[:, k + sub, :], acts.lo[:, k + sub, :], gain(k + sub)
                        ql = dve(lambda hi=hi, lo=lo, o=o, g=g: V.scalar_tensor_tensor(
                            lo, o, g, hi.bitcast(F32), ALU.mult, ALU.subtract), qh)
                        acts.tok[k + sub] = ql
                b.free = [ql]

        main = Acts(a_hi[:, :, :], a_lo[:, :, :])

        def prenorm(ready, gname, g0):
            qs = []
            for j in range(2):
                qs.append(act(lambda j=j: nc.scalar.activation(h[:, j, :], x[:, j, :], ACT.Square,
                                                               accum_out=st[:, j:j + 1]), ready[j]))
            q = rsqrt(st[:, 2:4], st[:, 0:2], 2, 1.0 / D, 1e-6, qs)
            qh = [act(lambda: nc.scalar.activation(h[:, 0, :], x[:, 0, :], ACT.Copy, scale=st[:, 2:3]), q),
                  dve(lambda: V.tensor_scalar(h[:, 1, :], x[:, 1, :], st[:, 3:4], None, ALU.mult), q)]
            to_acts(h, qh, main, 8, gain=lambda k: vcol(gname, g0 + k))
            return qh

        prenorm([q_x, q_x], "norm1_g", 0)

        s1 = ExitStack()
        arena = sb("arena", [P, 101 * 256], F32, s1)

        def view(kb, n):
            at0 = int(round(kb * 256))
            return arena[:, at0:at0 + n]

        yb = view(0, 1024).rearrange("p (j c) -> p j c", j=2)
        gates = view(4, 4096).rearrange("p (j c) -> p j c", j=2)
        mq = view(4, 1024).rearrange("p (j c) -> p j c", j=2)
        mk = view(8, 1024).rearrange("p (j c) -> p j c", j=2)
        mqT = view(12, 1024).rearrange("p (t s) -> p t s", t=4)
        mkT = view(16, 1024).rearrange("p (t s) -> p t s", t=4)
        mv = view(20, 1024).rearrange("p (j c) -> p j c", j=2)
        prob = [view(24, 384), view(25.5, 384)]
        probT = [view(27, 384), view(28.5, 384)]
        sq = view(30, 512)
        rt = view(32, 512).rearrange("p (a n) -> p a n", a=4)
        qkg = sb("qkg", [P, 4, 64], F32, s1)
        posi = sb("posi", [P, 2], I32, s1)
        rope = sb("rope", [P, 6, 2, 8], F32, s1)
        q_m = [dma(qkg[:, :, :], A["qkg"], s_misc), dma(posi[:, :], A["posi"], s_misc)][-1]

        posf, ang, trn = rope[:, 0, :, 0], rope[:, 1, :, :], rope[:, 2, :, :]
        rsin, rcos, tmp8 = rope[:, 3, :, :], rope[:, 4, :, :], rope[:, 5, :, :]
        invf = const("invf", 8)
        q = dve(lambda: V.tensor_copy(posf, posi[:, :]), q_m)
        qa = [dve(lambda j=j: V.tensor_scalar(ang[:, j, :], invf, posf[:, j:j + 1], None, ALU.mult), q, q_con) for j in range(2)]
        q = dve(lambda: V.tensor_scalar(trn, ang, float(1 / (2 * np.pi)), MAGIC, ALU.mult, ALU.add), qa)
        q = dve(lambda: V.tensor_scalar(trn, trn, MAGIC, None, ALU.subtract), q)
        q2 = dve(lambda: V.scalar_tensor_tensor(ang, trn, -6.28125, ang, ALU.mult, ALU.add), q)
        q = dve(lambda: V.scalar_tensor_tensor(ang, trn, -float(2 * np.pi - 6.28125), ang, ALU.mult, ALU.add), q2)
        q = dve(lambda: V.tensor_scalar(ang, ang, 3.1415925, -3.1415925, ALU.min, ALU.max), q)
        q2 = dve(lambda: V.scalar_tensor_tensor(tmp8, ang, -1.0, ang, ALU.mult, ALU.max), q)
        q2 = dve(lambda: V.tensor_scalar(tmp8, tmp8, -1.0, float(np.pi / 2), ALU.mult, ALU.add), q2)
        q = act(lambda: nc.scalar.activation(rsin, ang, ACT.Sin), q)
        q_rope = act(lambda: nc.scalar.activation(rcos, tmp8, ACT.Sin), q2)
        q_qg = dve(lambda: V.tensor_scalar(qkg[:, 0:3:2, :], qkg[:, 0:3:2, :], 0.125, None, ALU.mult), q_m)

        def heads(ap, n):
            return ap.rearrange("p (h d) -> p h d", h=n)

        def wide(ap, n):
            return ap.unsqueeze(2).to_broadcast([ap.shape[0], ap.shape[1], n])

        def take_heads(banks, toks, dst, c0, ss, scratch):
            out_t = []
            for j in range(2):
                b = banks[j]
                q1 = act(lambda j=j, b=b: nc.scalar.activation(dst[:, j, c0:c0 + 512], b.t[:, :], ACT.Copy), toks[j])
                b.free = [q1]
                q2 = act(lambda j=j: nc.scalar.activation(scratch, dst[:, j, c0:c0 + 512], ACT.Square), q1, out_t)
                out_t = [dve(lambda j=j: V.tensor_reduce(ss[j], heads(scratch, 8), AX, ALU.add), q2)]
            return out_t

        def norm_heads(dst, j, n, r, g, *waits):
            d = heads(dst[:, j, :], n)
            q1 = dve(lambda: V.tensor_tensor(d, d, wide(r, 64), ALU.mult), *waits)
            gb = g.unsqueeze(1).to_broadcast([P, n, 64])
            return dve(lambda: V.tensor_tensor(d, d, gb, ALU.mult), q1)

        def to_heads_T(src, dst, nt_, ready):
            toks = []
            for kb in range(nt_ // 2):
                b = bank()
                for sub in range(2):
                    for j in range(2):
                        t = transpose(b.t[:, sub * S + j * P:sub * S + (j + 1) * P],
                                      src[:, j, (2 * kb + sub) * P:(2 * kb + sub + 1) * P], P,
                                      ready[j], b.free, q_con, sig=(sub == 1 and j == 1))
                o3 = b.t[:, :].rearrange("p (k s) -> p k s", k=2)
                e = (lambda kb=kb, o3=o3: nc.scalar.activation(dst[:, 2 * kb:2 * kb + 2, :], o3, ACT.Copy))
                b.free = [act(e, t)]
                toks.append(b.free[0])
            return toks

        class Head:
            pass

        def scores(h_, qT, kT, ready, prob_, free, sm, cq=None, ck=None):
            hd = Head()
            p0, t = 64 * (h_ % 2), h_ // 2
            b = bank()
            for j in range(2):
                nk_ = P * (j + 1)
                o = b.t[:, 0:P] if j == 0 else b.t[:, P:3 * P]
                qs, ks = qT[p0:p0 + 64, t, j * P:(j + 1) * P], kT[p0:p0 + 64, t, 0:nk_]
                pe(lambda o=o, qs=qs, ks=ks: T.matmul(o, qs, ks, start=True, stop=False), ready, b.free, sig=False)
                if ck is not None:
                    l, r = ck(h_, nk_)
                    pe(lambda o=o, l=l, r=r: T.matmul(o, l, r, start=False, stop=False), sig=False)
                causal = maskb[:, 2 - j:3, :].rearrange("p a s -> p (a s)")
                q = pe(lambda o=o, causal=causal: T.matmul(o, maskb[:, 0, :], causal, start=False, stop=True), q_con)
            mx, nb, rs = sm
            q1 = dve(lambda: V.tensor_reduce(mx[:, 0:1], b.t[:, 0:P], AX, ALU.max), q)
            q2 = dve(lambda: V.tensor_reduce(mx[:, 1:2], b.t[:, P:3 * P], AX, ALU.max), q)
            if cq is None:
                q3 = dve(lambda: V.tensor_scalar(nb, mx, -1.0, None, ALU.mult), q1, q2, free)
            else:
                q3 = dve(lambda: V.tensor_tensor(mx, mx, cq, ALU.add), q1, q2)
                q3 = dve(lambda: V.scalar_tensor_tensor(nb, mx, -1.0, cq, ALU.mult, ALU.add), q3, free)
            act(lambda: nc.scalar.activation(prob_[:, 0:P], b.t[:, 0:P], ACT.Exp, bias=nb[:, 0:1], accum_out=rs[:, 0:1]), q3, free)
            hd.exp = act(lambda: nc.scalar.activation(prob_[:, P:3 * P], b.t[:, P:3 * P], ACT.Exp, bias=nb[:, 1:2], accum_out=rs[:, 1:2]))
            b.free = [hd.exp]
            return hd

        def values(h_, hd, prob_, probT_, free, vt, vready, ob, obfree):
            b = bank()
            for i in range(3):
                q = transpose(b.t[:, i * P:(i + 1) * P], prob_[:, i * P:(i + 1) * P], P, hd.exp, b.free, sig=(i == 2))
            hd.trans = q
            q = dve(lambda: V.tensor_copy(probT_, b.t[:, 0:3 * P]), q, free)
            b.free = [q]
            c = (h_ % 4) * 64
            vv = [vt[:, kb, h_ * 64:(h_ + 1) * 64] for kb in range(2)]
            pe(lambda: T.matmul(ob.t[:, c:c + 64], probT_[:, 0:P], vv[0], start=True, stop=True), q, vready, obfree, sig=False)
            pe(lambda: T.matmul(ob.t[:, S + c:S + c + 64], probT_[:, P:2 * P], vv[0], start=True, stop=False), sig=False)
            hd.done = pe(lambda: T.matmul(ob.t[:, S + c:S + c + 64], probT_[:, 2 * P:3 * P], vv[1], start=False, stop=True))
            return hd.done

        def attention(nh, qT, kT, vt, qkready, vready, dst, prob_, probT_, mx, nb, rs, step, cq=None, ck=None):
            hds = []
            ob = None
            toks = []
            for h_ in range(nh + 1):
                if h_ < nh:
                    i = h_ % 2
                    free = [hds[h_ - 2].trans] if h_ >= 2 else []
                    sm = (mx[:, i, :], nb[:, i, :], rs[:, :, h_])
                    hds.append(scores(h_, qT, kT, qkready, prob_[i], free, sm, cq and cq(h_), ck))
                    step()
                if h_ >= 1:
                    g = h_ - 1
                    if g % 4 == 0:
                        ob = bank()
                        ob.held = True
                        obfree = ob.free
                    free = [hds[g - 2].done] if g >= 2 else []
                    q = values(g, hds[g], prob_[g % 2], probT_[g % 2], free, vt, vready, ob, obfree)
                    step()
                    if g % 4 == 3:
                        r4 = rs[:, :, g - 3:g + 1]
                        q1 = dve(lambda r4=r4: V.reciprocal(r4, r4), hds[g].exp)
                        o4 = ob.t[:, :].rearrange("p (j h d) -> p j h d", j=2, h=4)
                        d4 = dst[:, :, (g - 3) * 64:(g + 1) * 64].rearrange("p j (h d) -> p j h d", h=4)
                        for j in range(2):
                            q2 = dve(lambda j=j, r4=r4, o4=o4, d4=d4: V.tensor_tensor(
                                d4[:, j], o4[:, j], wide(r4[:, j, :], 64), ALU.mult), q, q1)
                        ob.free = [q2]
                        ob.held = False
                        toks.append(q2)
            return toks

        mss = st[:, 8:40].rearrange("p (i j h) -> p i j h", i=2, j=2)
        mrs = sb("mrs", [P, 32], F32, s1)
        rr = mrs[:, :].rearrange("p (i j h) -> p i j h", i=2, j=2)
        tk = []
        for i, (nm, dst) in enumerate((("mq", mq), ("mk", mk))):
            banks, toks = whole(stream(nm, 8, main))
            tk += take_heads(banks, toks, dst, 0, [mss[:, i, 0, :], mss[:, i, 1, :]], sq)
        q_r = rsqrt(mrs[:, :], st[:, 8:40], 32, 1.0 / 64, 1e-6, tk)
        q_rot = {}
        for i, dst in enumerate((mq, mk)):
            for j in range(2):
                q = norm_heads(dst, j, 8, rr[:, i, j, :], qkg[:, i, :], q_r, q_qg)
                hv = heads(dst[:, j, :], 8)
                x1, x2 = hv[:, :, 0:8], hv[:, :, 8:16]
                cb = rcos[:, j, :].unsqueeze(1).to_broadcast([P, 8, 8])
                sb_ = rsin[:, j, :].unsqueeze(1).to_broadcast([P, 8, 8])
                r4 = [rt[:, a, 64 * j:64 * j + 64].rearrange("p (h d) -> p h d", h=8) for a in range(4)]
                prev = q_rot.get((0, j))
                for a, (u, c) in enumerate(((x1, cb), (x2, sb_), (x2, cb), (x1, sb_))):
                    qm = pool(lambda a=a, u=u, c=c, r4=r4: G.tensor_tensor(r4[a], u, c, ALU.mult), q, q_rope, prev)
                pool(lambda x1=x1, r4=r4: G.tensor_tensor(x1, r4[0], r4[1], ALU.subtract), qm)
                q_rot[i, j] = pool(lambda x2=x2, r4=r4: G.tensor_tensor(x2, r4[2], r4[3], ALU.add), qm)
        banks, toks = whole(stream("mv", 8, main))
        q_mv = []
        for j in range(2):
            q_mv.append(act(lambda j=j, b=banks[j]: nc.scalar.activation(mv[:, j, :], b.t[:, :], ACT.Copy), toks[j]))
            banks[j].free = [q_mv[-1]]
        qk_t = to_heads_T(mq, mqT, 4, [q_rot[0, j] for j in range(2)])
        qk_t += to_heads_T(mk, mkT, 4, [q_rot[1, j] for j in range(2)])

        zr, zk, zv = (view(52 + 4 * i, 1024).rearrange("p (t s) -> p t s", t=4) for i in range(3))
        lor = view(64, 768).rearrange("p (t s) -> p t s", t=3)
        zt = view(67, 1024).rearrange("p (j c) -> p j c", j=2)
        zb = [view(71, 514).rearrange("p (k s) -> p k s", k=2), view(73.25, 514).rearrange("p (k s) -> p k s", k=2)]
        q_zb = [pool(lambda i=i: G.memset(zb[i][:, :, 0:1], 0.0)) for i in range(2)]
        z_tok = {}
        zb_free = [[], []]
        zt_free = [[]]

        def take_z(nm, banks, toks, dst, w, mu0):
            qz = []
            for j in range(2):
                qz.append(act(lambda j=j, b=banks[j]: nc.scalar.activation(zt[:, j, 0:w], b.t[:, 0:w], ACT.Copy), toks[j], zt_free[0]))
                banks[j].free = [qz[-1]]
            yield
            tiles = [(i, min(P, w - i * P)) for i in range((w + P - 1) // P)]
            out_t = []
            for kb in range(0, len(tiles), 2):
                grp = tiles[kb:kb + 2]
                b = bank()
                for sub, (i, rows) in enumerate(grp):
                    for j in range(2):
                        q = transpose(b.t[0:rows, sub * S + j * P:sub * S + (j + 1) * P], zt[:, j, i * P:i * P + rows], P,
                                      qz, b.free, q_con, sig=(j == 1))
                ib = (kb // 2) % 2
                z_ = zb[ib]
                n, rows = len(grp), grp[-1][1]
                o3 = b.t[0:rows, 0:n * S].rearrange("p (k s) -> p k s", k=n)
                q = act(lambda z_=z_, o3=o3, n=n, rows=rows: nc.scalar.activation(z_[0:rows, 0:n, 1:S + 1], o3, ACT.Copy), q, zb_free[ib], q_zb)
                b.free = [q]
                d = dst[0:rows, kb:kb + n, :]
                q1 = dve(lambda z_=z_, d=d, n=n, rows=rows: V.tensor_tensor(d, z_[0:rows, 0:n, 0:S], z_[0:rows, 0:n, 1:S + 1], ALU.subtract), q)
                zb_free[ib] = []
                for sub in range(n):
                    mu = vcol("rwkv_mu", mu0 + kb + sub, rows)
                    q2 = dve(lambda z_=z_, d=d, sub=sub, mu=mu, rows=rows: V.scalar_tensor_tensor(
                        d[:, sub, :], d[:, sub, :], mu, z_[0:rows, sub, 1:S + 1], ALU.mult, ALU.add), q1, q_con)
                    zb_free[ib].append(q2)
                    out_t.append(q2)
                yield
            zt_free[0] = [q]
            z_tok[nm] = out_t

        def rwkv_inputs():
            for nm, dst, w, m0 in (("wr", zr, 512, 0), ("wk", zk, 512, 4), ("wv", zv, 512, 8), ("wl", lor, 288, 12)):
                banks, toks = yield from stream(nm, 8, main)
                yield from take_z(nm, banks, toks, dst, w, m0)

        fillers.append(rwkv_inputs())
        mmx = sb("mmx", [P, 2, 2], F32, s1)
        mnb = sb("mnb", [P, 2, 2], F32, s1)
        msum = sb("msum", [P, 2, 8], F32, s1)
        q_yb = attention(8, mqT, mkT, mv, qk_t, q_mv, yb, prob, probT, mmx, mnb, msum, fill)
        finish()

        q_gates = {}

        def gate_groups():
            for g in range(4):
                banks, toks = yield from stream(f"g{g}", 8, main)
                for j in range(2):
                    o = gates[:, j, g * 512:(g + 1) * 512]
                    q = act(lambda o=o, b=banks[j]: nc.scalar.activation(o, b.t[:, :], ACT.Sigmoid), toks[j])
                    banks[j].free = [q]
                    q_gates[g, j] = q
                q_gates["pe"] = toks[1]
                yield

        fillers.append(gate_groups())

        def v48(kb, n=1024):
            return view(kb, n).rearrange("p (t s) -> p t s", t=4)

        AR = view(20, 2048).rearrange("p (t c a s) -> p t c a s", t=4, c=2, a=2)
        btl, ktl = (view(kb, 1024).rearrange("p (t c s) -> p t c s", t=4, c=2) for kb in (28, 32))
        Vt = view(36, 1024).rearrange("p (c n) -> p c n", c=2)
        Bt, Kt = view(40, 512), view(42, 512)
        bon, gg = v48(44), v48(48)
        cs = view(76, 1032).rearrange("p (n s) -> p n s", n=8)
        Wp = view(80.25, 1032).rearrange("p (n s) -> p n s", n=8)
        Wn = view(84.5, 1024).rearrange("p (n s) -> p n s", n=8)
        av, kk, tm = v48(88.5), v48(92.5), v48(96.5)
        wlo_sb = sb("wlora", [P, 512 * 2], F32, s1)
        wg2 = sb("wgate2", [32, 512], F32, s1)
        fac = sb("fac", [P, 2, 4], F32, s1)
        q_wl = dma(wlo_sb[:, :], A["wlora"], s_misc)
        q_wl = dma(wg2[:, :], A["wg2"], s_misc)
        wda, wgu = wlo_sb[:, 0:512], wlo_sb[:, 512:1024]

        qt = z_tok["wl"]
        q_th = act(lambda: nc.scalar.activation(lor[0:64, 0, :], lor[0:64, 0, :], ACT.Tanh), qt)
        q_sg = act(lambda: nc.scalar.activation(lor[:, 1, :], lor[:, 1, :], ACT.Sigmoid), qt)
        q_sg = act(lambda: nc.scalar.activation(lor[0:32, 2, :], lor[0:32, 2, :], ACT.Sigmoid), qt)
        q_dec, q_a, q_g = [], [], []
        for kb in range(2):
            for what in range(3):
                b = bank()
                for sub in range(2):
                    t = 2 * kb + sub
                    o = b.t[:, sub * S:(sub + 1) * S]
                    if what < 2:
                        r = slice(64 * what, 64 * what + 64)
                        w, z_ = wda[r, t * P:(t + 1) * P], lor[r, 0, :]
                        q = pe(lambda o=o, w=w, z_=z_: T.matmul(o, w, z_, start=True, stop=True), q_th, qt, q_wl, b.free)
                    else:
                        w, w2 = wgu[:, t * P:(t + 1) * P], wg2[:, t * P:(t + 1) * P]
                        pe(lambda o=o, w=w: T.matmul(o, w, lor[:, 1, :], start=True, stop=False), q_sg, q_wl, b.free, sig=False)
                        q = pe(lambda o=o, w2=w2: T.matmul(o, w2, lor[0:32, 2, :], start=False, stop=True))
                for sub in range(2):
                    t = 2 * kb + sub
                    o = b.t[:, sub * S:(sub + 1) * S]
                    if what == 0:
                        f = act(lambda t=t, o=o: nc.scalar.activation(tm[:, t, :], o, ACT.Sigmoid, bias=vcol("decay_bias", t)), q)
                        q_dec.append(f)
                    elif what == 1:
                        f = act(lambda t=t, o=o: nc.scalar.activation(av[:, t, :], o, ACT.Sigmoid, bias=vcol("aaa_bias", t)), q)
                        q_a.append(f)
                    else:
                        f = act(lambda t=t, o=o: nc.scalar.activation(gg[:, t, :], o, ACT.Copy), q)
                        q_g.append(f)
                b.free = [f]
        fill(2)

        q0 = dve(lambda: V.memset(cs[:, :, 0:1], 0.0), z_tok["wl"])
        qs = []
        one = eps[:, 2:3].to_broadcast([P, P])
        for t in range(4):
            for c in range(2):
                qs.append(dve(lambda t=t, c=c: V.tensor_tensor_scan(
                    cs[:, 2 * t + c, 1:P + 1], one, tm[:, t, c * P:(c + 1) * P], 0.0, ALU.mult, ALU.add), q_dec, q_eps))
        q = dve(lambda: V.tensor_tensor(Wp[:, :, :], cs[:, :, :], cs[:, :, 64:65].to_broadcast([P, 8, P + 1]), ALU.subtract), qs, q0)
        q_wn = act(lambda: nc.scalar.activation(Wn[:, :, :], Wp[:, :, 1:P + 1], ACT.Exp, scale=E05), q)
        q_wp = act(lambda: nc.scalar.activation(Wp[:, :, :], Wp[:, :, :], ACT.Exp, scale=-E05), q, q_wn)

        def per_head_sums(src, ready):
            res = []
            for kb in range(2):
                b = bank()
                for sub in range(2):
                    o, i = b.t[:, sub * S:(sub + 1) * S], src[:, 2 * kb + sub, :]
                    q = pe(lambda o=o, i=i: T.matmul(o, bones, i, start=True, stop=True), ready, b.free, q_con)
                res.append((b, q))
            return res

        q = [dve(lambda t=t: V.tensor_scalar(kk[:, t, :], zk[:, t, :], vcol("k_k", t), None, ALU.mult), z_tok["wk"]) for t in range(4)]
        q = dve(lambda: V.tensor_tensor(tm, kk, kk, ALU.mult), q, qs)
        fill(1)
        q_in = []
        for kb, (b, qb) in enumerate(per_head_sums(tm, q)):
            o3 = b.t[:, :].rearrange("p (k s) -> p k s", k=2)
            t2 = tm[:, 2 * kb:2 * kb + 2, :]
            f = act(lambda o3=o3, t2=t2: nc.scalar.activation(t2, o3, ACT.Sqrt), qb)
            b.free = [f]
            f = dve(lambda t2=t2: V.tensor_scalar(t2, t2, 1e-12, None, ALU.max), f)
            q_in.append(dve(lambda t2=t2: V.reciprocal(t2, t2), f))
        q_kk = dve(lambda: V.tensor_tensor(kk, kk, tm, ALU.mult), q_in)
        q1 = [dve(lambda t=t: V.tensor_scalar(tm[:, t, :], av[:, t, :], 1.0, vcol("k_a", t), ALU.subtract, ALU.mult), q_a, q_kk) for t in range(4)]
        q_k2 = dve(lambda: V.scalar_tensor_tensor(zk, tm, 1.0, zk, ALU.add, ALU.mult), q1)
        wp1 = Wp[:, :, 1:P + 1].rearrange("p (t c) s -> p t c s", t=4)
        wp0 = Wp[:, :, 0:P].rearrange("p (t c) s -> p t c s", t=4)
        wn = Wn[:, :, :].rearrange("p (t c) s -> p t c s", t=4)

        def tcs(ap):
            return ap.rearrange("p t (c s) -> p t c s", c=2)

        fill(1)
        q_ar = []
        q_bk = []
        q_ka = dve(lambda: V.tensor_tensor(av, kk, av, ALU.mult), q_kk, q1)
        for t in range(4):
            q_ar.append(dve(lambda t=t: V.scalar_tensor_tensor(AR[:, t, :, 0, :], tcs(kk)[:, t], -1.0, wp0[:, t], ALU.mult, ALU.mult), q_kk, q_wp))
            q_ar.append(dve(lambda t=t: V.tensor_tensor(AR[:, t, :, 1, :], tcs(zr)[:, t], wp1[:, t], ALU.mult), z_tok["wr"], q_wp))
            q_bk.append(dve(lambda t=t: V.tensor_tensor(btl[:, t], tcs(av)[:, t], wn[:, t], ALU.mult), q_ka, q_wn))
            q_bk.append(dve(lambda t=t: V.tensor_tensor(ktl[:, t], tcs(zk)[:, t], wn[:, t], ALU.mult), q_k2, q_wn))
        q = dve(lambda: V.reciprocal(fac[:, 0, :], Wp[:, 1:8:2, 0]), q_wp)
        q_fac = dve(lambda: V.tensor_tensor(fac[:, 1, :], fac[:, 0, :], Wp[:, 0:8:2, P], ALU.mult), q)
        q1 = [dve(lambda t=t: V.scalar_tensor_tensor(tm[:, t, :], zr[:, t, :], vcol("r_k", t), zk[:, t, :], ALU.mult, ALU.mult), q_k2) for t in range(4)]
        q_bon = []
        for kb, (b, qb) in enumerate(per_head_sums(tm, q1)):
            o3 = b.t[:, :].rearrange("p (k s) -> p k s", k=2)
            f = dve(lambda o3=o3, kb=kb: V.tensor_tensor(bon[:, 2 * kb:2 * kb + 2, :], o3, zv[:, 2 * kb:2 * kb + 2, :], ALU.mult), qb, z_tok["wv"])
            b.free = [f]
            q_bon.append(f)

        def tokens_on_partitions(src, dst, ready):
            b = bank()
            for t in range(4):
                q = transpose(b.t[:, t * P:(t + 1) * P], src(t), P, ready, b.free, sig=(t == 3))
            b.free = [act(lambda: nc.scalar.activation(dst, b.t[:, :], ACT.Copy), q)]
            return b.free[0]

        q_vt = [tokens_on_partitions(lambda t, c=c: zv[:, t, c * P:(c + 1) * P], Vt[:, c, :], z_tok["wv"]) for c in range(2)]
        q_bt = tokens_on_partitions(lambda t: btl[:, t, 0, :], Bt, q_bk)
        q_kt = tokens_on_partitions(lambda t: ktl[:, t, 0, :], Kt, q_bk)
        early_done = [q_ar, q_bk, q_fac, q_bon, q_vt, q_k2, q_g]

        Sm = view(52, 4096).rearrange("p (h a s) -> p h a s", h=8, a=4)
        Ti = view(68, 1024).rearrange("p (h s) -> p h s", h=8)
        TT = view(72, 1024).rearrange("p (h s) -> p h s", h=8)
        M1 = view(76, 1024).rearrange("p (h s) -> p h s", h=8)
        Ao = [view(80, 512).rearrange("p (h s) -> p h s", h=4), view(82, 512).rearrange("p (h s) -> p h s", h=4)]
        RU, U = view(84, 512), view(86, 512)
        S0 = view(88, 256).rearrange("p (t v) -> p t v", t=4)
        Y = v48(89)
        Y2, Y3 = v48(93), v48(97)
        mask4 = const("mask4", 512)
        lev0 = const("lev0", P)
        levs = const("levs", 768).rearrange("p (l s) -> p l s", l=6)

        def both(ap):
            return ap.unsqueeze(1).to_broadcast([P, 4, P])

        q_y = []
        q_s0 = None
        prevU = []
        for c in range(2):
            q_sm = []
            for hh in range(8):
                p0, t = 64 * (hh % 2), hh // 2
                b = bank()
                ar = AR[p0:p0 + 64, t, c, :, :].rearrange("p a s -> p (a s)")
                lb, lk = btl[p0:p0 + 64, t, c, :], ktl[p0:p0 + 64, t, c, :]
                pe(lambda b=b, lb=lb, ar=ar: T.matmul(b.t[:, 0:256], lb, ar, start=True, stop=True), q_ar, q_bk, b.free, sig=False)
                q = pe(lambda b=b, lk=lk, ar=ar: T.matmul(b.t[:, 256:512], lk, ar, start=True, stop=True))
                d = Sm[:, hh].rearrange("p a s -> p (a s)")
                q_sm.append(dve(lambda b=b, d=d: V.tensor_tensor(d, b.t[:, :], mask4, ALU.mult), q, early_done, prevU))
                b.free = [q_sm[-1]]
            q_T, q_TT = [None, None], [None, None]
            q_ao = [[], []]
            for g in range(2):
                hs = slice(4 * g, 4 * g + 4)
                q = pool(lambda hs=hs: G.tensor_tensor(TT[:, hs, :], Sm[:, hs, 0, :], both(lev0), ALU.mult), q_sm[4 * g:4 * g + 4], prevU)
                q_TT[g] = pool(lambda hs=hs: G.tensor_tensor(TT[:, hs, :], TT[:, hs, :], both(ident), ALU.add), q)
            for g in range(2):
                b = bank()
                for i in range(4):
                    q = transpose(b.t[:, i * P:(i + 1) * P], TT[:, 4 * g + i, :], P, q_TT[g], b.free, sig=(i == 3))
                o3 = b.t[:, :].rearrange("p (h s) -> p h s", h=4)
                q_T[g] = act(lambda g=g, o3=o3: nc.scalar.activation(Ti[:, 4 * g:4 * g + 4, :], o3, ACT.Copy), q)
                b.free = [q_T[g]]
            q_m1pe = [None, None]
            for l in range(6):
                q_m1 = [None, None]
                for g in range(2):
                    hs = slice(4 * g, 4 * g + 4)
                    q = pool(lambda g=g, hs=hs, l=l: G.tensor_tensor(Ao[g], Sm[:, hs, 0, :], both(levs[:, l, :]), ALU.mult),
                             q_sm[4 * g:4 * g + 4], q_m1pe[g], early_done)
                    b = bank()
                    for i in range(4):
                        q2 = pe(lambda b=b, g=g, i=i: T.matmul(b.t[:, i * P:(i + 1) * P], Ao[g][:, i, :], Ti[:, 4 * g + i, :],
                                                               start=True, stop=True), q, q_T[g], b.free, sig=(i == 3))
                    q_m1pe[g] = q2
                    o3 = b.t[:, :].rearrange("p (h s) -> p h s", h=4)
                    q_m1[g] = act(lambda hs=hs, o3=o3: nc.scalar.activation(M1[:, hs, :], o3, ACT.Copy), q2)
                    b.free = [q_m1[g]]
                fill(1)
                for g in range(2):
                    hs = slice(4 * g, 4 * g + 4)
                    if l < 5:
                        b = bank()
                        for i in range(4):
                            q2 = pe(lambda b=b, g=g, i=i: T.matmul(b.t[:, i * P:(i + 1) * P], TT[:, 4 * g + i, :], M1[:, 4 * g + i, :],
                                                                   start=True, stop=True), q_m1[g], q_TT[g], b.free, sig=(i == 3))
                        o3 = b.t[:, :].rearrange("p (h s) -> p h s", h=4)
                        q_T[g] = dve(lambda hs=hs, o3=o3: V.tensor_tensor(Ti[:, hs, :], Ti[:, hs, :], o3, ALU.add), q2)
                        b.free = [q_T[g]]
                    b = bank()
                    for i in range(4):
                        q2 = pe(lambda b=b, g=g, i=i: T.matmul(b.t[:, i * P:(i + 1) * P], M1[:, 4 * g + i, :], TT[:, 4 * g + i, :],
                                                               start=True, stop=True), q_m1[g], q_TT[g], b.free, sig=(i == 3))
                    o3 = b.t[:, :].rearrange("p (h s) -> p h s", h=4)
                    q_TT[g] = dve(lambda hs=hs, o3=o3: V.tensor_tensor(TT[:, hs, :], TT[:, hs, :], o3, ALU.add), q2)
                    b.free = [q_TT[g]]
            q_ru = []
            for par in range(2):
                b = bank()
                p0 = 64 * par
                for t in range(4):
                    hh = 2 * t + par
                    o = b.t[:, t * 64:(t + 1) * 64]
                    v_ = Vt[:, c, hh * 64:(hh + 1) * 64]
                    q = pe(lambda o=o, hh=hh, v_=v_, c=c: T.matmul(o, Sm[:, hh, 2, :], v_, start=True, stop=(c == 0)), q_sm, q_vt, b.free)
                    if c == 1:
                        q = pe(lambda o=o, t=t, p0=p0: T.matmul(o, AR[p0:p0 + 64, t, 1, 0, :], S0[p0:p0 + 64, t, :], start=False, stop=True), q_s0)
                d = RU.rearrange("p (t a v) -> p t a v", t=4, a=2)[:, :, par, :]
                o3 = b.t[:, 0:256].rearrange("p (t v) -> p t v", t=4)
                q_ru.append(act(lambda d=d, o3=o3: nc.scalar.activation(d, o3, ACT.Copy), q, early_done))
                b.free = [q_ru[-1]]
            b = bank()
            for hh in range(8):
                o = b.t[:, hh * 64:(hh + 1) * 64]
                q = pe(lambda o=o, hh=hh: T.matmul(o, TT[:, hh, :], RU[:, hh * 64:(hh + 1) * 64], start=True, stop=True), q_ru, q_TT, b.free)
            q_u = act(lambda b=b: nc.scalar.activation(U, b.t[:, :], ACT.Copy), q)
            b.free = [q_u]
            if c == 0:
                b = bank()
                for hh in range(8):
                    p0, t = 64 * (hh % 2), hh // 2
                    o = b.t[p0:p0 + 64, t * 64:(t + 1) * 64]
                    hd = slice(hh * 64, hh * 64 + 64)
                    pe(lambda o=o, hd=hd: T.matmul(o, Bt[:, hd], U[:, hd], start=True, stop=False), q_u, q_bt, b.free, sig=False)
                    q = pe(lambda o=o, hd=hd: T.matmul(o, Kt[:, hd], Vt[:, 0, hd], start=False, stop=True), q_kt, q_vt)
                o3 = b.t[:, 0:256].rearrange("p (t v) -> p t v", t=4)
                q_s0 = dve(lambda o3=o3: V.tensor_tensor(S0, o3, wide(fac[:, 1, :], 64), ALU.mult), q, q_fac)
                b.free = [q_s0]
            b = bank()
            for hh in range(8):
                p0, t = 64 * (hh % 2), hh // 2
                o = b.t[p0:p0 + 64, t * P:(t + 1) * P]
                hd = slice(hh * 64, hh * 64 + 64)
                pe(lambda o=o, hd=hd, hh=hh, c=c: T.matmul(o, Vt[:, c, hd], Sm[:, hh, 3, :], start=True, stop=False), q_u, b.free, sig=False)
                if c == 1:
                    pe(lambda o=o, t=t, p0=p0: T.matmul(o, S0[p0:p0 + 64, t, :], AR[p0:p0 + 64, t, 1, 1, :], start=False, stop=False), sig=False)
                q = pe(lambda o=o, hd=hd, hh=hh: T.matmul(o, U[:, hd], Sm[:, hh, 1, :], start=False, stop=True))
            prevU = [q]
            o3 = b.t[:, :].rearrange("p (t s) -> p t s", t=4)
            q_y.append(act(lambda b=b, o3=o3, c=c: nc.scalar.activation(Y[:, :, c * P:(c + 1) * P], o3, ACT.Copy), q, early_done))
            b.free = [q_y[-1]]

        q_c = []
        for kb, (b, qb) in enumerate(per_head_sums(Y, q_y)):
            o3 = b.t[:, :].rearrange("p (k s) -> p k s", k=2)
            f = dve(lambda o3=o3, kb=kb: V.scalar_tensor_tensor(Y[:, 2 * kb:2 * kb + 2, :], o3, -1.0 / 64, Y[:, 2 * kb:2 * kb + 2, :], ALU.mult, ALU.add), qb, q_c)
            b.free = [f]
            q_c.append(f)
        q = act(lambda: nc.scalar.activation(Y2, Y, ACT.Square), q_c)
        q_v = []
        for kb, (b, qb) in enumerate(per_head_sums(Y2, q)):
            o3 = b.t[:, :].rearrange("p (k s) -> p k s", k=2)
            d = Y3[:, 2 * kb:2 * kb + 2, :]
            f = act(lambda o3=o3, d=d: nc.scalar.activation(d, o3, ACT.Sqrt, bias=eps[:, 1:2], scale=1.0 / 64), qb, q_eps)
            b.free = [f]
            q_v.append(dve(lambda d=d: V.reciprocal(d, d), f))
        q = dve(lambda: V.tensor_tensor(Y, Y, Y3, ALU.mult), q_v)
        q = [dve(lambda t=t: V.tensor_scalar(Y[:, t, :], Y[:, t, :], vcol("ln_g", t), vcol("ln_b", t), ALU.mult, ALU.add), q) for t in range(4)]
        q = dve(lambda: V.tensor_tensor(Y, Y, bon, ALU.add), q, q_bon)
        q = dve(lambda: V.tensor_tensor(Y, Y, gg, ALU.mult), q, q_g)
        finish()
        ya = Acts(a_hi[:, 4:8, :], a_lo[:, 4:8, :])
        ybA = Acts(a_hi[:, 0:4, :], a_lo[:, 0:4, :])
        to_acts(yb, [q_yb, q_yb], ybA, 4, wait_free=(q_gates["pe"],))
        q1 = act(lambda: nc.scalar.activation(ya.hi, Y, ACT.Copy), q, q_gates["pe"])
        q1 = dve(lambda: V.tensor_tensor(ya.lo, Y, ya.hi.bitcast(F32), ALU.subtract), q1)
        for k in range(4):
            ya.tok[k] = q1

        q_h = [[], []]
        for c in range(2):
            ba, ta = whole(stream(f"ba{c}", 4, ya))
            bb, tb = whole(stream(f"bb{c}", 4, ybA))
            for j in range(2):
                d, t2 = h[:, j, c * 512:(c + 1) * 512], view(52 + 2 * (2 * c + j), 512)
                ga, gb = gates[:, j, c * 512:(c + 1) * 512], gates[:, j, 1024 + c * 512:1024 + (c + 1) * 512]
                f = dve(lambda d=d, ga=ga, b=ba[j]: V.tensor_tensor(d, b.t[:, :], ga, ALU.mult), ta[j], q_gates[c, j])
                ba[j].free = [f]
                f2 = dve(lambda t2=t2, gb=gb, b=bb[j]: V.tensor_tensor(t2, b.t[:, :], gb, ALU.mult), tb[j], q_gates[2 + c, j])
                bb[j].free = [f2]
                q_h[j].append(dve(lambda d=d, t2=t2: V.tensor_tensor(d, d, t2, ALU.add), f, f2))
        to_acts(h, q_h, main, 8)
        q_x1 = [[], []]
        for c in range(2):
            banks, toks = whole(stream(f"wo{c}", 8, main))
            for j in range(2):
                xs = x[:, j, c * 512:(c + 1) * 512]
                f = dve(lambda xs=xs, b=banks[j]: V.tensor_tensor(xs, xs, b.t[:, :], ALU.add), toks[j])
                banks[j].free = [f]
                q_x1[j].append(f)
        s1.close()

        s3 = ExitStack()

        def hidden(name, stack):
            return Acts(sb(name + "_hi", [P, 22, S], F32R, stack)[:, :, :], sb(name + "_lo", [P, 22, S], F32R, stack)[:, :, :])

        ffn = hidden("f0", s3)
        at_ = [sb(f"at{i}", [P, 2, 512], F32, s3) for i in range(2)]
        aT = [sb(f"aT{i}", [P, 2, S], F32, s3) for i in range(2)]
        cv = [sb(f"cv{i}", [P, 2, S], F32, s3) for i in range(2)]
        prenorm(q_x1, "norm2_g", 0)
        at_free = [[], []]
        cv_free = [[], []]
        aT_free = [[], []]
        ncv = [0]

        def take(banks, toks, dst, free):
            qs = []
            for j in range(2):
                q = act(lambda j=j, b=banks[j]: nc.scalar.activation(dst[:, j, :], b.t[:, :], ACT.Copy), toks[j], free)
                banks[j].free = [q]
                qs.append(q)
            return qs

        def conv_tiles(k0, na, a_src, qa, ca, b_src, qb, cb):
            qa_pe = qb_pe = None
            for kb in range(na // 2):
                i = ncv[0] % 2
                ncv[0] += 1
                ab, bb = bank(), bank()
                for b, src, rdy, c0 in ((ab, a_src, qa, ca), (bb, b_src, qb, cb)):
                    for sub in range(2):
                        for j in range(2):
                            q = transpose(b.t[:, sub * S + j * P:sub * S + (j + 1) * P],
                                          src[:, j, c0 + (2 * kb + sub) * P:c0 + (2 * kb + sub + 1) * P], P,
                                          rdy[j], b.free, sig=(sub == 1 and j == 1))
                    if b is ab:
                        qa_pe = q
                    else:
                        qb_pe = q
                a3 = ab.t[:, :].rearrange("p (k s) -> p k s", k=2)
                b3 = bb.t[:, :].rearrange("p (k s) -> p k s", k=2)
                q = act(lambda i=i, a3=a3: nc.scalar.activation(aT[i][:, :, :], a3, ACT.Copy), qa_pe, aT_free[i])
                ab.free = [q]
                qg = []
                for sub in range(2):
                    k = k0 + 2 * kb + sub
                    a_, c_ = aT[i][:, sub, :], cv[i][:, sub, :]
                    w0, w1, w2, bi = (vcol(n_, k) for n_ in ("conv_w0", "conv_w1", "conv_w2", "conv_b"))
                    f = dve(lambda a_=a_, c_=c_, w2=w2, bi=bi: V.tensor_scalar(c_, a_, w2, bi, ALU.mult, ALU.add), q, cv_free[i])
                    f = dve(lambda a_=a_, c_=c_, w1=w1: V.scalar_tensor_tensor(
                        c_[:, 1:S], a_[:, 0:S - 1], w1, c_[:, 1:S], ALU.mult, ALU.add), f)
                    qg.append(dve(lambda a_=a_, c_=c_, w0=w0: V.scalar_tensor_tensor(
                        c_[:, 2:S], a_[:, 0:S - 2], w0, c_[:, 2:S], ALU.mult, ALU.add), f))
                aT_free[i] = qg
                f = act(lambda i=i: nc.scalar.activation(cv[i][:, :, :], cv[i][:, :, :], ACT.Gelu), qg)
                f = dve(lambda i=i, b3=b3: V.tensor_tensor(cv[i][:, :, :], cv[i][:, :, :], b3, ALU.mult), f, qb_pe)
                bb.free = [f]
                k = k0 + 2 * kb
                hi, lo = ffn.hi[:, k:k + 2, :], ffn.lo[:, k:k + 2, :]
                f = act(lambda i=i, hi=hi: nc.scalar.activation(hi, cv[i][:, :, :], ACT.Copy), f)
                f = dve(lambda i=i, hi=hi, lo=lo: V.tensor_tensor(lo, cv[i][:, :, :], hi.bitcast(F32), ALU.subtract), f)
                cv_free[i] = [f]
                ffn.tok[k] = ffn.tok[k + 1] = f
            at_free[0] = [qa_pe, qb_pe]
            at_free[1] = [qa_pe, qb_pe]

        for i in range(5):
            banks, toks = whole(stream(f"ua{i}", 8, main))
            qa = take(banks, toks, at_[0], at_free[0])
            banks, toks = whole(stream(f"ub{i}", 8, main))
            qb = take(banks, toks, at_[1], at_free[1])
            pending.append(lambda i=i, qa=qa, qb=qb: conv_tiles(4 * i, 4, at_[0], qa, 0, at_[1], qb, 0))
        banks, toks = whole(stream("ut", 8, main))
        qa = take(banks, toks, at_[0], at_free[0])
        conv_tiles(20, 2, at_[0], qa, 0, at_[0], qa, 256)
        q_x2 = [[], []]
        for c in range(2):
            banks, toks = whole(stream(f"dn{c}", 22, ffn))
            for j in range(2):
                xs = x[:, j, c * 512:(c + 1) * 512]
                f = dve(lambda xs=xs, b=banks[j]: V.tensor_tensor(xs, xs, b.t[:, :], ALU.add), toks[j])
                banks[j].free = [f]
                q_x2[j].append(f)
        s3.close()

        gain = [sb("gain0", [P, D])]
        ngain = [0]

        def load_gain(free):
            i = ngain[0]
            ngain[0] += 1
            g = gain[0]
            return g, dma(g[:, :], A["post"][i:i + 1, :].to_broadcast([P, D]), s_gain[0], free)

        gfree = [[]]
        sq_last = []

        def postnorm(names, nk, acts, xready):
            g, qg = load_gain(gfree[0])
            ss, qt_ = [[], []], [[], []]
            for c in range(2):
                banks, toks = whole(stream(names[c], nk, acts))
                for j in range(2):
                    cols = slice(c * 512, (c + 1) * 512)
                    b = banks[j]
                    f = act(lambda j=j, c=c, b=b: nc.scalar.activation(sqj[:, :], b.t[:, :], ACT.Square,
                                                                      accum_out=st[:, 40 + 2 * j + c:41 + 2 * j + c]), toks[j], sq_last)
                    sq_last[:] = [f]
                    ss[j].append(f)
                    f = dve(lambda j=j, cols=cols, b=b, g=g: V.tensor_tensor(h[:, j, cols], b.t[:, :], g[:, cols], ALU.mult), f, qg)
                    b.free = [f]
                    qt_[j].append(f)
            gfree[0] = [qt_]
            s4 = st[:, 40:44].rearrange("p (j c) -> p j c", j=2)
            q = dve(lambda: V.tensor_tensor(st[:, 44:46], s4[:, :, 0], s4[:, :, 1], ALU.add), ss)
            q = rsqrt(st[:, 46:48], st[:, 44:46], 2, 1.0 / D, 1e-6, q)
            return [[dve(lambda j=j: V.scalar_tensor_tensor(x[:, j, :], h[:, j, :], st[:, 46 + j:47 + j], x[:, j, :], ALU.mult, ALU.add),
                         q, qt_[j], xready)] for j in range(2)]

        sqj = sb("sqj", [P, 512])

        def swiglu(l, xready):
            prenorm(xready, "ffn_pre", 8 * l)
            s5 = ExitStack()
            ffn = hidden(f"f{l + 1}", s5)
            sg = [sb(f"sg{l}_{i}", [P, 2, 512], F32, s5) for i in range(2)]
            sg_free = [[], []]

            def groups(i, qp):
                to_acts_at(sg[i % 2], qp, 4, 4 * i)

            def to_acts_at(src, qp, nk_, k0):
                to_acts(src, qp, ffn, nk_, k0=k0)
                sg_free[(k0 // 4) % 2] = [ffn.tok[k0 + nk_ - 1]]

            for i in range(5):
                banks, toks = whole(stream(f"{l}ug{i}", 8, main))
                s_ = sg[i % 2]
                qs = []
                for j in range(2):
                    q = act(lambda j=j, b=banks[j], s_=s_: nc.scalar.activation(s_[:, j, :], b.t[:, :], ACT.Silu), toks[j], sg_free[i % 2])
                    banks[j].free = [q]
                    qs.append(q)
                banks, toks = whole(stream(f"{l}uu{i}", 8, main))
                qp = []
                for j in range(2):
                    q = dve(lambda j=j, b=banks[j], s_=s_: V.tensor_tensor(s_[:, j, :], s_[:, j, :], b.t[:, :], ALU.mult), toks[j], qs[j])
                    banks[j].free = [q]
                    qp.append(q)
                pending.append(lambda i=i, qp=qp: groups(i, qp))
            banks, toks = whole(stream(f"{l}ut", 8, main))
            s_ = sg[1]
            qp = []
            for j in range(2):
                q = act(lambda j=j, b=banks[j]: nc.scalar.activation(s_[:, j, 0:256], b.t[:, 0:256], ACT.Silu), toks[j], sg_free[1])
                q = dve(lambda j=j, b=banks[j]: V.tensor_tensor(s_[:, j, 0:256], s_[:, j, 0:256], b.t[:, 256:512], ALU.mult), q)
                banks[j].free = [q]
                qp.append(q)
            to_acts(s_, qp, ffn, 2, k0=20)
            res = postnorm([f"{l}dn0", f"{l}dn1"], 22, ffn, [])
            s5.close()
            return res

        s4_ = ExitStack()
        fq, fk = sb("fq", [P, 2, D], F32, s4_), sb("fk", [P, 2, D], F32, s4_)
        fv = sb("fv", [P, 2, D], F32, s4_)
        fgt = sb("fgt", [P, 2, D], F32, s4_)
        fo = fq
        wf = sb("wf", [P, 8, 16], F32, s4_)
        fprob = [sb(f"fprob{i}", [P, 384], F32, s4_) for i in range(2)]
        fprobT = [sb(f"fprobT{i}", [P, 384], F32, s4_) for i in range(2)]
        fc = sb("fc", [16, 4, S], F32, s4_)
        cqt = sb("cqt", [P, 2, 16], F32, s4_)
        frs = sb("frs", [P, 2, 16], F32, s4_)
        fmx = sb("fmx", [P, 2, 2], F32, s4_)
        fnb = sb("fnb", [P, 2, 2], F32, s4_)
        fg4 = sb("fg4", [P, 2, 64], F32, s4_)
        q_wf = dma(wf[:, :, :], A["wf"], s_misc)
        q_fg4 = dma(fg4[:, :, :], A["fg4"], s_misc)
        q_fg4 = dve(lambda: V.tensor_scalar(fg4[:, 0, :], fg4[:, 0, :], 0.125, None, ALU.mult), q_fg4)
        prenorm(q_x2, "mix_pre", 0)

        b = bank()
        for k in range(8):
            for n_, part in enumerate((main.hi, main.lo)):
                q = pe(lambda k=k, part=part, n_=n_, b=b: T.matmul(b.t[0:16, 0:S], wf[:, k, :], part[:, k, :].bitcast(F32),
                                                                  start=(k == 0 and n_ == 0), stop=(k == 7 and n_ == 1)),
                       main.tok[k], q_wf, b.free, sig=(k == 7 and n_ == 1))
        f0, f1, f2, f3 = (fc[:, i, :] for i in range(4))
        q = act(lambda b=b: nc.scalar.activation(f0, b.t[0:16, 0:S], ACT.Identity, bias=vcol("b_f", 0, 16)), q)
        b.free = [q]
        q1 = dve(lambda: V.scalar_tensor_tensor(f1, f0, -1.0, f0, ALU.mult, ALU.max), q)
        q1 = act(lambda: nc.scalar.activation(f1, f1, ACT.Exp, scale=-1.0), q1)
        q1 = act(lambda: nc.scalar.activation(f1, f1, ACT.Ln, bias=eps[0:16, 2:3]), q1, q_eps)
        q2 = dve(lambda: V.tensor_scalar(f0, f0, 0.0, None, ALU.min), q)
        q2 = dve(lambda: V.tensor_tensor(f0, f0, f1, ALU.subtract), q1, q2)
        q_c = dve(lambda: V.tensor_tensor_scan(f2, eps[0:16, 2:3].to_broadcast([16, S]), f0, 0.0, ALU.mult, ALU.add), q2)
        q_nc = dve(lambda: V.tensor_scalar(f3, f2, -1.0, None, ALU.mult), q_c)

        fss = sb("fss", [P, 64], F32, s4_)
        frr = sb("frr", [P, 64], F32, s4_)
        fs4 = fss[:, :].rearrange("p (i j h) -> p i j h", i=2, j=2)
        fr4 = frr[:, :].rearrange("p (i j h) -> p i j h", i=2, j=2)
        tk = []
        for i, (nm, dst) in enumerate((("fq", fq), ("fk", fk))):
            for c in range(2):
                banks, toks = whole(stream(f"{nm}{c}", 8, main))
                tk += take_heads(banks, toks, dst, c * 512, [fs4[:, i, j, 8 * c:8 * c + 8] for j in range(2)], sqj[:, :])
        q_cq = []
        b = bank()
        for j in range(2):
            q = transpose(b.t[:, 16 * j:16 * j + 16], f2[:, j * P:(j + 1) * P], 16, q_c, b.free, sig=(j == 1))
        q_cq = act(lambda b=b: nc.scalar.activation(cqt[:, :, :], b.t[:, 0:32].rearrange("p (j h) -> p j h", j=2), ACT.Copy), q)
        b.free = [q_cq]
        q_r = rsqrt(frr[:, :], fss[:, :], 64, 1.0 / 64, 1e-6, tk)
        q_n = {}
        for i, dst in enumerate((fq, fk)):
            for j in range(2):
                q_n[i, j] = norm_heads(dst, j, 16, fr4[:, i, j, :], fg4[:, i, :], q_r, q_fg4)
        q_fv = []
        for c in range(2):
            banks, toks = whole(stream(f"fv{c}", 8, main))
            for j in range(2):
                q = act(lambda j=j, c=c, b=banks[j]: nc.scalar.activation(fv[:, j, c * 512:(c + 1) * 512], b.t[:, :], ACT.Copy), toks[j])
                banks[j].free = [q]
                q_fv.append(q)
        fqT, fkT = sb("fqT", [P, 8, S], F32, s4_), sb("fkT", [P, 8, S], F32, s4_)
        qk_t = to_heads_T(fq, fqT, 8, [q_n[0, j] for j in range(2)])
        qk_t += to_heads_T(fk, fkT, 8, [q_n[1, j] for j in range(2)])
        q_fgt = {}

        def fox_gates():
            for c in range(2):
                banks, toks = yield from stream(f"fg{c}", 8, main)
                for j in range(2):
                    o = fgt[:, j, c * 512:(c + 1) * 512]
                    q = act(lambda o=o, b=banks[j]: nc.scalar.activation(o, b.t[:, :], ACT.Sigmoid), toks[j])
                    banks[j].free = [q]
                    q_fgt[c, j] = q
                yield

        fillers.append(fox_gates())
        half = [0]

        def step4():
            half[0] += 1
            if half[0] % 3 == 0:
                fill()

        q_o = attention(16, fqT, fkT, fv, qk_t + [q_cq, q_nc], q_fv, fo, [p[:, :] for p in fprob], [p[:, :] for p in fprobT],
                        fmx, fnb, frs, step4, cq=lambda h_: cqt[:, :, h_],
                        ck=lambda h_, n_: (ident[0:16, h_:h_ + 1].to_broadcast([16, P]), f3[:, 0:n_]))
        finish()
        q_og = [dve(lambda j=j: V.tensor_tensor(fo[:, j, :], fo[:, j, :], fgt[:, j, :], ALU.mult), q_o, [q_fgt[c, j] for c in range(2)])
                for j in range(2)]
        to_acts(fo, q_og, main, 8)
        s4_.close()
        q_x3 = postnorm(["fo0", "fo1"], 8, main, [])
        q_x4 = swiglu(0, q_x3)

        s6 = ExitStack()
        ct = sb("ct", [P, 32, P], F32, s6)
        stb = sb("stb", [P, 32, P], F32, s6)
        d0 = sb("d0", [P, 32, P], F32, s6)
        pr = sb("pr", [P, 16, 32], F32, s6)
        bz = sb("bz", [P, 8, 2, P], F32, s6)
        cz = sb("cz", [P, 32, 4, 32], F32, s6)
        q_bz = dma(bz[:, :, :, :], A["bz"], s_misc)
        q_cz = dma(cz[:, :, 0:2, :], A["cz"], s_misc)
        lre, lim = vcols("lam_re", 32), vcols("lam_im", 32)
        dt, mag, th, tr, are, aim, den, zre, zim, t1, t2, nre, i_re, i_im, th2, t3 = (pr[:, i, :] for i in range(16))
        q = act(lambda: nc.scalar.activation(dt, vcols("log_dt", 32), ACT.Exp), q_con)
        q1 = dve(lambda: V.tensor_tensor(t1, lre, dt, ALU.mult), q)
        q_mag = act(lambda: nc.scalar.activation(mag, t1, ACT.Exp), q1)
        q1 = dve(lambda: V.tensor_tensor(th, lim, dt, ALU.mult), q)
        q1 = dve(lambda: V.tensor_scalar(t2, th, float(1 / (2 * np.pi)), MAGIC, ALU.mult, ALU.add), q1)
        q1 = dve(lambda: V.tensor_scalar(t2, t2, MAGIC, None, ALU.subtract), q1)
        q1 = dve(lambda: V.scalar_tensor_tensor(th, t2, -6.28125, th, ALU.mult, ALU.add), q1)
        q1 = dve(lambda: V.scalar_tensor_tensor(th, t2, -float(2 * np.pi - 6.28125), th, ALU.mult, ALU.add), q1)
        q_tr = dve(lambda: V.tensor_scalar(tr, th, float(1 / (2 * np.pi)), None, ALU.mult), q1)
        iota = const("iota", P)
        q = pool(lambda: G.tensor_tensor(stb[:, :, :], wide(tr, P), iota.unsqueeze(1).to_broadcast([P, 32, P]), ALU.mult), q_tr, q_con)
        q1 = dve(lambda: V.tensor_scalar(ct[:, :, :], stb[:, :, :], MAGIC, MAGIC, ALU.add, ALU.subtract), q)
        q = pool(lambda: G.tensor_tensor(stb[:, :, :], stb[:, :, :], ct[:, :, :], ALU.subtract), q1)
        q1 = dve(lambda: V.scalar_tensor_tensor(ct[:, :, :], stb[:, :, :], -1.0, stb[:, :, :], ALU.mult, ALU.max), q)
        q1 = dve(lambda: V.tensor_scalar(ct[:, :, :], ct[:, :, :], -float(2 * np.pi), float(np.pi / 2), ALU.mult, ALU.add), q1)
        q2 = dve(lambda: V.tensor_scalar(stb[:, :, :], stb[:, :, :], float(2 * np.pi), 3.1415925, ALU.mult, ALU.min), q)
        q2 = dve(lambda: V.tensor_scalar(stb[:, :, :], stb[:, :, :], -3.1415925, None, ALU.max), q2, q1)
        q_ct = act(lambda: nc.scalar.activation(ct[:, :, :], ct[:, :, :], ACT.Sin), q1)
        q_st = act(lambda: nc.scalar.activation(stb[:, :, :], stb[:, :, :], ACT.Sin), q2)
        q = pool(lambda: G.tensor_copy(d0[:, :, :], wide(mag, P)), q_mag)
        q_d0 = pool(lambda: G.memset(d0[:, :, 0:1], 0.0), q)
        q = dve(lambda: V.tensor_tensor(are, mag, ct[:, :, 1], ALU.mult), q_ct, q_mag)
        q2 = dve(lambda: V.tensor_tensor(aim, mag, stb[:, :, 1], ALU.mult), q_st, q_mag)
        q = dve(lambda: V.tensor_scalar(nre, are, 1.0, None, ALU.subtract), q)
        q3 = dve(lambda: V.tensor_tensor(t1, lre, lre, ALU.mult), q_mag)
        q4 = dve(lambda: V.tensor_tensor(t2, lim, lim, ALU.mult), q_tr)
        q3 = dve(lambda: V.tensor_tensor(den, t1, t2, ALU.add), q3, q4)
        q3 = dve(lambda: V.reciprocal(den, den), q3)
        q4 = dve(lambda: V.tensor_tensor(t1, nre, lre, ALU.mult), q, q3)
        q5 = dve(lambda: V.tensor_tensor(t2, aim, lim, ALU.mult), q2, q3)
        q4 = dve(lambda: V.tensor_tensor(t1, t1, t2, ALU.add), q4, q5)
        q_zr = dve(lambda: V.tensor_tensor(zre, t1, den, ALU.mult), q4, q3)
        q4 = dve(lambda: V.tensor_tensor(t1, aim, lre, ALU.mult), q_zr)
        q5 = dve(lambda: V.tensor_tensor(t2, nre, lim, ALU.mult), q_zr)
        q4 = dve(lambda: V.tensor_tensor(t1, t1, t2, ALU.subtract), q4, q5)
        q_zi = dve(lambda: V.tensor_tensor(zim, t1, den, ALU.mult), q4)
        cre, cim = cz[:, :, 0, :], cz[:, :, 1, :]
        q = dve(lambda: V.tensor_tensor(cz[:, :, 2, :], cre, wide(zre, 32), ALU.mult), q_cz, q_zr)
        q1 = dve(lambda: V.tensor_tensor(cz[:, :, 3, :], cre, wide(zim, 32), ALU.mult), q_zi, q_cz)
        q2 = dve(lambda: V.tensor_tensor(cre, cim, wide(zim, 32), ALU.mult), q, q1, q_zi)
        q = dve(lambda: V.tensor_tensor(cz[:, :, 2, :], cz[:, :, 2, :], cre, ALU.subtract), q, q2)
        q2 = dve(lambda: V.tensor_tensor(cim, cim, wide(zre, 32), ALU.mult), q2, q_zr)
        q1 = dve(lambda: V.scalar_tensor_tensor(cz[:, :, 3, :].rearrange("p t c -> p t c"), cz[:, :, 3, :], -1.0, cim, ALU.mult, ALU.subtract), q1, q2)
        q_c0 = dve(lambda: V.tensor_scalar(cre, cz[:, :, 2, :], -1.0, None, ALU.mult), q)
        q_cz = [q, q1, q_c0]
        q = dve(lambda: V.tensor_scalar(t1, tr, 128.0, None, ALU.mult), q_zi)
        q1 = dve(lambda: V.tensor_scalar(t2, t1, MAGIC, MAGIC, ALU.add, ALU.subtract), q)
        q = dve(lambda: V.tensor_tensor(t1, t1, t2, ALU.subtract), q1)
        q1 = dve(lambda: V.scalar_tensor_tensor(t2, t1, -1.0, t1, ALU.mult, ALU.max), q)
        q1 = dve(lambda: V.tensor_scalar(t2, t2, -float(2 * np.pi), float(np.pi / 2), ALU.mult, ALU.add), q1)
        q2 = dve(lambda: V.tensor_scalar(t1, t1, float(2 * np.pi), 3.1415925, ALU.mult, ALU.min), q1)
        q2 = dve(lambda: V.tensor_scalar(t1, t1, -3.1415925, None, ALU.max), q2)
        q_h = [act(lambda: nc.scalar.activation(th2, t2, ACT.Sin), q1), act(lambda: nc.scalar.activation(t3, t1, ACT.Sin), q2)]

        uT = sb("uT", [P, 8, S], F32, s6)
        prenorm(q_x4, "mix_pre", 8)
        us = h
        q_us = [[], []]
        for c in range(2):
            banks, toks = whole(stream(f"si{c}", 8, main))
            for j in range(2):
                q = act(lambda j=j, c=c, b=banks[j]: nc.scalar.activation(us[:, j, c * 512:(c + 1) * 512], b.t[:, :], ACT.Copy), toks[j])
                banks[j].free = [q]
                q_us[j].append(q)
        q_ut = to_heads_T(us, uT, 8, q_us)
        s8 = ExitStack()
        ra = [sb(f"ra{i}", [P, 2, 2, P], F32, s8) for i in range(2)]
        rb = [sb(f"rb{i}", [P, 2, 2, P], F32, s8) for i in range(2)]
        rz = [sb(f"rz{i}", [P, 2, 2, P], F32, s8) for i in range(2)]
        last = sb("last", [P, 2, 32], F32, s8)
        ybuf = uT
        free_r = [[], []]
        free_z = [[], []]
        q_last = []
        q_y5 = []
        q_ini = None
        for half_ in range(2):
            cols = slice(half_ * P, (half_ + 1) * P)
            ybank = None
            for s2_ in range(16):
                i = s2_ % 2
                b = bank()
                m_, q_ = s2_ // 4, s2_ % 4
                pair = (8 * m_ + q_, 8 * m_ + 4 + q_)
                for u_ in range(2):
                    t = pair[u_]
                    p0, kt = 32 * (t % 4), t // 4
                    for ri in range(2):
                        o = b.t[:, (2 * u_ + ri) * P:(2 * u_ + ri + 1) * P]
                        l, r = bz[p0:p0 + 32, kt, ri, :], uT[p0:p0 + 32, kt, cols]
                        q = pe(lambda o=o, l=l, r=r, p0=p0: T.matmul(o, l, r, start=True, stop=True, tile_position=(p0, 0)),
                               q_ut, q_bz, b.free, sig=(u_ == 1 and ri == 1))
                b4 = b.t[:, :].rearrange("p (t r s) -> p t r s", t=2, r=2)
                tt = slice(pair[0], pair[1] + 1, 4)
                c4 = ct[:, tt, :].unsqueeze(2).to_broadcast([P, 2, 2, P])
                n4 = stb[:, tt, :].unsqueeze(2).to_broadcast([P, 2, 2, P])
                A_, B_, Z_, C_, S_ = ra[i], rb[i], rz[i], ra[i], rb[i]
                q1 = dve(lambda A_=A_, b4=b4, c4=c4: V.tensor_tensor(A_[:, :, :, :], b4, c4, ALU.mult), q, q_ct, free_r[i])
                q2 = dve(lambda B_=B_, b4=b4, n4=n4: V.tensor_tensor(B_[:, :, :, :], b4, n4, ALU.mult), q, q_st, free_r[i])
                b.free = [q2]
                q3 = [pool(lambda A_=A_, B_=B_: G.tensor_tensor(A_[:, :, 0, :], A_[:, :, 0, :], B_[:, :, 1, :], ALU.add), q1, q2),
                      pool(lambda A_=A_, B_=B_: G.tensor_tensor(A_[:, :, 1, :], A_[:, :, 1, :], B_[:, :, 0, :], ALU.subtract), q1, q2)]
                if half_ == 1:
                    for ri, ini in enumerate((i_re, i_im)):
                        q3.append(dve(lambda A_=A_, ri=ri, ini=ini, tt=tt: V.tensor_tensor(
                            A_[:, :, ri, 0], A_[:, :, ri, 0], ini[:, tt], ALU.add), q3[0:2], q_ini))
                q4 = []
                for u_ in range(2):
                    t = pair[u_]
                    for ri in range(2):
                        q4.append(dve(lambda Z_=Z_, A_=A_, u_=u_, ri=ri, t=t: V.tensor_tensor_scan(
                            Z_[:, u_, ri, :], d0[:, t, :], A_[:, u_, ri, :], 0.0, ALU.mult, ALU.add), q3, q_d0, free_z[i]))
                if half_ == 0:
                    for ri in range(2):
                        q_last.append(pool(lambda Z_=Z_, ri=ri, tt=tt: G.tensor_copy(last[:, ri, tt], Z_[:, :, ri, P - 1]), q4))
                q5 = dve(lambda C_=C_, Z_=Z_, c4=c4: V.tensor_tensor(C_[:, :, :, :], Z_[:, :, :, :], c4, ALU.mult), q4, free_z[i])
                q6 = pool(lambda S_=S_, Z_=Z_, n4=n4: G.tensor_tensor(S_[:, :, :, :], Z_[:, :, :, :], n4, ALU.mult), q4, free_z[i], q_st)
                for u_ in range(2):
                    t = pair[u_]
                    p0, kt = 32 * (t % 4), t // 4
                    if t % 16 == 0:
                        ybank = bank()
                        ybank.held = True
                        yfree = ybank.free
                    o = ybank.t[p0:p0 + 32, (kt % 4) * P:(kt % 4 + 1) * P]
                    terms = ((2, C_[:, u_, 0, :]), (0, S_[:, u_, 1, :]), (3, S_[:, u_, 0, :]), (3, C_[:, u_, 1, :]))
                    for n_, (w, m) in enumerate(terms):
                        q = pe(lambda o=o, w=w, m=m, t=t, n_=n_, p0=p0: T.matmul(o, cz[:, t, w, :], m, start=(n_ == 0), stop=(n_ == 3),
                                                                                 tile_position=(0, p0)),
                               q5, q6, q_cz, yfree, sig=(n_ == 3))
                free_r[i] = [q]
                free_z[i] = [q5, q6]
                if t % 16 == 15:
                    for k4 in range(4):
                        kt = t // 4 - 3 + k4
                        o = ybank.t[:, k4 * P:(k4 + 1) * P]
                        q7 = dve(lambda o=o, kt=kt, cols=cols: V.scalar_tensor_tensor(
                            ybuf[:, kt, cols], uT[:, kt, cols], vcol("d_skip", kt), o, ALU.mult, ALU.add), q)
                        q_y5.append(q7)
                    ybank.free = [q7]
                    ybank.held = False
            if half_ == 0:
                q = dve(lambda: V.tensor_tensor(t1, last[:, 0, :], th2, ALU.mult), q_last, q_h)
                q1 = dve(lambda: V.tensor_tensor(t2, last[:, 1, :], t3, ALU.mult), q_last, q_h)
                q = dve(lambda: V.tensor_tensor(t1, t1, t2, ALU.subtract), q, q1)
                q_i1 = dve(lambda: V.tensor_tensor(i_re, t1, mag, ALU.mult), q)
                q = dve(lambda: V.tensor_tensor(t1, last[:, 0, :], t3, ALU.mult), q_i1)
                q1 = dve(lambda: V.tensor_tensor(t2, last[:, 1, :], th2, ALU.mult), q_i1)
                q = dve(lambda: V.tensor_tensor(t1, t1, t2, ALU.add), q, q1)
                q_ini = [q_i1, dve(lambda: V.tensor_tensor(i_im, t1, mag, ALU.mult), q)]
        q_g5 = act(lambda: nc.scalar.activation(ybuf[:, :, :], ybuf[:, :, :], ACT.Gelu_apprx_tanh), q_y5)
        for kb in range(4):
            k2_ = slice(2 * kb, 2 * kb + 2)
            q = act(lambda k2_=k2_: nc.scalar.activation(main.hi[:, k2_, :], ybuf[:, k2_, :], ACT.Copy), q_g5, q_ut)
            q = dve(lambda k2_=k2_: V.tensor_tensor(main.lo[:, k2_, :], ybuf[:, k2_, :], main.hi[:, k2_, :].bitcast(F32), ALU.subtract), q)
            main.tok[2 * kb] = main.tok[2 * kb + 1] = q
        q_yg = [[], []]
        for c in range(2):
            banks, toks = whole(stream(f"sg{c}", 8, main))
            for j in range(2):
                o = h[:, j, c * 512:(c + 1) * 512]
                q = act(lambda o=o, b=banks[j]: nc.scalar.activation(o, b.t[:, :], ACT.Sigmoid), toks[j])
                banks[j].free = [q]
                b = bank()
                for k4 in range(4):
                    q2 = transpose(b.t[:, k4 * P:(k4 + 1) * P], ybuf[:, 4 * c + k4, j * P:(j + 1) * P], P, q_g5, b.free, sig=(k4 == 3))
                q = dve(lambda o=o, b=b: V.tensor_tensor(o, o, b.t[:, :], ALU.mult), q, q2)
                b.free = [q]
                q_yg[j].append(q)
        to_acts(h, q_yg, main, 8)
        s8.close()
        s6.close()
        q_x5 = postnorm(["so0", "so1"], 8, main, [])
        q_x6 = swiglu(1, q_x5)
        for j in range(2):
            dma(out[j * P:(j + 1) * P, :], x[:, j, :], s_out, q_x6[j])

        block = ctx.enter_context(nc.Block())

        @block.sync
        def _(eng):
            seen = {}
            for fn, waits, s in sp_items:
                for sm, v in waits:
                    if seen.get(id(sm), 0) < v:
                        eng.wait_ge(sm, v)
                        seen[id(sm)] = v
                fn().then_inc(s, 16)
            eng.wait_ge(s_out, dma_sems[s_out])

        @block.scalar
        def _(eng):
            act.play(eng)

        @block.vector
        def _(eng):
            dve.play(eng)

        @block.gpsimd
        def _(eng):
            pool.play(eng)

        @block.tensor
        def _(eng):
            pe.play(eng)


def constants():
    t = np.arange(P)
    con = np.zeros((P, NCON), np.float32)

    def put(name, a):
        con[:, CON_AT[name]:CON_AT[name] + a.shape[1]] = a

    def level(n):
        same = (t[:, None] // (2 * n)) == (t[None, :] // (2 * n))
        return (same & (t[:, None] % (2 * n) < n) & (t[None, :] % (2 * n) >= n)).astype(np.float32)

    put("ident", np.eye(P, dtype=np.float32))
    put("bones", np.kron(np.eye(2), np.ones((64, 64))).astype(np.float32))
    put("lev0", level(1))
    put("levs", np.concatenate([level(2 << l) for l in range(6)], 1))
    strict = (t[:, None] < t[None, :]).astype(np.float32)
    incl = (t[:, None] <= t[None, :]).astype(np.float32)
    put("mask4", np.concatenate([strict, incl, strict, incl], 1))
    put("iota", np.broadcast_to(t.astype(np.float32), (P, P)))
    half = 8
    inv = np.float32(500000.0) ** (-np.arange(half, dtype=np.float32) / np.float32(half))
    put("invf", np.broadcast_to(inv.astype(np.float32), (P, half)))
    words = np.concatenate([np.eye(P), np.zeros((P, P)), np.where(t[None, :] > t[:, None], -1e30, 0.0)], 1).astype(np.float32)
    return con, (words.view(np.uint32) >> 16).astype(np.uint16).view(np.int16)


def arrays_of(inputs):
    I = {k: np.asarray(v) for k, v in inputs.items()}
    out = {"x": np.ascontiguousarray(I["x"][0])}
    out["con"], out["mask"] = constants()

    def cols(a, n):
        a = a.reshape(-1)
        if a.size < n * P:
            a = np.concatenate([a, np.zeros(n * P - a.size, a.dtype)])
        return a.reshape(n, P).T

    cw = I["ffn_conv_w"][0]
    parts = {
        "norm1_g": I["norm1_g"], "rwkv_mu": I["rwkv_mu"], "decay_bias": I["decay_bias"], "aaa_bias": I["aaa_bias"],
        "k_k": I["rwkv_k_k"], "k_a": I["rwkv_k_a"], "r_k": I["rwkv_r_k"], "ln_g": I["rwkv_ln_g"], "ln_b": I["rwkv_ln_b"],
        "norm2_g": I["norm2_g"], "conv_w0": cw[0], "conv_w1": cw[1], "conv_w2": cw[2], "conv_b": I["ffn_conv_b"],
        "b_f": I["fox_b_f_2"], "log_dt": np.repeat(I["s5_log_dt_2"].reshape(-1), 64), "lam_re": I["s5_lam_re_2"],
        "lam_im": I["s5_lam_im_2"], "d_skip": I["s5_d_2"], "mix_pre": I["mix_pre_gain_2"], "ffn_pre": I["ffn_pre_gain_2"],
    }
    out["vec"] = np.concatenate([cols(parts[n], k) for n, k in VEC_TILES], 1)
    rows = lambda a: np.broadcast_to(a.reshape(1, -1), (P, a.size))
    out["qkg"] = np.stack([rows(I["q_norm_g"]), rows(I["k_norm_g"]), rows(I["q_norm_g"]), rows(I["k_norm_g"])], 1)
    out["fg4"] = np.stack([rows(I["fox_q_gain_2"]), rows(I["fox_k_gain_2"])], 1)
    out["posi"] = I["positions"].reshape(2, P).T
    out["wlora"] = np.concatenate([np.concatenate([I["w_decay_up"][0], I["w_aaa_up"][0]], 0), I["w_gate_up"][0][:P]], 1)
    out["wg2"] = I["w_gate_up"][0][P:]
    fw = I["fox_w_in_2"][0]
    out["wf"] = fw[:, 4096:].reshape(8, P, 16).transpose(1, 0, 2)
    mp, fp = I["mix_post_gain_2"], I["ffn_post_gain_2"]
    out["post"] = np.stack([mp[0], fp[0], mp[1], fp[1]])
    bz = np.zeros((8, 4, 2, 16, 2, 2, 64), np.float32)
    cz = np.zeros((32, 2, 2, 64, 2, 16), np.float32)
    for ri, (bn, cn) in enumerate((("s5_b_re_2", "s5_c_re_2"), ("s5_b_im_2", "s5_c_im_2"))):
        b = I[bn][0].reshape(8, 4, 2, 64, 16).transpose(0, 1, 2, 4, 3)
        c = I[cn][0].reshape(32, 2, 16, 64).transpose(0, 1, 3, 2)
        for g in range(2):
            bz[:, :, g, :, ri, g, :] = b[:, :, g]
            cz[:, ri, g, :, g, :] = c[:, g]
    out["bz"] = bz.reshape(8, P, 2, P).transpose(1, 0, 2, 3)
    out["cz"] = cz.reshape(32, 2, P, 32).transpose(2, 0, 1, 3)

    wi = I["w_in"][0]
    r0, m0 = 0, 1824
    g0 = m0 + 1536
    src = {}
    for i, n in enumerate(("mq", "mk", "mv")):
        src[n] = wi[:, m0 + 512 * i:m0 + 512 * (i + 1)]
    for i, n in enumerate(("wr", "wk", "wv")):
        src[n] = wi[:, 512 * i:512 * (i + 1)]
    src["wl"] = wi[:, 1536:1824]
    for i in range(4):
        src[f"g{i}"] = wi[:, g0 + 512 * i:g0 + 512 * (i + 1)]

    def halves(n, a):
        for i in range(2):
            src[f"{n}{i}"] = a[:, 512 * i:512 * (i + 1)]

    def updown(pa, pb, pt, a, b):
        for i in range(5):
            src[f"{pa}{i}"] = a[:, 512 * i:512 * (i + 1)]
            src[f"{pb}{i}"] = b[:, 512 * i:512 * (i + 1)]
        src[pt] = np.concatenate([a[:, 2560:], b[:, 2560:]], 1)

    halves("ba", I["w_branch_a"][0])
    halves("bb", I["w_branch_b"][0])
    halves("wo", I["w_out"][0])
    up = I["w_ffn_up"][0]
    updown("ua", "ub", "ut", up[:, :FF], up[:, FF:])
    halves("dn", I["w_ffn_down"][0])
    for i, n in enumerate(("fq", "fk", "fv", "fg")):
        halves(n, fw[:, 1024 * i:1024 * (i + 1)])
    halves("fo", I["fox_w_out_2"][0])
    halves("si", I["s5_w_in_2"][0])
    halves("sg", I["s5_w_glu_2"][0])
    halves("so", I["s5_w_out_2"][0])
    for l in range(2):
        updown(f"{l}ug", f"{l}uu", f"{l}ut", I["ffn_w_gate_2"][l], I["ffn_w_up_2"][l])
        halves(f"{l}dn", I["ffn_w_down_2"][l])
    for name, nk, w in stream_plan():
        a = src[name]
        assert a.shape == (nk * P, w), (name, a.shape)
        out["w_" + name] = a.reshape(nk // 2, 2, P, w).transpose(0, 2, 1, 3).reshape(nk // 2, P, 2 * w)
    return {k: np.ascontiguousarray(v) for k, v in out.items()}


def kernel(**inputs):
    import concourse.bacc as bacc
    from concourse.bass_utils import run_bass_kernel_spmd

    arrays = arrays_of(inputs)
    nc = bacc.Bacc("TRN2", target_bir_lowering=False, num_devices=1)
    A = {k: nc.dram_tensor("in_" + k, a.shape, mybir.dt.from_np(a.dtype), kind="ExternalInput").ap() for k, a in arrays.items()}
    out = nc.dram_tensor("out_x", (S, D), F32, kind="ExternalOutput").ap()
    program(nc, A, out)
    r = run_bass_kernel_spmd(nc, [{"in_" + k: a for k, a in arrays.items()}], core_ids=[0])
    return r.results[0]["out_x"].reshape(1, S, D)
```

```python
from contextlib import ExitStack

import numpy as np

import concourse.bass as bass
from concourse import mybir

ALU = mybir.AluOpType
ACT = mybir.ActivationFunctionType
F32 = mybir.dt.float32
F32R = mybir.dt.float32r
BF16 = mybir.dt.bfloat16
I32 = mybir.dt.int32
AX = mybir.AxisListType.X

P = 128
S = 256
D = 1024
FF = 2816
NR = 6
NS = 4
LOOK = 2
MAGIC = 12582912.0
RSQ = 0x5F3759DF - (1 << 31)
E05 = float(np.exp(np.float32(-0.5)))


def stream_plan():
    plan = [("mq", 8, 512), ("mk", 8, 512), ("mv", 8, 512)]
    plan += [("wr", 8, 512), ("wk", 8, 512), ("wv", 8, 512), ("wl", 8, 288)]
    plan += [(f"g{i}", 8, 512) for i in range(4)]
    for c in range(2):
        plan += [(f"ba{c}", 4, 512), (f"bb{c}", 4, 512)]
    plan += [("wo0", 8, 512), ("wo1", 8, 512)]
    for i in range(5):
        plan += [(f"ua{i}", 8, 512), (f"ub{i}", 8, 512)]
    plan += [("ut", 8, 512)]
    plan += [("dn0", 22, 512), ("dn1", 22, 512)]
    plan += [(f"fq{i}", 8, 512) for i in range(2)] + [(f"fk{i}", 8, 512) for i in range(2)]
    plan += [(f"fv{i}", 8, 512) for i in range(2)] + [(f"fg{i}", 8, 512) for i in range(2)]
    plan += [("fo0", 8, 512), ("fo1", 8, 512)]
    for l in range(2):
        if l == 1:
            plan += [(f"si{i}", 8, 512) for i in range(2)]
            plan += [(f"sg{i}", 8, 512) for i in range(2)]
            plan += [(f"so{i}", 8, 512) for i in range(2)]
        for i in range(5):
            plan += [(f"{l}ug{i}", 8, 512), (f"{l}uu{i}", 8, 512)]
        plan += [(f"{l}ut", 8, 512)]
        plan += [(f"{l}dn0", 22, 512), (f"{l}dn1", 22, 512)]
    return plan


VEC_TILES = [
    ("norm1_g", 8), ("rwkv_mu", 15), ("decay_bias", 4), ("aaa_bias", 4), ("k_k", 4), ("k_a", 4), ("r_k", 4),
    ("ln_g", 4), ("ln_b", 4), ("norm2_g", 8), ("conv_w0", 22), ("conv_w1", 22), ("conv_w2", 22), ("conv_b", 22),
    ("b_f", 1), ("log_dt", 32), ("lam_re", 32), ("lam_im", 32), ("d_skip", 8), ("mix_pre", 16), ("ffn_pre", 16),
]
VEC_AT = {}
_n = 0
for _name, _k in VEC_TILES:
    VEC_AT[_name] = _n
    _n += _k
NVEC = _n

CON = [("ident", 128), ("bones", 128), ("lev0", 128), ("levs", 768), ("mask4", 512), ("iota", 128), ("invf", 8)]
CON_AT = {}
_n = 0
for _name, _k in CON:
    CON_AT[_name] = _n
    _n += _k
NCON = _n


class Queue:

    def __init__(self, sem):
        self.sem, self.n, self.items = sem, 0, []

    def __call__(self, fn, *waits, sig=True):
        self.items.append((fn, list(flat(waits)), sig))
        if sig:
            self.n += 1
        return (self.sem, self.n)

    def play(self, eng):
        seen = {}
        for fn, waits, sig in self.items:
            for s, v in waits:
                if seen.get(id(s), 0) < v:
                    eng.wait_ge(s, v)
                    seen[id(s)] = v
            ins = fn()
            if sig:
                ins.then_inc(self.sem, 1)


def flat(waits):
    for w in waits:
        if w is None:
            continue
        if isinstance(w, list):
            yield from flat(w)
        else:
            yield w


class Bank:

    def __init__(self, t):
        self.t, self.free, self.held = t, [], False


class Acts:

    def __init__(self, hi, lo):
        self.hi, self.lo, self.tok = hi, lo, {}


def program(nc, A, out):
    ctx = ExitStack()
    with ctx:
        def sem(name):
            return ctx.enter_context(nc.semaphore(name))

        def sb(name, shape, dt=F32, stack=None):
            return (stack or ctx).enter_context(nc.sbuf_tensor(name, shape, dt))

        pe, act, dve, pool = (Queue(sem("s_" + n)) for n in ("pe", "act", "dve", "pool"))
        sp_items = []
        dma_sems = {}

        def dma(dst, src, s, *waits):
            dma_sems[s] = dma_sems.get(s, 0) + 16
            sp_items.append((lambda: nc.sync.dma_start(dst, src), list(flat(waits)), s))
            return (s, dma_sems[s])

        V, G, T = nc.vector, nc.gpsimd, nc.tensor

        raw = [sb(f"raw{i}", [P, 1024]) for i in range(NR)]
        whi = [sb(f"whi{i}", [P, 1024], F32R) for i in range(NS)]
        wlo = [sb(f"wlo{i}", [P, 1024], F32R) for i in range(NS)]
        x = sb("x", [P, 2, D])
        h = sb("h", [P, 2, D])
        a_hi = sb("a_hi", [P, 8, S], F32R)
        a_lo = sb("a_lo", [P, 8, S], F32R)
        vec = sb("vec", [P, NVEC])
        con = sb("con", [P, NCON])
        maskw = sb("maskw", [P, 3 * P], mybir.dt.int16)
        maskb = maskw[:, :].bitcast(BF16).rearrange("p (a s) -> p a s", a=3)
        eps = sb("eps", [P, 4])
        st = sb("st", [P, 64])
        nt = sb("nt", [P, 4, 64])
        wps = [Bank(ctx.enter_context(nc.psum_tensor(f"wps{i}", [P, 512], F32))) for i in range(4)]
        tps = [Bank(ctx.enter_context(nc.psum_tensor(f"tps{i}", [P, 512], F32))) for i in range(4)]

        s_raw = [sem(f"s_raw{i}") for i in range(NR)]
        s_x, s_con = [sem("s_x0"), sem("s_x1")], sem("s_con")
        s_gain = sem("s_gain")
        s_out = sem("s_out")
        s_att, s_lora, s_wf, s_fg4, s_bz, s_cz = (sem(n) for n in ("s_att", "s_lora", "s_wf", "s_fg4", "s_bz", "s_cz"))

        def vcol(name, i=0, rows=P):
            return vec[0:rows, VEC_AT[name] + i:VEC_AT[name] + i + 1]

        def vcols(name, n):
            return vec[:, VEC_AT[name]:VEC_AT[name] + n]

        def const(name, n):
            return con[:, CON_AT[name]:CON_AT[name] + n]

        ident = const("ident", P)
        bones = const("bones", P)

        q_x = [dma(x[:, j, :], A["x"][j * P:(j + 1) * P, :], s_x[j]) for j in range(2)]
        q_con = dma(con[:, :], A["con"], s_con)
        q_con = dma(vec[:, :], A["vec"], s_con)
        q_con = dma(maskw[:, :], A["mask"], s_con)
        q_eps = [pool(lambda i=i, v=v: G.memset(eps[:, i:i + 1], v)) for i, v in enumerate((1e-6, 64e-5, 1.0, 0.0))]

        plan = stream_plan()
        slabs = []
        for name, nk, w in plan:
            for kp in range(nk // 2):
                slabs.append((name, kp, w))
        load_tok, split_tok, used_tok = {}, {}, {}
        at = {"load": 0, "split": 0, "use": 0}

        def load_next():
            n = at["load"]
            if n >= len(slabs):
                return
            at["load"] += 1
            name, kp, w = slabs[n]
            load_tok[n] = dma(raw[n % NR][:, 0:2 * w], A["w_" + name][kp], s_raw[n % NR], split_tok.get(n - NR))

        def split_next():
            n = at["split"]
            if n >= len(slabs):
                return
            at["split"] += 1
            w = 2 * slabs[n][2]
            r, hi, lo = raw[n % NR][:, 0:w], whi[n % NS][:, 0:w], wlo[n % NS][:, 0:w]
            q = act(lambda: nc.scalar.activation(hi, r, ACT.Copy), load_tok[n], used_tok.get(n - NS))
            split_tok[n] = dve(lambda: V.tensor_tensor(lo, r, hi.bitcast(F32), ALU.subtract), q)
            load_next()

        for _ in range(NR):
            load_next()

        wpair = [0]
        pending = []
        background = []

        def stream(name, nk, acts):
            i = wpair[0]
            wpair[0] ^= 1
            banks = wps[2 * i:2 * i + 2]
            toks = [None, None]
            for kp in range(nk // 2):
                n = at["use"]
                nm, kk, w = slabs[n]
                assert (nm, kk) == (name, kp), (nm, kk, name, kp)
                while at["split"] <= min(n + LOOK, len(slabs) - 1):
                    split_next()
                hi, lo = whi[n % NS], wlo[n % NS]
                for sub in range(2):
                    k = 2 * kp + sub
                    wh, wl = hi[:, sub * w:(sub + 1) * w], lo[:, sub * w:(sub + 1) * w]
                    for j in range(2):
                        o = banks[j].t[:, 0:w]
                        xh, xl = acts.hi[:, k, j * P:(j + 1) * P], acts.lo[:, k, j * P:(j + 1) * P]
                        first, last = k == 0, k == nk - 1
                        dep = (split_tok[n], acts.tok[k]) + ((banks[j].free,) if first else ())
                        pe(lambda o=o, xh=xh, wh=wh, f=first: T.matmul(o, xh, wh, start=f, stop=False), *dep, sig=False)
                        pe(lambda o=o, xl=xl, wh=wh: T.matmul(o, xl, wh, start=False, stop=False), sig=False)
                        done = last or (sub == 1 and j == 1)
                        t = pe(lambda o=o, xh=xh, wl=wl, l=last: T.matmul(o, xh, wl, start=False, stop=l), sig=done)
                        if last:
                            toks[j] = t
                used_tok[n] = t
                at["use"] += 1
                if kp == min(1, nk // 2 - 1):
                    while pending:
                        pending.pop(0)()
                for g in list(background):
                    if next(g, g) is g:
                        background.remove(g)
                yield
            return banks, toks

        def whole(gen):
            while True:
                try:
                    next(gen)
                except StopIteration as e:
                    return e.value

        def settle():
            while background:
                whole(background.pop(0))

        fillers = []

        def fill(n=1):
            for _ in range(n):
                while fillers:
                    try:
                        next(fillers[0])
                        break
                    except StopIteration:
                        fillers.pop(0)

        def finish():
            while fillers:
                fill()

        def bank():
            for _ in range(4):
                b = tps.pop(0)
                tps.append(b)
                if not b.held:
                    return b
            raise ValueError("no bank")

        def transpose(o, i, n, *waits, sig=False):
            return pe(lambda: T.transpose(o, i, ident[0:n, 0:n]), *waits, sig=sig)

        def rsqrt(dst, src, n, scale, add, *waits):
            m, xh, t = nt[:, 0, 0:n], nt[:, 1, 0:n], nt[:, 2, 0:n]
            y = nt[:, 3, 0:n]
            q = dve(lambda: V.tensor_scalar(m, src, scale, add, ALU.mult, ALU.add), *waits)
            q2 = dve(lambda: V.tensor_scalar(xh, src, scale * 0.5, add * 0.5, ALU.mult, ALU.add), *waits)
            q = dve(lambda: V.tensor_scalar(t.bitcast(I32), m.bitcast(I32), 1, None, ALU.logical_shift_right), q)
            q = dve(lambda: V.tensor_scalar(y.bitcast(I32), t.bitcast(I32), -1.0, float(RSQ), ALU.mult, ALU.add), q)
            for s in range(3):
                o = dst if s == 2 else y
                q = dve(lambda: V.tensor_tensor(t, y, y, ALU.mult), q)
                q = dve(lambda: V.tensor_tensor(t, t, xh, ALU.mult), q, q2)
                q = dve(lambda o=o: V.scalar_tensor_tensor(o, t, 1.5, y, ALU.subtract, ALU.mult), q)
            return q

        class Halves(list):
            pass

        def part(ready, kb):
            return ready[kb // 2] if isinstance(ready, Halves) else ready

        def to_acts(src, ready, acts, nk, gain=None, k0=0, wait_free=(), kbs=None):
            for kb in kbs or range(nk // 2):
                b = bank()
                for sub in range(2):
                    for j in range(2):
                        o = b.t[:, sub * S + j * P:sub * S + (j + 1) * P]
                        i = src[:, j, (2 * kb + sub) * P:(2 * kb + sub + 1) * P]
                        q = transpose(o, i, P, part(ready[j], kb), b.free, q_con, sig=(sub == 1 and j == 1))
                k = k0 + 2 * kb
                if gain is None:
                    o3 = b.t[:, :].rearrange("p (k s) -> p k s", k=2)
                    hi, lo = acts.hi[:, k:k + 2, :], acts.lo[:, k:k + 2, :]
                    qh = act(lambda hi=hi, o3=o3: nc.scalar.activation(hi, o3, ACT.Copy), q, *wait_free)
                    ql = dve(lambda hi=hi, lo=lo, o3=o3: V.tensor_tensor(lo, o3, hi.bitcast(F32), ALU.subtract), qh)
                    acts.tok[k] = acts.tok[k + 1] = ql
                else:
                    for sub in range(2):
                        o = b.t[:, sub * S:(sub + 1) * S]
                        hi, lo, g = acts.hi[:, k + sub, :], acts.lo[:, k + sub, :], gain(k + sub)
                        qh = act(lambda hi=hi, o=o, g=g: nc.scalar.activation(hi, o, ACT.Copy, scale=g), q, *wait_free)
                        acts.tok[k + sub] = qh
                    for sub in range(2):
                        o = b.t[:, sub * S:(sub + 1) * S]
                        hi, lo, g = acts.hi[:, k + sub, :], acts.lo[:, k + sub, :], gain(k + sub)
                        ql = dve(lambda hi=hi, lo=lo, o=o, g=g: V.scalar_tensor_tensor(
                            lo, o, g, hi.bitcast(F32), ALU.mult, ALU.subtract), qh)
                        acts.tok[k + sub] = ql
                b.free = [ql]

        main = Acts(a_hi[:, :, :], a_lo[:, :, :])

        norm = {}

        def prenorm(ready, gname, g0, early=()):
            to_acts(x, ready, main, 8, gain=lambda k: vcol(gname, g0 + k), kbs=[kb for kb in range(4) if kb not in early])
            busy = norm.get("h")

            def root():
                qs = []
                for j in range(2):
                    qs.append(act(lambda j=j: nc.scalar.activation(h[:, j, :], x[:, j, :], ACT.Square,
                                                                   accum_out=st[:, j:j + 1]), ready[j], busy))
                    yield
                norm["tok"] = rsqrt(st[:, 2:4], st[:, 0:2], 2, 1.0 / D, 1e-6, qs)

            norm["r"], norm["tok"] = [st[:, 2:3], st[:, 3:4]], None
            background.insert(0, root())

        def normed(o, i, func, j, *waits):
            assert norm["tok"] is not None
            return act(lambda: nc.scalar.activation(o, i, func, scale=norm["r"][j]), norm["tok"], *waits)

        prenorm(q_x, "norm1_g", 0)

        s1 = ExitStack()
        arena = sb("arena", [P, 101 * 256], F32, s1)

        def view(kb, n):
            at0 = int(round(kb * 256))
            return arena[:, at0:at0 + n]

        yb = view(0, 1024).rearrange("p (j c) -> p j c", j=2)
        gates = view(4, 4096).rearrange("p (j c) -> p j c", j=2)
        mq = view(4, 1024).rearrange("p (j c) -> p j c", j=2)
        mk = view(8, 1024).rearrange("p (j c) -> p j c", j=2)
        mqT = view(12, 1024).rearrange("p (t s) -> p t s", t=4)
        mkT = view(16, 1024).rearrange("p (t s) -> p t s", t=4)
        mv = view(20, 1024).rearrange("p (j c) -> p j c", j=2)
        prob = [view(24, 384), view(25.5, 384)]
        probT = [view(27, 384), view(28.5, 384)]
        sq = view(30, 512)
        rt = view(32, 512).rearrange("p (a n) -> p a n", a=4)
        qkg = sb("qkg", [P, 4, 64], F32, s1)
        posi = sb("posi", [P, 2], I32, s1)
        rope = sb("rope", [P, 6, 2, 8], F32, s1)
        q_m = [dma(qkg[:, :, :], A["qkg"], s_att), dma(posi[:, :], A["posi"], s_att)][-1]

        posf, ang, trn = rope[:, 0, :, 0], rope[:, 1, :, :], rope[:, 2, :, :]
        rsin, rcos, tmp8 = rope[:, 3, :, :], rope[:, 4, :, :], rope[:, 5, :, :]
        invf = const("invf", 8)
        tabs = {}

        def rope_tables():
            q = dve(lambda: V.tensor_copy(posf, posi[:, :]), q_m)
            qa = [dve(lambda j=j: V.tensor_scalar(ang[:, j, :], invf, posf[:, j:j + 1], None, ALU.mult), q, q_con) for j in range(2)]
            q = dve(lambda: V.tensor_scalar(trn, ang, float(1 / (2 * np.pi)), MAGIC, ALU.mult, ALU.add), qa)
            yield
            q = dve(lambda: V.tensor_scalar(trn, trn, MAGIC, None, ALU.subtract), q)
            q2 = dve(lambda: V.scalar_tensor_tensor(ang, trn, -6.28125, ang, ALU.mult, ALU.add), q)
            q = dve(lambda: V.scalar_tensor_tensor(ang, trn, -float(2 * np.pi - 6.28125), ang, ALU.mult, ALU.add), q2)
            yield
            q = dve(lambda: V.tensor_scalar(ang, ang, 3.1415925, -3.1415925, ALU.min, ALU.max), q)
            q2 = dve(lambda: V.scalar_tensor_tensor(tmp8, ang, -1.0, ang, ALU.mult, ALU.max), q)
            q2 = dve(lambda: V.tensor_scalar(tmp8, tmp8, -1.0, float(np.pi / 2), ALU.mult, ALU.add), q2)
            yield
            q = act(lambda: nc.scalar.activation(rsin, ang, ACT.Sin), q)
            tabs["rope"] = act(lambda: nc.scalar.activation(rcos, tmp8, ACT.Sin), q2)
            tabs["gain"] = dve(lambda: V.tensor_scalar(qkg[:, 0:3:2, :], qkg[:, 0:3:2, :], 0.125, None, ALU.mult), q_m)

        background.append(rope_tables())

        def heads(ap, n):
            return ap.rearrange("p (h d) -> p h d", h=n)

        def wide(ap, n):
            return ap.unsqueeze(2).to_broadcast([ap.shape[0], ap.shape[1], n])

        def take_heads(banks, toks, dst, c0, ss, scratch):
            out_t = []
            for j in range(2):
                b = banks[j]
                q1 = normed(dst[:, j, c0:c0 + 512], b.t[:, :], ACT.Copy, j, toks[j])
                b.free = [q1]
                q2 = act(lambda j=j: nc.scalar.activation(scratch, dst[:, j, c0:c0 + 512], ACT.Square), q1, out_t)
                out_t = [dve(lambda j=j: V.tensor_reduce(ss[j], heads(scratch, 8), AX, ALU.add), q2)]
            return out_t

        def norm_heads(dst, j, n, r, g, *waits):
            d = heads(dst[:, j, :], n)
            q1 = dve(lambda: V.tensor_tensor(d, d, wide(r, 64), ALU.mult), *waits)
            gb = g.unsqueeze(1).to_broadcast([P, n, 64])
            return dve(lambda: V.tensor_tensor(d, d, gb, ALU.mult), q1)

        def to_heads_T(src, dst, nt_, ready):
            toks = []
            for kb in range(nt_ // 2):
                b = bank()
                for sub in range(2):
                    for j in range(2):
                        t = transpose(b.t[:, sub * S + j * P:sub * S + (j + 1) * P],
                                      src[:, j, (2 * kb + sub) * P:(2 * kb + sub + 1) * P], P,
                                      ready[j], b.free, q_con, sig=(sub == 1 and j == 1))
                o3 = b.t[:, :].rearrange("p (k s) -> p k s", k=2)
                e = (lambda kb=kb, o3=o3: nc.scalar.activation(dst[:, 2 * kb:2 * kb + 2, :], o3, ACT.Copy))
                b.free = [act(e, t)]
                toks.append(b.free[0])
            return toks

        class Head:
            pass

        def scores(h_, qT, kT, ready, prob_, free, sm, cq=None, ck=None):
            hd = Head()
            p0, t = 64 * (h_ % 2), h_ // 2
            b = bank()
            for j in range(2):
                nk_ = P * (j + 1)
                o = b.t[:, 0:P] if j == 0 else b.t[:, P:3 * P]
                qs, ks = qT[p0:p0 + 64, t, j * P:(j + 1) * P], kT[p0:p0 + 64, t, 0:nk_]
                pe(lambda o=o, qs=qs, ks=ks: T.matmul(o, qs, ks, start=True, stop=False), ready, b.free, sig=False)
                if ck is not None:
                    l, r = ck(h_, nk_)
                    pe(lambda o=o, l=l, r=r: T.matmul(o, l, r, start=False, stop=False), sig=False)
                causal = maskb[:, 2 - j:3, :].rearrange("p a s -> p (a s)")
                q = pe(lambda o=o, causal=causal: T.matmul(o, maskb[:, 0, :], causal, start=False, stop=True), q_con)
            mx, nb, rs = sm
            q1 = dve(lambda: V.tensor_reduce(mx[:, 0:1], b.t[:, 0:P], AX, ALU.max), q)
            q2 = dve(lambda: V.tensor_reduce(mx[:, 1:2], b.t[:, P:3 * P], AX, ALU.max), q)
            if cq is None:
                q3 = dve(lambda: V.tensor_scalar(nb, mx, -1.0, None, ALU.mult), q1, q2, free)
            else:
                q3 = dve(lambda: V.tensor_tensor(mx, mx, cq, ALU.add), q1, q2)
                q3 = dve(lambda: V.scalar_tensor_tensor(nb, mx, -1.0, cq, ALU.mult, ALU.add), q3, free)
            act(lambda: nc.scalar.activation(prob_[:, 0:P], b.t[:, 0:P], ACT.Exp, bias=nb[:, 0:1], accum_out=rs[:, 0:1]), q3, free)
            hd.exp = act(lambda: nc.scalar.activation(prob_[:, P:3 * P], b.t[:, P:3 * P], ACT.Exp, bias=nb[:, 1:2], accum_out=rs[:, 1:2]))
            b.free = [hd.exp]
            return hd

        def across(hd, prob_, probT_, free):
            b = bank()
            for i in range(3):
                q = transpose(b.t[:, i * P:(i + 1) * P], prob_[:, i * P:(i + 1) * P], P, hd.exp, b.free, sig=(i == 2))
            hd.trans = q
            hd.probs = dve(lambda: V.tensor_copy(probT_, b.t[:, 0:3 * P]), q, free)
            b.free = [hd.probs]

        def values(h_, hd, probT_, vt, vready, ob, obfree):
            c = (h_ % 4) * 64
            vv = [vt[:, kb, h_ * 64:(h_ + 1) * 64] for kb in range(2)]
            pe(lambda: T.matmul(ob.t[:, c:c + 64], probT_[:, 0:P], vv[0], start=True, stop=True), hd.probs, vready, obfree, sig=False)
            pe(lambda: T.matmul(ob.t[:, S + c:S + c + 64], probT_[:, P:2 * P], vv[0], start=True, stop=False), sig=False)
            hd.done = pe(lambda: T.matmul(ob.t[:, S + c:S + c + 64], probT_[:, 2 * P:3 * P], vv[1], start=False, stop=True))

        def attention(nh, qT, kT, vt, qkready, vready, dst, prob_, probT_, mx, nb, rs, step, cq=None, ck=None):
            hds = []
            ob = None
            toks = []
            for h_ in range(nh + 2):
                if h_ < nh:
                    i = h_ % 2
                    free = [hds[h_ - 2].trans] if h_ >= 2 else []
                    sm = (mx[:, i, :], nb[:, i, :], rs[:, :, h_])
                    hds.append(scores(h_, qT, kT, qkready, prob_[i], free, sm, cq and cq(h_), ck))
                g = h_ - 2
                if g >= 0:
                    if g % 4 == 0:
                        ob = bank()
                        ob.held = True
                        obfree = ob.free
                    values(g, hds[g], probT_[g % 2], vt, vready, ob, obfree)
                    if g % 4 == 3:
                        r4 = rs[:, :, g - 3:g + 1]
                        q1 = dve(lambda r4=r4: V.reciprocal(r4, r4), hds[g].exp)
                        o4 = ob.t[:, :].rearrange("p (j h d) -> p j h d", j=2, h=4)
                        d4 = dst[:, :, (g - 3) * 64:(g + 1) * 64].rearrange("p j (h d) -> p j h d", h=4)
                        for j in range(2):
                            q2 = dve(lambda j=j, r4=r4, o4=o4, d4=d4: V.tensor_tensor(
                                d4[:, j], o4[:, j], wide(r4[:, j, :], 64), ALU.mult), hds[g].done, q1)
                        ob.free = [q2]
                        ob.held = False
                        toks.append(q2)
                step()
                if 1 <= h_ <= nh:
                    g = h_ - 1
                    across(hds[g], prob_[g % 2], probT_[g % 2], [hds[g - 2].done] if g >= 2 else [])
                step()
            return toks

        mss = st[:, 8:40].rearrange("p (i j h) -> p i j h", i=2, j=2)
        mrs = sb("mrs", [P, 32], F32, s1)
        rr = mrs[:, :].rearrange("p (i j h) -> p i j h", i=2, j=2)
        tk = []
        for i, (nm, dst) in enumerate((("mq", mq), ("mk", mk))):
            banks, toks = whole(stream(nm, 8, main))
            tk += take_heads(banks, toks, dst, 0, [mss[:, i, 0, :], mss[:, i, 1, :]], sq)
        q_r = rsqrt(mrs[:, :], st[:, 8:40], 32, 1.0 / 64, 1e-6, tk)
        q_rot = {}
        for i, dst in enumerate((mq, mk)):
            for j in range(2):
                q = norm_heads(dst, j, 8, rr[:, i, j, :], qkg[:, i, :], q_r, tabs["gain"])
                hv = heads(dst[:, j, :], 8)
                x1, x2 = hv[:, :, 0:8], hv[:, :, 8:16]
                cb = rcos[:, j, :].unsqueeze(1).to_broadcast([P, 8, 8])
                sb_ = rsin[:, j, :].unsqueeze(1).to_broadcast([P, 8, 8])
                r4 = [rt[:, a, 64 * j:64 * j + 64].rearrange("p (h d) -> p h d", h=8) for a in range(4)]
                prev = q_rot.get((0, j))
                for a, (u, c) in enumerate(((x1, cb), (x2, sb_), (x2, cb), (x1, sb_))):
                    qm = pool(lambda a=a, u=u, c=c, r4=r4: G.tensor_tensor(r4[a], u, c, ALU.mult), q, tabs["rope"], prev)
                pool(lambda x1=x1, r4=r4: G.tensor_tensor(x1, r4[0], r4[1], ALU.subtract), qm)
                q_rot[i, j] = pool(lambda x2=x2, r4=r4: G.tensor_tensor(x2, r4[2], r4[3], ALU.add), qm)
        banks, toks = whole(stream("mv", 8, main))
        q_mv = []
        for j in range(2):
            q_mv.append(normed(mv[:, j, :], banks[j].t[:, :], ACT.Copy, j, toks[j]))
            banks[j].free = [q_mv[-1]]
        qk_t = to_heads_T(mq, mqT, 4, [q_rot[0, j] for j in range(2)])
        qk_t += to_heads_T(mk, mkT, 4, [q_rot[1, j] for j in range(2)])

        zr, zk, zv = (view(52 + 4 * i, 1024).rearrange("p (t s) -> p t s", t=4) for i in range(3))
        lor = view(64, 768).rearrange("p (t s) -> p t s", t=3)
        zt = view(67, 1024).rearrange("p (j c) -> p j c", j=2)
        zb = [view(71, 514).rearrange("p (k s) -> p k s", k=2), view(73.25, 514).rearrange("p (k s) -> p k s", k=2)]
        q_zb = [pool(lambda i=i: G.memset(zb[i][:, :, 0:1], 0.0)) for i in range(2)]
        z_tok = {}
        zb_free = [[], []]
        zt_free = [[]]

        def take_z(nm, banks, toks, dst, w, mu0):
            qz = []
            for j in range(2):
                qz.append(normed(zt[:, j, 0:w], banks[j].t[:, 0:w], ACT.Copy, j, toks[j], zt_free[0]))
                banks[j].free = [qz[-1]]
            yield
            tiles = [(i, min(P, w - i * P)) for i in range((w + P - 1) // P)]
            out_t = []
            for kb in range(0, len(tiles), 2):
                grp = tiles[kb:kb + 2]
                b = bank()
                for sub, (i, rows) in enumerate(grp):
                    for j in range(2):
                        q = transpose(b.t[0:rows, sub * S + j * P:sub * S + (j + 1) * P], zt[:, j, i * P:i * P + rows], P,
                                      qz, b.free, q_con, sig=(j == 1))
                ib = (kb // 2) % 2
                z_ = zb[ib]
                n, rows = len(grp), grp[-1][1]
                o3 = b.t[0:rows, 0:n * S].rearrange("p (k s) -> p k s", k=n)
                q = act(lambda z_=z_, o3=o3, n=n, rows=rows: nc.scalar.activation(z_[0:rows, 0:n, 1:S + 1], o3, ACT.Copy), q, zb_free[ib], q_zb)
                b.free = [q]
                d = dst[0:rows, kb:kb + n, :]
                q1 = dve(lambda z_=z_, d=d, n=n, rows=rows: V.tensor_tensor(d, z_[0:rows, 0:n, 0:S], z_[0:rows, 0:n, 1:S + 1], ALU.subtract), q)
                zb_free[ib] = []
                for sub in range(n):
                    mu = vcol("rwkv_mu", mu0 + kb + sub, rows)
                    q2 = dve(lambda z_=z_, d=d, sub=sub, mu=mu, rows=rows: V.scalar_tensor_tensor(
                        d[:, sub, :], d[:, sub, :], mu, z_[0:rows, sub, 1:S + 1], ALU.mult, ALU.add), q1, q_con)
                    zb_free[ib].append(q2)
                    out_t.append(q2)
                yield
            zt_free[0] = [q]
            z_tok[nm] = out_t

        def rwkv_inputs():
            for nm, dst, w, m0 in (("wr", zr, 512, 0), ("wk", zk, 512, 4), ("wv", zv, 512, 8), ("wl", lor, 288, 12)):
                banks, toks = yield from stream(nm, 8, main)
                yield from take_z(nm, banks, toks, dst, w, m0)

        fillers.append(rwkv_inputs())
        mmx = sb("mmx", [P, 2, 2], F32, s1)
        mnb = sb("mnb", [P, 2, 2], F32, s1)
        msum = sb("msum", [P, 2, 8], F32, s1)
        q_yb = attention(8, mqT, mkT, mv, qk_t, q_mv, yb, prob, probT, mmx, mnb, msum, fill)
        finish()

        q_gates = {}

        def gate_groups():
            for g in range(4):
                banks, toks = yield from stream(f"g{g}", 8, main)
                for j in range(2):
                    o = gates[:, j, g * 512:(g + 1) * 512]
                    q = normed(o, banks[j].t[:, :], ACT.Sigmoid, j, toks[j])
                    banks[j].free = [q]
                    q_gates[g, j] = q
                q_gates["pe"] = toks[1]
                yield

        fillers.append(gate_groups())

        def v48(kb, n=1024):
            return view(kb, n).rearrange("p (t s) -> p t s", t=4)

        AR = view(20, 2048).rearrange("p (t c a s) -> p t c a s", t=4, c=2, a=2)
        btl, ktl = (view(kb, 1024).rearrange("p (t c s) -> p t c s", t=4, c=2) for kb in (28, 32))
        Vt = view(36, 1024).rearrange("p (c n) -> p c n", c=2)
        Bt, Kt = view(40, 512), view(42, 512)
        bon, gg = v48(44), v48(48)
        cs = view(76, 1032).rearrange("p (n s) -> p n s", n=8)
        Wp = view(80.25, 1032).rearrange("p (n s) -> p n s", n=8)
        Wn = view(84.5, 1024).rearrange("p (n s) -> p n s", n=8)
        av, kk, tm = v48(88.5), v48(92.5), v48(96.5)
        wlo_sb = sb("wlora", [P, 512 * 2], F32, s1)
        wg2 = sb("wgate2", [32, 512], F32, s1)
        fac = sb("fac", [P, 2, 4], F32, s1)
        q_wl = dma(wlo_sb[:, :], A["wlora"], s_lora)
        q_wl = dma(wg2[:, :], A["wg2"], s_lora)
        wda, wgu = wlo_sb[:, 0:512], wlo_sb[:, 512:1024]

        qt = z_tok["wl"]
        q_th = act(lambda: nc.scalar.activation(lor[0:64, 0, :], lor[0:64, 0, :], ACT.Tanh), qt)
        q_sg = act(lambda: nc.scalar.activation(lor[:, 1, :], lor[:, 1, :], ACT.Sigmoid), qt)
        q_sg = act(lambda: nc.scalar.activation(lor[0:32, 2, :], lor[0:32, 2, :], ACT.Sigmoid), qt)
        q_dec, q_a, q_g = [], [], []
        for kb in range(2):
            for what in range(3):
                b = bank()
                for sub in range(2):
                    t = 2 * kb + sub
                    o = b.t[:, sub * S:(sub + 1) * S]
                    if what < 2:
                        r = slice(64 * what, 64 * what + 64)
                        w, z_ = wda[r, t * P:(t + 1) * P], lor[r, 0, :]
                        q = pe(lambda o=o, w=w, z_=z_: T.matmul(o, w, z_, start=True, stop=True), q_th, qt, q_wl, b.free)
                    else:
                        w, w2 = wgu[:, t * P:(t + 1) * P], wg2[:, t * P:(t + 1) * P]
                        pe(lambda o=o, w=w: T.matmul(o, w, lor[:, 1, :], start=True, stop=False), q_sg, q_wl, b.free, sig=False)
                        q = pe(lambda o=o, w2=w2: T.matmul(o, w2, lor[0:32, 2, :], start=False, stop=True))
                for sub in range(2):
                    t = 2 * kb + sub
                    o = b.t[:, sub * S:(sub + 1) * S]
                    if what == 0:
                        f = act(lambda t=t, o=o: nc.scalar.activation(tm[:, t, :], o, ACT.Sigmoid, bias=vcol("decay_bias", t)), q)
                        q_dec.append(f)
                    elif what == 1:
                        f = act(lambda t=t, o=o: nc.scalar.activation(av[:, t, :], o, ACT.Sigmoid, bias=vcol("aaa_bias", t)), q)
                        q_a.append(f)
                    else:
                        f = act(lambda t=t, o=o: nc.scalar.activation(gg[:, t, :], o, ACT.Copy), q)
                        q_g.append(f)
                b.free = [f]
        fill(2)

        q0 = dve(lambda: V.memset(cs[:, :, 0:1], 0.0), z_tok["wl"])
        qs = []
        one = eps[:, 2:3].to_broadcast([P, P])
        for t in range(4):
            for c in range(2):
                qs.append(dve(lambda t=t, c=c: V.tensor_tensor_scan(
                    cs[:, 2 * t + c, 1:P + 1], one, tm[:, t, c * P:(c + 1) * P], 0.0, ALU.mult, ALU.add), q_dec, q_eps))
        q = dve(lambda: V.tensor_tensor(Wp[:, :, :], cs[:, :, :], cs[:, :, 64:65].to_broadcast([P, 8, P + 1]), ALU.subtract), qs, q0)
        q_wn = act(lambda: nc.scalar.activation(Wn[:, :, :], Wp[:, :, 1:P + 1], ACT.Exp, scale=E05), q)
        q_wp = act(lambda: nc.scalar.activation(Wp[:, :, :], Wp[:, :, :], ACT.Exp, scale=-E05), q, q_wn)

        def per_head_sums(src, ready):
            res = []
            for kb in range(2):
                b = bank()
                for sub in range(2):
                    o, i = b.t[:, sub * S:(sub + 1) * S], src[:, 2 * kb + sub, :]
                    q = pe(lambda o=o, i=i: T.matmul(o, bones, i, start=True, stop=True), ready, b.free, q_con)
                res.append((b, q))
            return res

        q = [dve(lambda t=t: V.tensor_scalar(kk[:, t, :], zk[:, t, :], vcol("k_k", t), None, ALU.mult), z_tok["wk"]) for t in range(4)]
        q = dve(lambda: V.tensor_tensor(tm, kk, kk, ALU.mult), q, qs)
        fill(1)
        q_in = []
        for kb, (b, qb) in enumerate(per_head_sums(tm, q)):
            o3 = b.t[:, :].rearrange("p (k s) -> p k s", k=2)
            t2 = tm[:, 2 * kb:2 * kb + 2, :]
            f = act(lambda o3=o3, t2=t2: nc.scalar.activation(t2, o3, ACT.Sqrt), qb)
            b.free = [f]
            f = dve(lambda t2=t2: V.tensor_scalar(t2, t2, 1e-12, None, ALU.max), f)
            q_in.append(dve(lambda t2=t2: V.reciprocal(t2, t2), f))
        q_kk = dve(lambda: V.tensor_tensor(kk, kk, tm, ALU.mult), q_in)
        q1 = [dve(lambda t=t: V.tensor_scalar(tm[:, t, :], av[:, t, :], 1.0, vcol("k_a", t), ALU.subtract, ALU.mult), q_a, q_kk) for t in range(4)]
        q_k2 = dve(lambda: V.scalar_tensor_tensor(zk, tm, 1.0, zk, ALU.add, ALU.mult), q1)
        wp1 = Wp[:, :, 1:P + 1].rearrange("p (t c) s -> p t c s", t=4)
        wp0 = Wp[:, :, 0:P].rearrange("p (t c) s -> p t c s", t=4)
        wn = Wn[:, :, :].rearrange("p (t c) s -> p t c s", t=4)

        def tcs(ap):
            return ap.rearrange("p t (c s) -> p t c s", c=2)

        fill(1)
        q_ar = []
        q_bk = []
        q_ka = dve(lambda: V.tensor_tensor(av, kk, av, ALU.mult), q_kk, q1)
        for t in range(4):
            q_ar.append(dve(lambda t=t: V.scalar_tensor_tensor(AR[:, t, :, 0, :], tcs(kk)[:, t], -1.0, wp0[:, t], ALU.mult, ALU.mult), q_kk, q_wp))
            q_ar.append(dve(lambda t=t: V.tensor_tensor(AR[:, t, :, 1, :], tcs(zr)[:, t], wp1[:, t], ALU.mult), z_tok["wr"], q_wp))
            q_bk.append(dve(lambda t=t: V.tensor_tensor(btl[:, t], tcs(av)[:, t], wn[:, t], ALU.mult), q_ka, q_wn))
            q_bk.append(dve(lambda t=t: V.tensor_tensor(ktl[:, t], tcs(zk)[:, t], wn[:, t], ALU.mult), q_k2, q_wn))
        q = dve(lambda: V.reciprocal(fac[:, 0, :], Wp[:, 1:8:2, 0]), q_wp)
        q_fac = dve(lambda: V.tensor_tensor(fac[:, 1, :], fac[:, 0, :], Wp[:, 0:8:2, P], ALU.mult), q)
        q1 = [dve(lambda t=t: V.scalar_tensor_tensor(tm[:, t, :], zr[:, t, :], vcol("r_k", t), zk[:, t, :], ALU.mult, ALU.mult), q_k2) for t in range(4)]
        q_bon = []
        for kb, (b, qb) in enumerate(per_head_sums(tm, q1)):
            o3 = b.t[:, :].rearrange("p (k s) -> p k s", k=2)
            f = dve(lambda o3=o3, kb=kb: V.tensor_tensor(bon[:, 2 * kb:2 * kb + 2, :], o3, zv[:, 2 * kb:2 * kb + 2, :], ALU.mult), qb, z_tok["wv"])
            b.free = [f]
            q_bon.append(f)

        def tokens_on_partitions(src, dst, ready):
            b = bank()
            for t in range(4):
                q = transpose(b.t[:, t * P:(t + 1) * P], src(t), P, ready, b.free, sig=(t == 3))
            b.free = [act(lambda: nc.scalar.activation(dst, b.t[:, :], ACT.Copy), q)]
            return b.free[0]

        q_vt = [tokens_on_partitions(lambda t, c=c: zv[:, t, c * P:(c + 1) * P], Vt[:, c, :], z_tok["wv"]) for c in range(2)]
        q_bt = tokens_on_partitions(lambda t: btl[:, t, 0, :], Bt, q_bk)
        q_kt = tokens_on_partitions(lambda t: ktl[:, t, 0, :], Kt, q_bk)
        early_done = [q_ar, q_bk, q_fac, q_bon, q_vt, q_k2, q_g]

        Sm = view(52, 4096).rearrange("p (h a s) -> p h a s", h=8, a=4)
        Ti = view(68, 1024).rearrange("p (h s) -> p h s", h=8)
        TT = view(72, 1024).rearrange("p (h s) -> p h s", h=8)
        M1 = view(76, 1024).rearrange("p (h s) -> p h s", h=8)
        Ao = [view(80, 512).rearrange("p (h s) -> p h s", h=4), view(82, 512).rearrange("p (h s) -> p h s", h=4)]
        RU, U = view(84, 512), view(86, 512)
        S0 = view(88, 256).rearrange("p (t v) -> p t v", t=4)
        Y = v48(89)
        Y2, Y3 = v48(93), v48(97)
        mask4 = const("mask4", 512)
        lev0 = const("lev0", P)
        levs = const("levs", 768).rearrange("p (l s) -> p l s", l=6)

        def both(ap):
            return ap.unsqueeze(1).to_broadcast([P, 4, P])

        q_y = []
        q_s0 = None
        prevU = []
        for c in range(2):
            q_sm = []
            for hh in range(8):
                p0, t = 64 * (hh % 2), hh // 2
                b = bank()
                ar = AR[p0:p0 + 64, t, c, :, :].rearrange("p a s -> p (a s)")
                lb, lk = btl[p0:p0 + 64, t, c, :], ktl[p0:p0 + 64, t, c, :]
                pe(lambda b=b, lb=lb, ar=ar: T.matmul(b.t[:, 0:256], lb, ar, start=True, stop=True), q_ar, q_bk, b.free, sig=False)
                q = pe(lambda b=b, lk=lk, ar=ar: T.matmul(b.t[:, 256:512], lk, ar, start=True, stop=True))
                d = Sm[:, hh].rearrange("p a s -> p (a s)")
                q_sm.append(dve(lambda b=b, d=d: V.tensor_tensor(d, b.t[:, :], mask4, ALU.mult), q, early_done, prevU))
                b.free = [q_sm[-1]]
            q_T, q_TT = [None, None], [None, None]
            q_ao = [[], []]
            for g in range(2):
                hs = slice(4 * g, 4 * g + 4)
                q = pool(lambda hs=hs: G.tensor_tensor(TT[:, hs, :], Sm[:, hs, 0, :], both(lev0), ALU.mult), q_sm[4 * g:4 * g + 4], prevU)
                q_TT[g] = pool(lambda hs=hs: G.tensor_tensor(TT[:, hs, :], TT[:, hs, :], both(ident), ALU.add), q)
            for g in range(2):
                b = bank()
                for i in range(4):
                    q = transpose(b.t[:, i * P:(i + 1) * P], TT[:, 4 * g + i, :], P, q_TT[g], b.free, sig=(i == 3))
                o3 = b.t[:, :].rearrange("p (h s) -> p h s", h=4)
                q_T[g] = act(lambda g=g, o3=o3: nc.scalar.activation(Ti[:, 4 * g:4 * g + 4, :], o3, ACT.Copy), q)
                b.free = [q_T[g]]
            q_m1pe = [None, None]
            for l in range(6):
                q_m1 = [None, None]
                for g in range(2):
                    hs = slice(4 * g, 4 * g + 4)
                    q = pool(lambda g=g, hs=hs, l=l: G.tensor_tensor(Ao[g], Sm[:, hs, 0, :], both(levs[:, l, :]), ALU.mult),
                             q_sm[4 * g:4 * g + 4], q_m1pe[g], early_done)
                    b = bank()
                    for i in range(4):
                        q2 = pe(lambda b=b, g=g, i=i: T.matmul(b.t[:, i * P:(i + 1) * P], Ao[g][:, i, :], Ti[:, 4 * g + i, :],
                                                               start=True, stop=True), q, q_T[g], b.free, sig=(i == 3))
                    q_m1pe[g] = q2
                    o3 = b.t[:, :].rearrange("p (h s) -> p h s", h=4)
                    q_m1[g] = act(lambda hs=hs, o3=o3: nc.scalar.activation(M1[:, hs, :], o3, ACT.Copy), q2)
                    b.free = [q_m1[g]]
                fill(1)
                for g in range(2):
                    hs = slice(4 * g, 4 * g + 4)
                    if l < 5:
                        b = bank()
                        for i in range(4):
                            q2 = pe(lambda b=b, g=g, i=i: T.matmul(b.t[:, i * P:(i + 1) * P], TT[:, 4 * g + i, :], M1[:, 4 * g + i, :],
                                                                   start=True, stop=True), q_m1[g], q_TT[g], b.free, sig=(i == 3))
                        o3 = b.t[:, :].rearrange("p (h s) -> p h s", h=4)
                        q_T[g] = dve(lambda hs=hs, o3=o3: V.tensor_tensor(Ti[:, hs, :], Ti[:, hs, :], o3, ALU.add), q2)
                        b.free = [q_T[g]]
                    b = bank()
                    for i in range(4):
                        q2 = pe(lambda b=b, g=g, i=i: T.matmul(b.t[:, i * P:(i + 1) * P], M1[:, 4 * g + i, :], TT[:, 4 * g + i, :],
                                                               start=True, stop=True), q_m1[g], q_TT[g], b.free, sig=(i == 3))
                    o3 = b.t[:, :].rearrange("p (h s) -> p h s", h=4)
                    q_TT[g] = dve(lambda hs=hs, o3=o3: V.tensor_tensor(TT[:, hs, :], TT[:, hs, :], o3, ALU.add), q2)
                    b.free = [q_TT[g]]
            q_ru = []
            for par in range(2):
                b = bank()
                p0 = 64 * par
                for t in range(4):
                    hh = 2 * t + par
                    o = b.t[:, t * 64:(t + 1) * 64]
                    v_ = Vt[:, c, hh * 64:(hh + 1) * 64]
                    q = pe(lambda o=o, hh=hh, v_=v_, c=c: T.matmul(o, Sm[:, hh, 2, :], v_, start=True, stop=(c == 0)), q_sm, q_vt, b.free)
                    if c == 1:
                        q = pe(lambda o=o, t=t, p0=p0: T.matmul(o, AR[p0:p0 + 64, t, 1, 0, :], S0[p0:p0 + 64, t, :], start=False, stop=True), q_s0)
                d = RU.rearrange("p (t a v) -> p t a v", t=4, a=2)[:, :, par, :]
                o3 = b.t[:, 0:256].rearrange("p (t v) -> p t v", t=4)
                q_ru.append(act(lambda d=d, o3=o3: nc.scalar.activation(d, o3, ACT.Copy), q, early_done))
                b.free = [q_ru[-1]]
            b = bank()
            for hh in range(8):
                o = b.t[:, hh * 64:(hh + 1) * 64]
                q = pe(lambda o=o, hh=hh: T.matmul(o, TT[:, hh, :], RU[:, hh * 64:(hh + 1) * 64], start=True, stop=True), q_ru, q_TT, b.free)
            q_u = act(lambda b=b: nc.scalar.activation(U, b.t[:, :], ACT.Copy), q)
            b.free = [q_u]
            if c == 0:
                b = bank()
                for hh in range(8):
                    p0, t = 64 * (hh % 2), hh // 2
                    o = b.t[p0:p0 + 64, t * 64:(t + 1) * 64]
                    hd = slice(hh * 64, hh * 64 + 64)
                    pe(lambda o=o, hd=hd: T.matmul(o, Bt[:, hd], U[:, hd], start=True, stop=False), q_u, q_bt, b.free, sig=False)
                    q = pe(lambda o=o, hd=hd: T.matmul(o, Kt[:, hd], Vt[:, 0, hd], start=False, stop=True), q_kt, q_vt)
                o3 = b.t[:, 0:256].rearrange("p (t v) -> p t v", t=4)
                q_s0 = dve(lambda o3=o3: V.tensor_tensor(S0, o3, wide(fac[:, 1, :], 64), ALU.mult), q, q_fac)
                b.free = [q_s0]
            b = bank()
            for hh in range(8):
                p0, t = 64 * (hh % 2), hh // 2
                o = b.t[p0:p0 + 64, t * P:(t + 1) * P]
                hd = slice(hh * 64, hh * 64 + 64)
                pe(lambda o=o, hd=hd, hh=hh, c=c: T.matmul(o, Vt[:, c, hd], Sm[:, hh, 3, :], start=True, stop=False), q_u, b.free, sig=False)
                if c == 1:
                    pe(lambda o=o, t=t, p0=p0: T.matmul(o, S0[p0:p0 + 64, t, :], AR[p0:p0 + 64, t, 1, 1, :], start=False, stop=False), sig=False)
                q = pe(lambda o=o, hd=hd, hh=hh: T.matmul(o, U[:, hd], Sm[:, hh, 1, :], start=False, stop=True))
            prevU = [q]
            o3 = b.t[:, :].rearrange("p (t s) -> p t s", t=4)
            q_y.append(act(lambda b=b, o3=o3, c=c: nc.scalar.activation(Y[:, :, c * P:(c + 1) * P], o3, ACT.Copy), q, early_done))
            b.free = [q_y[-1]]

        q_c = []
        for kb, (b, qb) in enumerate(per_head_sums(Y, q_y)):
            o3 = b.t[:, :].rearrange("p (k s) -> p k s", k=2)
            f = dve(lambda o3=o3, kb=kb: V.scalar_tensor_tensor(Y[:, 2 * kb:2 * kb + 2, :], o3, -1.0 / 64, Y[:, 2 * kb:2 * kb + 2, :], ALU.mult, ALU.add), qb, q_c)
            b.free = [f]
            q_c.append(f)
        q = act(lambda: nc.scalar.activation(Y2, Y, ACT.Square), q_c)
        q_v = []
        for kb, (b, qb) in enumerate(per_head_sums(Y2, q)):
            o3 = b.t[:, :].rearrange("p (k s) -> p k s", k=2)
            d = Y3[:, 2 * kb:2 * kb + 2, :]
            f = act(lambda o3=o3, d=d: nc.scalar.activation(d, o3, ACT.Sqrt, bias=eps[:, 1:2], scale=1.0 / 64), qb, q_eps)
            b.free = [f]
            q_v.append(dve(lambda d=d: V.reciprocal(d, d), f))
        q = dve(lambda: V.tensor_tensor(Y, Y, Y3, ALU.mult), q_v)
        q = [dve(lambda t=t: V.tensor_scalar(Y[:, t, :], Y[:, t, :], vcol("ln_g", t), vcol("ln_b", t), ALU.mult, ALU.add), q) for t in range(4)]
        q = dve(lambda: V.tensor_tensor(Y, Y, bon, ALU.add), q, q_bon)
        q = dve(lambda: V.tensor_tensor(Y, Y, gg, ALU.mult), q, q_g)
        finish()
        ya = Acts(a_hi[:, 4:8, :], a_lo[:, 4:8, :])
        ybA = Acts(a_hi[:, 0:4, :], a_lo[:, 0:4, :])
        to_acts(yb, [q_yb, q_yb], ybA, 4, wait_free=(q_gates["pe"],))
        q1 = act(lambda: nc.scalar.activation(ya.hi, Y, ACT.Copy), q, q_gates["pe"])
        q1 = dve(lambda: V.tensor_tensor(ya.lo, Y, ya.hi.bitcast(F32), ALU.subtract), q1)
        for k in range(4):
            ya.tok[k] = q1

        q_h = [[], []]
        for c in range(2):
            ba, ta = whole(stream(f"ba{c}", 4, ya))
            bb, tb = whole(stream(f"bb{c}", 4, ybA))
            for j in range(2):
                d, t2 = h[:, j, c * 512:(c + 1) * 512], view(52 + 2 * (2 * c + j), 512)
                ga, gb = gates[:, j, c * 512:(c + 1) * 512], gates[:, j, 1024 + c * 512:1024 + (c + 1) * 512]
                f = dve(lambda d=d, ga=ga, b=ba[j]: V.tensor_tensor(d, b.t[:, :], ga, ALU.mult), ta[j], q_gates[c, j])
                ba[j].free = [f]
                f2 = dve(lambda t2=t2, gb=gb, b=bb[j]: V.tensor_tensor(t2, b.t[:, :], gb, ALU.mult), tb[j], q_gates[2 + c, j])
                bb[j].free = [f2]
                q_h[j].append(dve(lambda d=d, t2=t2: V.tensor_tensor(d, d, t2, ALU.add), f, f2))
        to_acts(h, q_h, main, 8)
        q_x1 = [Halves(), Halves()]
        for c in range(2):
            banks, toks = whole(stream(f"wo{c}", 8, main))
            for j in range(2):
                xs = x[:, j, c * 512:(c + 1) * 512]
                f = dve(lambda xs=xs, b=banks[j]: V.tensor_tensor(xs, xs, b.t[:, :], ALU.add), toks[j])
                banks[j].free = [f]
                q_x1[j].append([f])
        s1.close()

        s3 = ExitStack()

        def hidden(name, stack):
            return Acts(sb(name + "_hi", [P, 22, S], F32R, stack)[:, :, :], sb(name + "_lo", [P, 22, S], F32R, stack)[:, :, :])

        ffn = hidden("f0", s3)
        at_ = [sb(f"at{i}", [P, 2, 512], F32, s3) for i in range(2)]
        aT = [sb(f"aT{i}", [P, 2, S], F32, s3) for i in range(2)]
        cv = [sb(f"cv{i}", [P, 2, S], F32, s3) for i in range(2)]
        prenorm(q_x1, "norm2_g", 0)
        at_free = [[], []]
        cv_free = [[], []]
        aT_free = [[], []]

        def take(banks, toks, dst, free):
            qs = []
            for j in range(2):
                q = normed(dst[:, j, :], banks[j].t[:, :], ACT.Copy, j, toks[j], free)
                banks[j].free = [q]
                qs.append(q)
            return qs

        def conv_tiles(k0, na, a_src, qa, ca, b_src, qb, cb):
            n = na // 2
            bk, q_a, q_b, q_cv, q_ge, q_pr, q_hi = ({} for _ in range(7))

            def across(u):
                bk[u] = (bank(), bank())
                for b, src, rdy, c0, res in ((bk[u][0], a_src, qa, ca, q_a), (bk[u][1], b_src, qb, cb, q_b)):
                    b.held = True
                    for sub in range(2):
                        for j in range(2):
                            q = transpose(b.t[:, sub * S + j * P:sub * S + (j + 1) * P],
                                          src[:, j, c0 + (2 * u + sub) * P:c0 + (2 * u + sub + 1) * P], P,
                                          rdy[j], b.free, sig=(sub == 1 and j == 1))
                    res[u] = q
                if u == n - 1:
                    at_free[0] = at_free[1] = [q_a[u], q_b[u]]

            def copy_a(u):
                b = bk[u][0]
                a3 = b.t[:, :].rearrange("p (k s) -> p k s", k=2)
                q_a[u] = act(lambda: nc.scalar.activation(aT[u][:, :, :], a3, ACT.Copy), q_a[u], aT_free[u])
                b.free, b.held = [q_a[u]], False

            def convolve(u):
                q_cv[u] = []
                for sub in range(2):
                    k = k0 + 2 * u + sub
                    a_, c_ = aT[u][:, sub, :], cv[u][:, sub, :]
                    w0, w1, w2, bi = (vcol(n_, k) for n_ in ("conv_w0", "conv_w1", "conv_w2", "conv_b"))
                    f = dve(lambda a_=a_, c_=c_, w2=w2, bi=bi: V.tensor_scalar(c_, a_, w2, bi, ALU.mult, ALU.add), q_a[u], cv_free[u])
                    f = dve(lambda a_=a_, c_=c_, w1=w1: V.scalar_tensor_tensor(
                        c_[:, 1:S], a_[:, 0:S - 1], w1, c_[:, 1:S], ALU.mult, ALU.add), f)
                    q_cv[u].append(dve(lambda a_=a_, c_=c_, w0=w0: V.scalar_tensor_tensor(
                        c_[:, 2:S], a_[:, 0:S - 2], w0, c_[:, 2:S], ALU.mult, ALU.add), f))
                aT_free[u] = q_cv[u]

            def gelu(u):
                q_ge[u] = act(lambda: nc.scalar.activation(cv[u][:, :, :], cv[u][:, :, :], ACT.Gelu), q_cv[u])

            def gate(u):
                b = bk[u][1]
                b3 = b.t[:, :].rearrange("p (k s) -> p k s", k=2)
                q_pr[u] = dve(lambda: V.tensor_tensor(cv[u][:, :, :], cv[u][:, :, :], b3, ALU.mult), q_ge[u], q_b[u])
                b.free, b.held = [q_pr[u]], False

            def part_hi(u):
                hi = ffn.hi[:, k0 + 2 * u:k0 + 2 * u + 2, :]
                q_hi[u] = act(lambda: nc.scalar.activation(hi, cv[u][:, :, :], ACT.Copy), q_pr[u])

            def part_lo(u):
                k = k0 + 2 * u
                hi, lo = ffn.hi[:, k:k + 2, :], ffn.lo[:, k:k + 2, :]
                f = dve(lambda: V.tensor_tensor(lo, cv[u][:, :, :], hi.bitcast(F32), ALU.subtract), q_hi[u])
                cv_free[u] = [f]
                ffn.tok[k] = ffn.tok[k + 1] = f

            stages = [across, copy_a, convolve, gelu, gate, part_hi, part_lo]
            for step in range(len(stages) + n - 1):
                for u in range(n):
                    if 0 <= step - u < len(stages):
                        stages[step - u](u)
                yield

        for i in range(5):
            banks, toks = whole(stream(f"ua{i}", 8, main))
            qa = take(banks, toks, at_[0], at_free[0])
            banks, toks = whole(stream(f"ub{i}", 8, main))
            settle()
            qb = take(banks, toks, at_[1], at_free[1])
            background.append(conv_tiles(4 * i, 4, at_[0], qa, 0, at_[1], qb, 0))
        banks, toks = whole(stream("ut", 8, main))
        qa = take(banks, toks, at_[0], at_free[0])
        settle()
        background.append(conv_tiles(20, 2, at_[0], qa, 0, at_[0], qa, 256))
        q_x2 = [Halves(), Halves()]
        for c in range(2):
            banks, toks = whole(stream(f"dn{c}", 22, ffn))
            for j in range(2):
                xs = x[:, j, c * 512:(c + 1) * 512]
                f = dve(lambda xs=xs, b=banks[j]: V.tensor_tensor(xs, xs, b.t[:, :], ALU.add), toks[j])
                banks[j].free = [f]
                q_x2[j].append([f])
            if c == 0:
                pending.append(lambda: to_acts(x, q_x2, main, 8, gain=lambda k: vcol("mix_pre", k), kbs=[0, 1]))
        s3.close()

        gain = [sb("gain0", [P, D])]
        ngain = [0]

        def load_gain(free):
            i = ngain[0]
            ngain[0] += 1
            g = gain[0]
            return g, dma(g[:, :], A["post"][i:i + 1, :].to_broadcast([P, D]), s_gain, free)

        gfree = [[]]
        sq_last = []

        def postnorm(names, nk, acts, xready):
            g, qg = load_gain(gfree[0])
            ss, qt_ = [[], []], [[], []]
            for c in range(2):
                banks, toks = whole(stream(names[c], nk, acts))
                for j in range(2):
                    cols = slice(c * 512, (c + 1) * 512)
                    b = banks[j]
                    f = act(lambda j=j, c=c, b=b: nc.scalar.activation(sqj[:, :], b.t[:, :], ACT.Square,
                                                                      accum_out=st[:, 40 + 2 * j + c:41 + 2 * j + c]), toks[j], sq_last)
                    sq_last[:] = [f]
                    ss[j].append(f)
                    f = dve(lambda j=j, cols=cols, b=b, g=g: V.tensor_tensor(h[:, j, cols], b.t[:, :], g[:, cols], ALU.mult), f, qg)
                    b.free = [f]
                    qt_[j].append(f)
            gfree[0] = [qt_]
            s4 = st[:, 40:44].rearrange("p (j c) -> p j c", j=2)
            q = dve(lambda: V.tensor_tensor(st[:, 44:46], s4[:, :, 0], s4[:, :, 1], ALU.add), ss)
            q = rsqrt(st[:, 46:48], st[:, 44:46], 2, 1.0 / D, 1e-6, q)
            done = [Halves(), Halves()]
            for c in range(2):
                for j in range(2):
                    cols = slice(c * 512, (c + 1) * 512)
                    done[j].append([dve(lambda j=j, cols=cols: V.scalar_tensor_tensor(
                        x[:, j, cols], h[:, j, cols], st[:, 46 + j:47 + j], x[:, j, cols], ALU.mult, ALU.add), q, qt_[j], xready)])
            norm["h"] = [done]
            return done

        sqj = sb("sqj", [P, 512])

        def swiglu(l, xready):
            prenorm(xready, "ffn_pre", 8 * l)
            s5 = ExitStack()
            ffn = hidden(f"f{l + 1}", s5)
            sg = [h[:, :, i * 512:(i + 1) * 512] for i in range(2)]
            sg_free = [[], []]

            def groups(i, qp):
                to_acts_at(sg[i % 2], qp, 4, 4 * i)

            def to_acts_at(src, qp, nk_, k0):
                to_acts(src, qp, ffn, nk_, k0=k0)
                sg_free[(k0 // 4) % 2] = [ffn.tok[k0 + nk_ - 1]]

            for i in range(5):
                banks, toks = whole(stream(f"{l}ug{i}", 8, main))
                s_ = sg[i % 2]
                qs = []
                for j in range(2):
                    q = normed(s_[:, j, :], banks[j].t[:, :], ACT.Silu, j, toks[j], sg_free[i % 2])
                    banks[j].free = [q]
                    qs.append(q)
                banks, toks = whole(stream(f"{l}uu{i}", 8, main))
                qp = []
                for j in range(2):
                    q = dve(lambda j=j, b=banks[j], s_=s_: V.scalar_tensor_tensor(s_[:, j, :], b.t[:, :], norm["r"][j], s_[:, j, :], ALU.mult, ALU.mult), toks[j], qs[j])
                    banks[j].free = [q]
                    qp.append(q)
                pending.append(lambda i=i, qp=qp: groups(i, qp))
            banks, toks = whole(stream(f"{l}ut", 8, main))
            s_ = sg[1]
            qp = []
            for j in range(2):
                q = normed(s_[:, j, 0:256], banks[j].t[:, 0:256], ACT.Silu, j, toks[j], sg_free[1])
                q = dve(lambda j=j, b=banks[j]: V.scalar_tensor_tensor(
                    s_[:, j, 0:256], b.t[:, 256:512], norm["r"][j], s_[:, j, 0:256], ALU.mult, ALU.mult), q)
                banks[j].free = [q]
                qp.append(q)
            to_acts(s_, qp, ffn, 2, k0=20)
            res = postnorm([f"{l}dn0", f"{l}dn1"], 22, ffn, [])
            s5.close()
            return res

        s4_ = ExitStack()
        fq, fk = sb("fq", [P, 2, D], F32, s4_), sb("fk", [P, 2, D], F32, s4_)
        fv = sb("fv", [P, 2, D], F32, s4_)
        fgt = sb("fgt", [P, 2, D], F32, s4_)
        fo = fq
        wf = sb("wf", [P, 8, 16], F32, s4_)
        fprob = [sb(f"fprob{i}", [P, 384], F32, s4_) for i in range(2)]
        fprobT = [sb(f"fprobT{i}", [P, 384], F32, s4_) for i in range(2)]
        fc = sb("fc", [16, 4, S], F32, s4_)
        cqt = sb("cqt", [P, 2, 16], F32, s4_)
        frs = sb("frs", [P, 2, 16], F32, s4_)
        fmx = sb("fmx", [P, 2, 2], F32, s4_)
        fnb = sb("fnb", [P, 2, 2], F32, s4_)
        fg4 = sb("fg4", [P, 2, 64], F32, s4_)
        q_wf = dma(wf[:, :, :], A["wf"], s_wf)
        q_fg4 = dma(fg4[:, :, :], A["fg4"], s_fg4)
        q_fg4 = dve(lambda: V.tensor_scalar(fg4[:, 0, :], fg4[:, 0, :], 0.125, None, ALU.mult), q_fg4)
        prenorm(q_x2, "mix_pre", 0, early=(0, 1))

        tabs = {}

        def forget_gates():
            b = bank()
            for j in range(2):
                o = b.t[:, 16 * j:16 * j + 16]
                for k in range(8):
                    for n_, a_ in enumerate((main.hi, main.lo)):
                        l = a_[:, k, j * P:(j + 1) * P].bitcast(F32)
                        q = pe(lambda k=k, l=l, n_=n_, o=o: T.matmul(o, l, wf[:, k, :], start=(k == 0 and n_ == 0), stop=(k == 7 and n_ == 1)),
                               main.tok[k], q_wf, b.free, sig=(k == 7 and n_ == 1))
            while norm["tok"] is None:
                yield
            q = [normed(cqt[:, j, :], b.t[:, 16 * j:16 * j + 16], ACT.Copy, j, q) for j in range(2)]
            b.free = [q]
            b = bank()
            for j in range(2):
                q2 = transpose(b.t[0:16, j * P:(j + 1) * P], cqt[:, j, :], P, q, b.free, sig=True)
            yield
            q = act(lambda b=b: nc.scalar.activation(f0, b.t[0:16, 0:S], ACT.Identity, bias=vcol("b_f", 0, 16)), q2)
            b.free = [q]
            q1 = dve(lambda: V.scalar_tensor_tensor(f1, f0, -1.0, f0, ALU.mult, ALU.max), q)
            yield
            q1 = act(lambda: nc.scalar.activation(f1, f1, ACT.Exp, scale=-1.0), q1)
            yield
            q1 = act(lambda: nc.scalar.activation(f1, f1, ACT.Ln, bias=eps[0:16, 2:3]), q1, q_eps)
            q2 = dve(lambda: V.tensor_scalar(f0, f0, 0.0, None, ALU.min), q)
            yield
            q2 = dve(lambda: V.tensor_tensor(f0, f0, f1, ALU.subtract), q1, q2)
            yield
            q_c = dve(lambda: V.tensor_tensor_scan(f2, eps[0:16, 2:3].to_broadcast([16, S]), f0, 0.0, ALU.mult, ALU.add), q2)
            tabs["nc"] = dve(lambda: V.tensor_scalar(f3, f2, -1.0, None, ALU.mult), q_c)
            tabs["c"] = q_c

        f0, f1, f2, f3 = (fc[:, i, :] for i in range(4))
        background.append(forget_gates())
        fss = sb("fss", [P, 64], F32, s4_)
        frr = sb("frr", [P, 64], F32, s4_)
        fs4 = fss[:, :].rearrange("p (i j h) -> p i j h", i=2, j=2)
        fr4 = frr[:, :].rearrange("p (i j h) -> p i j h", i=2, j=2)
        tk = []
        for i, (nm, dst) in enumerate((("fq", fq), ("fk", fk))):
            for c in range(2):
                banks, toks = whole(stream(f"{nm}{c}", 8, main))
                tk += take_heads(banks, toks, dst, c * 512, [fs4[:, i, j, 8 * c:8 * c + 8] for j in range(2)], sqj[:, :])
        settle()
        q_c, q_nc = tabs["c"], tabs["nc"]
        b = bank()
        for j in range(2):
            q = transpose(b.t[:, 16 * j:16 * j + 16], f2[:, j * P:(j + 1) * P], 16, q_c, b.free, sig=(j == 1))
        q_cq = act(lambda b=b: nc.scalar.activation(cqt[:, :, :], b.t[:, 0:32].rearrange("p (j h) -> p j h", j=2), ACT.Copy), q)
        b.free = [q_cq]
        q_r = rsqrt(frr[:, :], fss[:, :], 64, 1.0 / 64, 1e-6, tk)
        q_n = {}
        for i, dst in enumerate((fq, fk)):
            for j in range(2):
                q_n[i, j] = norm_heads(dst, j, 16, fr4[:, i, j, :], fg4[:, i, :], q_r, q_fg4)
        q_fv = []
        for c in range(2):
            banks, toks = whole(stream(f"fv{c}", 8, main))
            for j in range(2):
                q = normed(fv[:, j, c * 512:(c + 1) * 512], banks[j].t[:, :], ACT.Copy, j, toks[j])
                banks[j].free = [q]
                q_fv.append(q)
        fqT, fkT = sb("fqT", [P, 8, S], F32, s4_), sb("fkT", [P, 8, S], F32, s4_)
        qk_t = to_heads_T(fq, fqT, 8, [q_n[0, j] for j in range(2)])
        qk_t += to_heads_T(fk, fkT, 8, [q_n[1, j] for j in range(2)])
        q_fgt = {}

        def fox_gates():
            for c in range(2):
                banks, toks = yield from stream(f"fg{c}", 8, main)
                for j in range(2):
                    o = fgt[:, j, c * 512:(c + 1) * 512]
                    q = normed(o, banks[j].t[:, :], ACT.Sigmoid, j, toks[j])
                    banks[j].free = [q]
                    q_fgt[c, j] = q
                yield

        fillers.append(fox_gates())
        half = [0]

        def step4():
            half[0] += 1
            if half[0] % 3 == 0:
                fill()

        q_o = attention(16, fqT, fkT, fv, qk_t + [q_cq, q_nc], q_fv, fo, [p[:, :] for p in fprob], [p[:, :] for p in fprobT],
                        fmx, fnb, frs, step4, cq=lambda h_: cqt[:, :, h_],
                        ck=lambda h_, n_: (ident[0:16, h_:h_ + 1].to_broadcast([16, P]), f3[:, 0:n_]))
        finish()
        q_og = [dve(lambda j=j: V.tensor_tensor(fo[:, j, :], fo[:, j, :], fgt[:, j, :], ALU.mult), q_o, [q_fgt[c, j] for c in range(2)])
                for j in range(2)]
        to_acts(fo, q_og, main, 8)
        s4_.close()
        q_x3 = postnorm(["fo0", "fo1"], 8, main, [])
        s6 = ExitStack()
        ct = sb("ct", [P, 32, P], F32, s6)
        stb = sb("stb", [P, 32, P], F32, s6)
        pr = sb("pr", [P, 16, 32], F32, s6)
        bz = sb("bz", [P, 8, 2, P], F32, s6)
        cz = sb("cz", [P, 32, 4, 32], F32, s6)
        q_bz = dma(bz[:, :, :, :], A["bz"], s_bz, q_x3)
        q_cz = dma(cz[:, :, 0:2, :], A["cz"], s_cz, q_x3)
        dt, mag, th, tr, are, aim, den, zre, zim, t1, t2, nre, i_re, i_im, th2, t3 = (pr[:, i, :] for i in range(16))
        tab = {}

        def s5_tables():
            two_pi = float(2 * np.pi)
            lre, lim = vcols("lam_re", 32), vcols("lam_im", 32)
            iota = const("iota", P)
            q = act(lambda: nc.scalar.activation(dt, vcols("log_dt", 32), ACT.Exp), q_con, q_x3)
            q1 = dve(lambda: V.tensor_tensor(t1, lre, dt, ALU.mult), q)
            tab["mag"] = q_mag = act(lambda: nc.scalar.activation(mag, t1, ACT.Exp), q1)
            yield
            q1 = dve(lambda: V.tensor_tensor(th, lim, dt, ALU.mult), q)
            q1 = dve(lambda: V.tensor_scalar(t2, th, 1 / two_pi, MAGIC, ALU.mult, ALU.add), q1, q_mag)
            q1 = dve(lambda: V.tensor_scalar(t2, t2, MAGIC, None, ALU.subtract), q1)
            q1 = dve(lambda: V.scalar_tensor_tensor(th, t2, -6.28125, th, ALU.mult, ALU.add), q1)
            q1 = dve(lambda: V.scalar_tensor_tensor(th, t2, -(two_pi - 6.28125), th, ALU.mult, ALU.add), q1)
            q_tr = dve(lambda: V.tensor_scalar(tr, th, 1 / two_pi, None, ALU.mult), q1)
            yield
            sines = []
            for g in range(4):
                c, s = ct[:, 8 * g:8 * g + 8, :], stb[:, 8 * g:8 * g + 8, :]
                q = pool(lambda g=g, s=s: G.tensor_tensor(s, wide(tr[:, 8 * g:8 * g + 8], P), iota.unsqueeze(1).to_broadcast([P, 8, P]), ALU.mult), q_tr)
                yield
                q1 = dve(lambda c=c, s=s: V.tensor_scalar(c, s, MAGIC, MAGIC, ALU.add, ALU.subtract), q)
                q = pool(lambda c=c, s=s: G.tensor_tensor(s, s, c, ALU.subtract), q1)
                yield
                yield
                q1 = dve(lambda c=c, s=s: V.scalar_tensor_tensor(c, s, -1.0, s, ALU.mult, ALU.max), q)
                yield
                q1 = dve(lambda c=c: V.tensor_scalar(c, c, -two_pi, two_pi / 4, ALU.mult, ALU.add), q1)
                yield
                q2 = dve(lambda s=s: V.tensor_scalar(s, s, two_pi, 3.1415925, ALU.mult, ALU.min), q, q1)
                yield
                q2 = dve(lambda s=s: V.tensor_scalar(s, s, -3.1415925, None, ALU.max), q2)
                yield
                sines.append((c, s, q1, q2))
            q = dve(lambda: V.tensor_scalar(t1, tr, 128.0, None, ALU.mult), q_tr, q_mag)
            q1 = dve(lambda: V.tensor_scalar(t2, t1, MAGIC, MAGIC, ALU.add, ALU.subtract), q)
            q = dve(lambda: V.tensor_tensor(t1, t1, t2, ALU.subtract), q1)
            q1 = dve(lambda: V.scalar_tensor_tensor(t2, t1, -1.0, t1, ALU.mult, ALU.max), q)
            q1 = dve(lambda: V.tensor_scalar(t2, t2, -two_pi, two_pi / 4, ALU.mult, ALU.add), q1)
            q2 = dve(lambda: V.tensor_scalar(t1, t1, two_pi, 3.1415925, ALU.mult, ALU.min), q1)
            q2 = dve(lambda: V.tensor_scalar(t1, t1, -3.1415925, None, ALU.max), q2)
            yield
            while at["use"] < sine_slab:
                yield
            q_h = [act(lambda: nc.scalar.activation(th2, t2, ACT.Sin), q1), act(lambda: nc.scalar.activation(t3, t1, ACT.Sin), q2)]
            tab["half"] = q_h
            for c, s, q1, q2 in sines:
                q_ct = act(lambda c=c: nc.scalar.activation(c, c, ACT.Sin), q1)
                q_st = act(lambda s=s: nc.scalar.activation(s, s, ACT.Sin), q2)
                yield
                yield
            tab["ct"], tab["st"] = q_ct, q_st
            q = dve(lambda: V.tensor_tensor(are, mag, ct[:, :, 1], ALU.mult), q_ct, q_mag)
            q2 = dve(lambda: V.tensor_tensor(aim, mag, stb[:, :, 1], ALU.mult), q_st, q_mag)
            q = dve(lambda: V.tensor_scalar(nre, are, 1.0, None, ALU.subtract), q)
            q3 = dve(lambda: V.tensor_tensor(t1, lre, lre, ALU.mult), q_h)
            q4 = dve(lambda: V.tensor_tensor(t2, lim, lim, ALU.mult), q_h)
            q3 = dve(lambda: V.tensor_tensor(den, t1, t2, ALU.add), q3, q4)
            q3 = dve(lambda: V.reciprocal(den, den), q3)
            yield
            q4 = dve(lambda: V.tensor_tensor(t1, nre, lre, ALU.mult), q, q3)
            q5 = dve(lambda: V.tensor_tensor(t2, aim, lim, ALU.mult), q2, q3)
            q4 = dve(lambda: V.tensor_tensor(t1, t1, t2, ALU.add), q4, q5)
            q_zr = dve(lambda: V.tensor_tensor(zre, t1, den, ALU.mult), q4, q3)
            q4 = dve(lambda: V.tensor_tensor(t1, aim, lre, ALU.mult), q_zr)
            q5 = dve(lambda: V.tensor_tensor(t2, nre, lim, ALU.mult), q_zr)
            q4 = dve(lambda: V.tensor_tensor(t1, t1, t2, ALU.subtract), q4, q5)
            q_zi = dve(lambda: V.tensor_tensor(zim, t1, den, ALU.mult), q4)
            yield
            cre, cim, c2, c3 = (cz[:, :, i, :] for i in range(4))
            q = dve(lambda: V.tensor_tensor(c2, cre, wide(zre, 32), ALU.mult), q_cz, q_zr)
            yield
            q1 = dve(lambda: V.tensor_tensor(c3, cre, wide(zim, 32), ALU.mult), q_zi, q_cz)
            yield
            q2 = dve(lambda: V.tensor_tensor(cre, cim, wide(zim, 32), ALU.mult), q, q1, q_zi)
            yield
            q = dve(lambda: V.tensor_tensor(c2, c2, cre, ALU.subtract), q, q2)
            yield
            q2 = dve(lambda: V.tensor_tensor(cim, cim, wide(zre, 32), ALU.mult), q2, q_zr)
            yield
            q1 = dve(lambda: V.scalar_tensor_tensor(c3, c3, -1.0, cim, ALU.mult, ALU.subtract), q1, q2)
            yield
            q_c0 = dve(lambda: V.tensor_scalar(cre, c2, -1.0, None, ALU.mult), q)
            tab["cz"] = [q, q1, q_c0]

        sine_slab = at["use"] + 46
        background.append(s5_tables())
        q_x4 = swiglu(0, q_x3)
        settle()
        q_mag, q_h, q_ct, q_st, q_cz = (tab[n] for n in ("mag", "half", "ct", "st", "cz"))

        uT = sb("uT", [P, 8, S], F32, s6)
        prenorm(q_x4, "mix_pre", 8)
        us = h
        q_us = [[], []]
        for c in range(2):
            banks, toks = whole(stream(f"si{c}", 8, main))
            for j in range(2):
                q = normed(us[:, j, c * 512:(c + 1) * 512], banks[j].t[:, :], ACT.Copy, j, toks[j])
                banks[j].free = [q]
                q_us[j].append(q)
        q_ut = to_heads_T(us, uT, 8, q_us)
        s8 = ExitStack()
        ra = [sb(f"ra{i}", [P, 2, 2, P], F32, s8) for i in range(3)]
        rb = [sb(f"rb{i}", [P, 2, 2, P], F32, s8) for i in range(3)]
        rz = [sb(f"rz{i}", [P, 2, 2, P], F32, s8) for i in range(2)]
        rd = [sb(f"rd{i}", [P, 2, 2, P], F32, s8) for i in range(2)]
        q_rd = [pool(lambda i=i: G.memset(rd[i][:, :, :, 0:1], 0.0), q_x4) for i in range(2)]
        last = sb("last", [P, 2, 32], F32, s8)
        ybuf = uT
        free_r = [[], [], []]
        free_z = [[], []]
        q_last = []
        q_y5 = []
        q_ini = None
        for half_ in range(2):
            cols = slice(half_ * P, (half_ + 1) * P)
            ybank = [None, None]
            bu, turned, prod = {}, {}, {}

            def pair_of(n):
                m_, q_ = n // 4, n % 4
                pair = (8 * m_ + q_, 8 * m_ + 4 + q_)
                tt = slice(pair[0], pair[1] + 1, 4)
                c4 = ct[:, tt, :].unsqueeze(2).to_broadcast([P, 2, 2, P])
                n4 = stb[:, tt, :].unsqueeze(2).to_broadcast([P, 2, 2, P])
                return pair, tt, c4, n4, ra[n % 3], rb[n % 3], rz[n % 2]

            def drive(n, cols=cols):
                pair = pair_of(n)[0]
                b = bank()
                for u_ in range(2):
                    t = pair[u_]
                    p0, kt = 32 * (t % 4), t // 4
                    for ri in range(2):
                        o = b.t[:, (2 * u_ + ri) * P:(2 * u_ + ri + 1) * P]
                        l, r = bz[p0:p0 + 32, kt, ri, :], uT[p0:p0 + 32, kt, cols]
                        q = pe(lambda o=o, l=l, r=r, p0=p0: T.matmul(o, l, r, start=True, stop=True, tile_position=(p0, 0)),
                               q_ut, q_bz, b.free, sig=(u_ == 1 and ri == 1))
                bu[n] = (b, q)

            def turn(n, half_=half_, q_ini=q_ini):
                pair, tt, c4, n4, A_, B_, Z_ = pair_of(n)
                b, q = bu.pop(n)
                b4 = b.t[:, :].rearrange("p (t r s) -> p t r s", t=2, r=2)
                q1 = dve(lambda: V.tensor_tensor(A_[:, :, :, :], b4, c4, ALU.mult), q, q_ct, free_r[n % 3])
                q2 = dve(lambda: V.tensor_tensor(B_[:, :, :, :], b4, n4, ALU.mult), q, q_st, free_r[n % 3])
                b.free = [q2]
                turned[n] = [pool(lambda: G.tensor_tensor(A_[:, :, 0, :], A_[:, :, 0, :], B_[:, :, 1, :], ALU.add), q1, q2),
                             pool(lambda: G.tensor_tensor(A_[:, :, 1, :], A_[:, :, 1, :], B_[:, :, 0, :], ALU.subtract), q1, q2)]

            def run(n, half_=half_, q_ini=q_ini):
                pair, tt, c4, n4, A_, B_, Z_ = pair_of(n)
                q3 = turned.pop(n)
                if half_ == 1:
                    q3 = q3 + [dve(lambda ri=ri, ini=ini: V.tensor_tensor(A_[:, :, ri, 0], A_[:, :, ri, 0], ini[:, tt], ALU.add), q3, q_ini)
                               for ri, ini in enumerate((i_re, i_im))]
                D_ = rd[n % 2]
                m4 = mag[:, tt].unsqueeze(2).unsqueeze(3).to_broadcast([P, 2, 2, P - 1])
                qd = act(lambda: nc.scalar.activation(D_[:, :, :, 1:P], m4, ACT.Copy), q_mag, free_z[n % 2])

                def flat3(a):
                    return a[:, :, :, :].rearrange("p t r s -> p (t r s)")

                q4 = dve(lambda: V.tensor_tensor_scan(flat3(Z_), flat3(D_), flat3(A_), 0.0, ALU.mult, ALU.add), q3, qd, q_rd, free_z[n % 2])
                if half_ == 0:
                    q_last.append(act(lambda: nc.scalar.activation(last[:, :, tt], Z_[:, :, :, P - 1].rearrange("p t r -> p r t"), ACT.Copy), q4))
                q5 = dve(lambda: V.tensor_tensor(A_[:, :, :, :], Z_[:, :, :, :], c4, ALU.mult), q4)
                q6 = pool(lambda: G.tensor_tensor(B_[:, :, :, :], Z_[:, :, :, :], n4, ALU.mult), q4, q_st)
                free_z[n % 2] = [q5, q6, q_last[-1]]
                prod[n] = [q5, q6]

            def gather(n, cols=cols):
                pair, tt, c4, n4, A_, B_, Z_ = pair_of(n)
                ready = prod.pop(n)
                for u_ in range(2):
                    t = pair[u_]
                    p0, kt = 32 * (t % 4), t // 4
                    if t % 16 == 0:
                        ybank[0] = bank()
                        ybank[0].held = True
                        ybank[1] = ybank[0].free
                    yb_ = ybank[0]
                    o = yb_.t[p0:p0 + 32, (kt % 4) * P:(kt % 4 + 1) * P]
                    terms = ((2, A_[:, u_, 0, :]), (0, B_[:, u_, 1, :]), (3, B_[:, u_, 0, :]), (3, A_[:, u_, 1, :]))
                    for n_, (w, m) in enumerate(terms):
                        q = pe(lambda o=o, w=w, m=m, t=t, n_=n_, p0=p0: T.matmul(o, cz[:, t, w, :], m, start=(n_ == 0), stop=(n_ == 3),
                                                                                 tile_position=(0, p0)),
                               ready, q_cz, ybank[1], sig=(n_ == 3))
                free_r[n % 3] = [q]
                if t % 16 == 15:
                    for k4 in range(4):
                        kt = t // 4 - 3 + k4
                        o = yb_.t[:, k4 * P:(k4 + 1) * P]
                        q7 = dve(lambda o=o, kt=kt: V.scalar_tensor_tensor(
                            ybuf[:, kt, cols], uT[:, kt, cols], vcol("d_skip", kt), o, ALU.mult, ALU.add), q)
                        q_y5.append(q7)
                    yb_.free = [q7]
                    yb_.held = False

            drive(0)
            drive(1)
            turn(0)
            for n in range(16):
                if n + 2 < 16:
                    drive(n + 2)
                if n + 1 < 16:
                    turn(n + 1)
                run(n)
                if n > 0:
                    gather(n - 1)
            gather(15)
            if half_ == 0:
                q = dve(lambda: V.tensor_tensor(t1, last[:, 0, :], th2, ALU.mult), q_last, q_h)
                q1 = dve(lambda: V.tensor_tensor(t2, last[:, 1, :], t3, ALU.mult), q_last, q_h)
                q = dve(lambda: V.tensor_tensor(t1, t1, t2, ALU.subtract), q, q1)
                q_i1 = dve(lambda: V.tensor_tensor(i_re, t1, mag, ALU.mult), q)
                q = dve(lambda: V.tensor_tensor(t1, last[:, 0, :], t3, ALU.mult), q_i1)
                q1 = dve(lambda: V.tensor_tensor(t2, last[:, 1, :], th2, ALU.mult), q_i1)
                q = dve(lambda: V.tensor_tensor(t1, t1, t2, ALU.add), q, q1)
                q_ini = [q_i1, dve(lambda: V.tensor_tensor(i_im, t1, mag, ALU.mult), q)]
        q_g5 = act(lambda: nc.scalar.activation(ybuf[:, :, :], ybuf[:, :, :], ACT.Gelu_apprx_tanh), q_y5)
        for kb in range(4):
            k2_ = slice(2 * kb, 2 * kb + 2)
            q = act(lambda k2_=k2_: nc.scalar.activation(main.hi[:, k2_, :], ybuf[:, k2_, :], ACT.Copy), q_g5, q_ut)
            q = dve(lambda k2_=k2_: V.tensor_tensor(main.lo[:, k2_, :], ybuf[:, k2_, :], main.hi[:, k2_, :].bitcast(F32), ALU.subtract), q)
            main.tok[2 * kb] = main.tok[2 * kb + 1] = q
        q_yg = [[], []]
        for c in range(2):
            banks, toks = whole(stream(f"sg{c}", 8, main))
            for j in range(2):
                o = h[:, j, c * 512:(c + 1) * 512]
                q = act(lambda o=o, b=banks[j]: nc.scalar.activation(o, b.t[:, :], ACT.Sigmoid), toks[j])
                banks[j].free = [q]
                b = bank()
                for k4 in range(4):
                    q2 = transpose(b.t[:, k4 * P:(k4 + 1) * P], ybuf[:, 4 * c + k4, j * P:(j + 1) * P], P, q_g5, b.free, sig=(k4 == 3))
                q = dve(lambda o=o, b=b: V.tensor_tensor(o, o, b.t[:, :], ALU.mult), q, q2)
                b.free = [q]
                q_yg[j].append(q)
        to_acts(h, q_yg, main, 8)
        s8.close()
        s6.close()
        q_x5 = postnorm(["so0", "so1"], 8, main, [])
        q_x6 = swiglu(1, q_x5)
        for j in range(2):
            dma(out[j * P:(j + 1) * P, :], x[:, j, :], s_out, q_x6[j])

        block = ctx.enter_context(nc.Block())

        @block.sync
        def _(eng):
            seen = {}
            for fn, waits, s in sp_items:
                for sm, v in waits:
                    if seen.get(id(sm), 0) < v:
                        eng.wait_ge(sm, v)
                        seen[id(sm)] = v
                fn().then_inc(s, 16)
            eng.wait_ge(s_out, dma_sems[s_out])

        @block.scalar
        def _(eng):
            act.play(eng)

        @block.vector
        def _(eng):
            dve.play(eng)

        @block.gpsimd
        def _(eng):
            pool.play(eng)

        @block.tensor
        def _(eng):
            pe.play(eng)


def constants():
    t = np.arange(P)
    con = np.zeros((P, NCON), np.float32)

    def put(name, a):
        con[:, CON_AT[name]:CON_AT[name] + a.shape[1]] = a

    def level(n):
        same = (t[:, None] // (2 * n)) == (t[None, :] // (2 * n))
        return (same & (t[:, None] % (2 * n) < n) & (t[None, :] % (2 * n) >= n)).astype(np.float32)

    put("ident", np.eye(P, dtype=np.float32))
    put("bones", np.kron(np.eye(2), np.ones((64, 64))).astype(np.float32))
    put("lev0", level(1))
    put("levs", np.concatenate([level(2 << l) for l in range(6)], 1))
    strict = (t[:, None] < t[None, :]).astype(np.float32)
    incl = (t[:, None] <= t[None, :]).astype(np.float32)
    put("mask4", np.concatenate([strict, incl, strict, incl], 1))
    put("iota", np.broadcast_to(t.astype(np.float32), (P, P)))
    half = 8
    inv = np.float32(500000.0) ** (-np.arange(half, dtype=np.float32) / np.float32(half))
    put("invf", np.broadcast_to(inv.astype(np.float32), (P, half)))
    words = np.concatenate([np.eye(P), np.zeros((P, P)), np.where(t[None, :] > t[:, None], -1e30, 0.0)], 1).astype(np.float32)
    return con, (words.view(np.uint32) >> 16).astype(np.uint16).view(np.int16)


def arrays_of(inputs):
    I = {k: np.asarray(v) for k, v in inputs.items()}
    out = {"x": np.ascontiguousarray(I["x"][0])}
    out["con"], out["mask"] = constants()

    def cols(a, n):
        a = a.reshape(-1)
        if a.size < n * P:
            a = np.concatenate([a, np.zeros(n * P - a.size, a.dtype)])
        return a.reshape(n, P).T

    cw = I["ffn_conv_w"][0]
    parts = {
        "norm1_g": I["norm1_g"], "rwkv_mu": I["rwkv_mu"], "decay_bias": I["decay_bias"], "aaa_bias": I["aaa_bias"],
        "k_k": I["rwkv_k_k"], "k_a": I["rwkv_k_a"], "r_k": I["rwkv_r_k"], "ln_g": I["rwkv_ln_g"], "ln_b": I["rwkv_ln_b"],
        "norm2_g": I["norm2_g"], "conv_w0": cw[0], "conv_w1": cw[1], "conv_w2": cw[2], "conv_b": I["ffn_conv_b"],
        "b_f": I["fox_b_f_2"], "log_dt": np.repeat(I["s5_log_dt_2"].reshape(-1), 64), "lam_re": I["s5_lam_re_2"],
        "lam_im": I["s5_lam_im_2"], "d_skip": I["s5_d_2"], "mix_pre": I["mix_pre_gain_2"], "ffn_pre": I["ffn_pre_gain_2"],
    }
    out["vec"] = np.concatenate([cols(parts[n], k) for n, k in VEC_TILES], 1)
    rows = lambda a: np.broadcast_to(a.reshape(1, -1), (P, a.size))
    out["qkg"] = np.stack([rows(I["q_norm_g"]), rows(I["k_norm_g"]), rows(I["q_norm_g"]), rows(I["k_norm_g"])], 1)
    out["fg4"] = np.stack([rows(I["fox_q_gain_2"]), rows(I["fox_k_gain_2"])], 1)
    out["posi"] = I["positions"].reshape(2, P).T
    out["wlora"] = np.concatenate([np.concatenate([I["w_decay_up"][0], I["w_aaa_up"][0]], 0), I["w_gate_up"][0][:P]], 1)
    out["wg2"] = I["w_gate_up"][0][P:]
    fw = I["fox_w_in_2"][0]
    out["wf"] = fw[:, 4096:].reshape(8, P, 16).transpose(1, 0, 2)
    mp, fp = I["mix_post_gain_2"], I["ffn_post_gain_2"]
    out["post"] = np.stack([mp[0], fp[0], mp[1], fp[1]])
    bz = np.zeros((8, 4, 2, 16, 2, 2, 64), np.float32)
    cz = np.zeros((32, 2, 2, 64, 2, 16), np.float32)
    for ri, (bn, cn) in enumerate((("s5_b_re_2", "s5_c_re_2"), ("s5_b_im_2", "s5_c_im_2"))):
        b = I[bn][0].reshape(8, 4, 2, 64, 16).transpose(0, 1, 2, 4, 3)
        c = I[cn][0].reshape(32, 2, 16, 64).transpose(0, 1, 3, 2)
        for g in range(2):
            bz[:, :, g, :, ri, g, :] = b[:, :, g]
            cz[:, ri, g, :, g, :] = c[:, g]
    out["bz"] = bz.reshape(8, P, 2, P).transpose(1, 0, 2, 3)
    out["cz"] = cz.reshape(32, 2, P, 32).transpose(2, 0, 1, 3)

    wi = I["w_in"][0]
    r0, m0 = 0, 1824
    g0 = m0 + 1536
    src = {}
    for i, n in enumerate(("mq", "mk", "mv")):
        src[n] = wi[:, m0 + 512 * i:m0 + 512 * (i + 1)]
    for i, n in enumerate(("wr", "wk", "wv")):
        src[n] = wi[:, 512 * i:512 * (i + 1)]
    src["wl"] = wi[:, 1536:1824]
    for i in range(4):
        src[f"g{i}"] = wi[:, g0 + 512 * i:g0 + 512 * (i + 1)]

    def halves(n, a):
        for i in range(2):
            src[f"{n}{i}"] = a[:, 512 * i:512 * (i + 1)]

    def updown(pa, pb, pt, a, b):
        for i in range(5):
            src[f"{pa}{i}"] = a[:, 512 * i:512 * (i + 1)]
            src[f"{pb}{i}"] = b[:, 512 * i:512 * (i + 1)]
        src[pt] = np.concatenate([a[:, 2560:], b[:, 2560:]], 1)

    halves("ba", I["w_branch_a"][0])
    halves("bb", I["w_branch_b"][0])
    halves("wo", I["w_out"][0])
    up = I["w_ffn_up"][0]
    updown("ua", "ub", "ut", up[:, :FF], up[:, FF:])
    halves("dn", I["w_ffn_down"][0])
    for i, n in enumerate(("fq", "fk", "fv", "fg")):
        halves(n, fw[:, 1024 * i:1024 * (i + 1)])
    halves("fo", I["fox_w_out_2"][0])
    halves("si", I["s5_w_in_2"][0])
    halves("sg", I["s5_w_glu_2"][0])
    halves("so", I["s5_w_out_2"][0])
    for l in range(2):
        updown(f"{l}ug", f"{l}uu", f"{l}ut", I["ffn_w_gate_2"][l], I["ffn_w_up_2"][l])
        halves(f"{l}dn", I["ffn_w_down_2"][l])
    for name, nk, w in stream_plan():
        a = src[name]
        assert a.shape == (nk * P, w), (name, a.shape)
        out["w_" + name] = a.reshape(nk // 2, 2, P, w).transpose(0, 2, 1, 3).reshape(nk // 2, P, 2 * w)
    return {k: np.ascontiguousarray(v) for k, v in out.items()}


def kernel(**inputs):
    import concourse.bacc as bacc
    from concourse.bass_utils import run_bass_kernel_spmd

    arrays = arrays_of(inputs)
    nc = bacc.Bacc("TRN2", target_bir_lowering=False, num_devices=1)
    A = {k: nc.dram_tensor("in_" + k, a.shape, mybir.dt.from_np(a.dtype), kind="ExternalInput").ap() for k, a in arrays.items()}
    out = nc.dram_tensor("out_x", (S, D), F32, kind="ExternalOutput").ap()
    program(nc, A, out)
    r = run_bass_kernel_spmd(nc, [{"in_" + k: a for k, a in arrays.items()}], core_ids=[0])
    return r.results[0]["out_x"].reshape(1, S, D)
```

```python
from contextlib import ExitStack

import numpy as np

import concourse.bass as bass
from concourse import mybir

ALU = mybir.AluOpType
ACT = mybir.ActivationFunctionType
F32 = mybir.dt.float32
F32R = mybir.dt.float32r
BF16 = mybir.dt.bfloat16
I32 = mybir.dt.int32
AX = mybir.AxisListType.X

P = 128
S = 256
D = 1024
FF = 2816
NR = 6
NS = 4
LOOK = 2
NT = 5
MAGIC = 12582912.0
RSQ = 0x5F3759DF - (1 << 31)
E05 = float(np.exp(np.float32(-0.5)))


def stream_plan():
    plan = [("mq", 8, 512), ("mk", 8, 512), ("mv", 8, 512)]
    plan += [("wl", 8, 288), ("wk", 8, 512), ("wr", 8, 512), ("wv", 8, 512)]
    plan += [(f"g{i}", 8, 512) for i in range(4)]
    plan += [("bb0", 4, 512), ("bb1", 4, 512), ("ba0", 4, 512), ("ba1", 4, 512)]
    plan += [("wo0", 8, 512), ("wo1", 8, 512)]
    for i in range(5):
        plan += [(f"ua{i}", 8, 512), (f"ub{i}", 8, 512)]
    plan += [("ut", 8, 512)]
    plan += [("dn0", 22, 512), ("dn1", 22, 512)]
    plan += [(f"fq{i}", 8, 512) for i in range(2)] + [(f"fk{i}", 8, 512) for i in range(2)]
    plan += [(f"fv{i}", 8, 512) for i in range(2)] + [(f"fg{i}", 8, 512) for i in range(2)]
    plan += [("fo0", 8, 512), ("fo1", 8, 512)]
    for l in range(2):
        if l == 1:
            plan += [(f"si{i}", 8, 512) for i in range(2)]
            plan += [(f"sg{i}", 8, 512) for i in range(2)]
            plan += [(f"so{i}", 8, 512) for i in range(2)]
        for i in range(5):
            plan += [(f"{l}ug{i}", 8, 512), (f"{l}uu{i}", 8, 512)]
        plan += [(f"{l}ut", 8, 512)]
        plan += [(f"{l}dn0", 22, 512), (f"{l}dn1", 22, 512)]
    return plan


VEC_TILES = [
    ("norm1_g", 8), ("rwkv_mu", 15), ("decay_bias", 4), ("aaa_bias", 4), ("k_k", 4), ("k_a", 4), ("r_k", 4),
    ("ln_g", 4), ("ln_b", 4), ("norm2_g", 8), ("conv_w0", 22), ("conv_w1", 22), ("conv_w2", 22), ("conv_b", 22),
    ("b_f", 1), ("log_dt", 32), ("lam_re", 32), ("lam_im", 32), ("d_skip", 8), ("mix_pre", 16), ("ffn_pre", 16), ("fox_g", 2),
]
VEC_AT = {}
_n = 0
for _name, _k in VEC_TILES:
    VEC_AT[_name] = _n
    _n += _k
NVEC = _n

CON = [("ident", 128), ("bones", 128), ("lev0", 128), ("levs", 768), ("mask2", 256), ("hsel", 32), ("hspread", 512), ("iota", 128), ("invf", 8)]
CON_AT = {}
_n = 0
for _name, _k in CON:
    CON_AT[_name] = _n
    _n += _k
NCON = _n


class Queue:

    def __init__(self, sem):
        self.sem, self.n, self.items = sem, 0, []

    def __call__(self, fn, *waits, sig=True):
        self.items.append((fn, list(flat(waits)), sig))
        if sig:
            self.n += 1
        return (self.sem, self.n)

    def play(self, eng):
        seen = {}
        for fn, waits, sig in self.items:
            for s, v in waits:
                if seen.get(id(s), 0) < v:
                    eng.wait_ge(s, v)
                    seen[id(s)] = v
            ins = fn()
            if sig:
                ins.then_inc(self.sem, 1)


def flat(waits):
    for w in waits:
        if w is None:
            continue
        if isinstance(w, list):
            yield from flat(w)
        else:
            yield w


class Bank:

    def __init__(self, t):
        self.t, self.free, self.held = t, [], False


class Acts:

    def __init__(self, hi, lo):
        self.hi, self.lo, self.tok = hi, lo, {}


def program(nc, A, out):
    ctx = ExitStack()
    with ctx:
        def sem(name):
            return ctx.enter_context(nc.semaphore(name))

        def sb(name, shape, dt=F32, stack=None):
            return (stack or ctx).enter_context(nc.sbuf_tensor(name, shape, dt))

        pe, act, dve, pool = (Queue(sem("s_" + n)) for n in ("pe", "act", "dve", "pool"))
        sp_items = []
        dma_sems = {}

        def dma(dst, src, s, *waits):
            dma_sems[s] = dma_sems.get(s, 0) + 16
            sp_items.append((lambda: nc.sync.dma_start(dst, src), list(flat(waits)), s))
            return (s, dma_sems[s])

        V, G, T = nc.vector, nc.gpsimd, nc.tensor

        raw = [sb(f"raw{i}", [P, 1024]) for i in range(NR)]
        whi = [sb(f"whi{i}", [P, 1024], F32R) for i in range(NS)]
        wlo = [sb(f"wlo{i}", [P, 1024], F32R) for i in range(NS)]
        x = sb("x", [P, 2, D])
        h = sb("h", [P, 2, D])
        a_hi = sb("a_hi", [P, 8, S], F32R)
        a_lo = sb("a_lo", [P, 8, S], F32R)
        vec = sb("vec", [P, NVEC])
        con = sb("con", [P, NCON])
        maskw = sb("maskw", [P, 3 * P], mybir.dt.int16)
        maskb = maskw[:, :].bitcast(BF16).rearrange("p (a s) -> p a s", a=3)
        eps = sb("eps", [P, 4])
        st = sb("st", [P, 64])
        nt = sb("nt", [P, 4, 64])
        wps = [Bank(ctx.enter_context(nc.psum_tensor(f"wps{i}", [P, 512], F32))) for i in range(4)]
        tps = [Bank(ctx.enter_context(nc.psum_tensor(f"tps{i}", [P, 512], F32))) for i in range(4)]

        s_raw = [sem(f"s_raw{i}") for i in range(NR)]
        s_x, s_con, s_tab = [sem("s_x0"), sem("s_x1")], sem("s_con"), sem("s_tab")
        s_gain = sem("s_gain")
        s_out = sem("s_out")
        s_att, s_lora, s_wf, s_bz, s_cz = (sem(n) for n in ("s_att", "s_lora", "s_wf", "s_bz", "s_cz"))

        def vcol(name, i=0, rows=P):
            return vec[0:rows, VEC_AT[name] + i:VEC_AT[name] + i + 1]

        def vcols(name, n):
            return vec[:, VEC_AT[name]:VEC_AT[name] + n]

        def const(name, n):
            return con[:, CON_AT[name]:CON_AT[name] + n]

        ident = const("ident", P)
        bones = const("bones", P)

        q_con = dma(con[:, 0:P], A["ident"], s_con)
        q_x = [dma(x[:, j, :], A["x"][j * P:(j + 1) * P, :], s_x[j]) for j in range(2)]
        q_con = dma(vec[:, :], A["vec"], s_con)
        q_eps = [pool(lambda i=i, v=v: G.memset(eps[:, i:i + 1], v)) for i, v in enumerate((1e-6, 64e-5, 1.0, 0.0))]

        plan = stream_plan()
        slabs = []
        for name, nk, w in plan:
            if name == "sg0":
                slabs += [(f"sg{c}", kp, w) for h_ in range(2) for c in range(2) for kp in (2 * h_, 2 * h_ + 1)]
            elif name != "sg1":
                slabs += [(name, kp, w) for kp in range(nk // 2)]
        load_tok, split_tok, used_tok = {}, {}, {}
        at = {"load": 0, "split": 0, "use": 0}

        def load_next():
            n = at["load"]
            if n >= len(slabs):
                return
            at["load"] += 1
            name, kp, w = slabs[n]
            load_tok[n] = dma(raw[n % NR][:, 0:2 * w], A["w_" + name][kp], s_raw[n % NR], split_tok.get(n - NR))

        def split_next(lo_on=None):
            n = at["split"]
            if n >= len(slabs):
                return
            at["split"] += 1
            w = 2 * slabs[n][2]
            r, hi, lo = raw[n % NR][:, 0:w], whi[n % NS][:, 0:w], wlo[n % NS][:, 0:w]
            q = act(lambda: nc.scalar.activation(hi, r, ACT.Copy), load_tok[n], used_tok.get(n - NS))
            on = lo_on or dve
            eng = G if on is pool else V
            split_tok[n] = on(lambda: eng.tensor_tensor(lo, r, hi.bitcast(F32), ALU.subtract), q)
            load_next()

        for _ in range(3):
            load_next()
        q_tab = dma(con[:, P:NCON], A["con"], s_tab)
        q_tab = dma(maskw[:, :], A["mask"], s_tab)
        for _ in range(NR - 3):
            load_next()

        wpair = [0]
        pending = []
        soon = []
        background = []

        class Sides(list):
            pass

        def side(tok, j):
            return tok[j] if isinstance(tok, Sides) else tok

        def stream(name, nk, acts, after=None, banks=None):
            if banks is None:
                i = wpair[0]
                wpair[0] ^= 1
                banks = wps[2 * i:2 * i + 2]
            toks = [None, None]

            def use(n, kp, j, sub, done):
                nm, kk, w = slabs[n]
                assert (nm, kk) == (name, kp), (nm, kk, name, kp)
                hi, lo = whi[n % NS], wlo[n % NS]
                k = 2 * kp + sub
                wh, wl = hi[:, sub * w:(sub + 1) * w], lo[:, sub * w:(sub + 1) * w]
                o = banks[j].t[:, 0:w]
                xh, xl = acts.hi[:, k, j * P:(j + 1) * P], acts.lo[:, k, j * P:(j + 1) * P]
                first, last = k == 0, k == nk - 1
                dep = (split_tok[n], side(acts.tok[k], j)) + ((banks[j].free,) if first else ())
                pe(lambda: T.matmul(o, xh, wh, start=first, stop=False), *dep, sig=False)
                pe(lambda: T.matmul(o, xl, wh, start=False, stop=False), sig=False)
                t = pe(lambda: T.matmul(o, xh, wl, start=False, stop=last), sig=last or done)
                if last:
                    toks[j] = t
                return t

            def beside():
                for g in list(background):
                    if next(g, g) is g:
                        background.remove(g)

            nkp = nk // 2
            whole_kp = nkp if after is None else nkp - NS
            for kp in range(whole_kp):
                n = at["use"]
                while at["split"] <= min(n + LOOK, len(slabs) - 1):
                    split_next()
                for sub in range(2):
                    for j in range(2):
                        t = use(n, kp, j, sub, sub == 1 and j == 1)
                used_tok[n] = t
                at["use"] += 1
                while soon:
                    soon.pop(0)()
                if kp == min(1, nkp - 1):
                    while pending:
                        pending.pop(0)()
                beside()
                yield
            if after is not None:
                assert not pending
                n0 = at["use"]
                while at["split"] < n0 + NS:
                    split_next()
                for j in range(2):
                    for m in range(NS):
                        for sub in range(2):
                            t = use(n0 + m, whole_kp + m, j, sub, j == 1 and sub == 1)
                        if j == 1:
                            used_tok[n0 + m] = t
                            at["use"] += 1
                            if m < 2:
                                split_next(pool)
                        if (j, m) in after:
                            after[j, m](banks, toks)
                        if j == 1:
                            if m >= 2 and (0, NS - 1) not in after:
                                split_next()
                            beside()
                            yield
            return banks, toks

        def whole(gen):
            while True:
                try:
                    next(gen)
                except StopIteration as e:
                    return e.value

        def settle():
            while background:
                whole(background.pop(0))

        fillers = []

        def fill(n=1):
            for _ in range(n):
                while fillers:
                    try:
                        next(fillers[0])
                        break
                    except StopIteration:
                        fillers.pop(0)

        def finish():
            while fillers:
                fill()

        def bank():
            for _ in range(4):
                b = tps.pop(0)
                tps.append(b)
                if not b.held:
                    return b
            raise ValueError("no bank")

        def transpose(o, i, n, *waits, sig=False):
            return pe(lambda: T.transpose(o, i, ident[0:n, 0:n]), *waits, sig=sig)

        def rsqrt(dst, src, n, scale, add, *waits):
            m, xh, t = nt[:, 0, 0:n], nt[:, 1, 0:n], nt[:, 2, 0:n]
            y = nt[:, 3, 0:n]
            q = dve(lambda: V.tensor_scalar(m, src, scale, add, ALU.mult, ALU.add), *waits)
            q2 = dve(lambda: V.tensor_scalar(xh, src, scale * 0.5, add * 0.5, ALU.mult, ALU.add), *waits)
            q = dve(lambda: V.tensor_scalar(t.bitcast(I32), m.bitcast(I32), 1, None, ALU.logical_shift_right), q)
            q = dve(lambda: V.tensor_scalar(y.bitcast(I32), t.bitcast(I32), -1.0, float(RSQ), ALU.mult, ALU.add), q)
            for s in range(3):
                o = dst if s == 2 else y
                q = dve(lambda: V.tensor_tensor(t, y, y, ALU.mult), q)
                q = dve(lambda: V.tensor_tensor(t, t, xh, ALU.mult), q, q2)
                q = dve(lambda o=o: V.scalar_tensor_tensor(o, t, 1.5, y, ALU.subtract, ALU.mult), q)
            return q

        class Halves(list):
            pass

        def part(ready, kb):
            return ready[kb // 2] if isinstance(ready, Halves) else ready

        def to_acts(src, ready, acts, nk, gain=None, k0=0, wait_free=(), kbs=None):
            for kb in kbs or range(nk // 2):
                b = bank()
                for sub in range(2):
                    for j in range(2):
                        o = b.t[:, sub * S + j * P:sub * S + (j + 1) * P]
                        i = src[:, j, (2 * kb + sub) * P:(2 * kb + sub + 1) * P]
                        q = transpose(o, i, P, part(ready[j], kb), b.free, q_con, sig=(sub == 1 and j == 1))
                k = k0 + 2 * kb
                if gain is None:
                    o3 = b.t[:, :].rearrange("p (k s) -> p k s", k=2)
                    hi, lo = acts.hi[:, k:k + 2, :], acts.lo[:, k:k + 2, :]
                    qh = act(lambda hi=hi, o3=o3: nc.scalar.activation(hi, o3, ACT.Copy), q, *wait_free)
                    ql = dve(lambda hi=hi, lo=lo, o3=o3: V.tensor_tensor(lo, o3, hi.bitcast(F32), ALU.subtract), qh)
                    acts.tok[k] = acts.tok[k + 1] = ql
                else:
                    for sub in range(2):
                        o = b.t[:, sub * S:(sub + 1) * S]
                        hi, lo, g = acts.hi[:, k + sub, :], acts.lo[:, k + sub, :], gain(k + sub)
                        qh = act(lambda hi=hi, o=o, g=g: nc.scalar.activation(hi, o, ACT.Copy, scale=g), q, *wait_free)
                        acts.tok[k + sub] = qh
                    for sub in range(2):
                        o = b.t[:, sub * S:(sub + 1) * S]
                        hi, lo, g = acts.hi[:, k + sub, :], acts.lo[:, k + sub, :], gain(k + sub)
                        ql = dve(lambda hi=hi, lo=lo, o=o, g=g: V.scalar_tensor_tensor(
                            lo, o, g, hi.bitcast(F32), ALU.mult, ALU.subtract), qh)
                        acts.tok[k + sub] = ql
                b.free = [ql]

        main = Acts(a_hi[:, :, :], a_lo[:, :, :])

        norm = {}

        def turnover(ready, gname, g0, early=()):
            kbs = [kb for kb in range(4) if kb not in early]

            def do(j):
                for kb in kbs:
                    b = bank()
                    for sub in range(2):
                        k = 2 * kb + sub
                        q = transpose(b.t[:, sub * P:(sub + 1) * P], x[:, j, k * P:(k + 1) * P], P, part(ready[j], kb), b.free,
                                      q_con, sig=(sub == 1))
                    parts_ = [(b.t[:, sub * P:(sub + 1) * P], main.hi[:, 2 * kb + sub, j * P:(j + 1) * P],
                               main.lo[:, 2 * kb + sub, j * P:(j + 1) * P], vcol(gname, g0 + 2 * kb + sub)) for sub in range(2)]
                    for o, hi, lo, g in parts_:
                        qh = act(lambda o=o, hi=hi, g=g: nc.scalar.activation(hi, o, ACT.Copy, scale=g), q)
                    for sub, (o, hi, lo, g) in enumerate(parts_):
                        ql = dve(lambda o=o, hi=hi, lo=lo, g=g: V.scalar_tensor_tensor(
                            lo, o, g, hi.bitcast(F32), ALU.mult, ALU.subtract), qh)
                        k = 2 * kb + sub
                        if j == 0:
                            main.tok[k] = Sides([ql, None])
                        else:
                            main.tok[k][1] = ql
                    b.free = [ql]

            def second():
                do(1)
                start_root(ready)

            norm["r"], norm["tok"] = [st[:, 2:3], st[:, 3:4]], None
            return lambda: do(0), second

        def prenorm(ready, gname, g0, early=()):
            to_acts(x, ready, main, 8, gain=lambda k: vcol(gname, g0 + k), kbs=[kb for kb in range(4) if kb not in early])
            start_root(ready)

        def start_root(ready):
            busy = norm.get("h")

            def root():
                qs = []
                for j in range(2):
                    qs.append(act(lambda j=j: nc.scalar.activation(h[:, j, :], x[:, j, :], ACT.Square,
                                                                   accum_out=st[:, j:j + 1]), ready[j], busy))
                    yield
                norm["tok"] = rsqrt(st[:, 2:4], st[:, 0:2], 2, 1.0 / D, 1e-6, qs)

            norm["r"], norm["tok"] = [st[:, 2:3], st[:, 3:4]], None
            background.insert(0, root())

        def normed(o, i, func, j, *waits):
            assert norm["tok"] is not None
            return act(lambda: nc.scalar.activation(o, i, func, scale=norm["r"][j]), norm["tok"], *waits)

        prenorm(q_x, "norm1_g", 0)

        s1 = ExitStack()
        arena = sb("arena", [P, 101 * 256], F32, s1)

        def view(kb, n):
            at0 = int(round(kb * 256))
            return arena[:, at0:at0 + n]

        yb = view(0, 1024).rearrange("p (j c) -> p j c", j=2)
        gates = view(4, 4096).rearrange("p (j c) -> p j c", j=2)
        mq = view(4, 1024).rearrange("p (j c) -> p j c", j=2)
        mk = view(8, 1024).rearrange("p (j c) -> p j c", j=2)
        mqT = view(12, 1024).rearrange("p (t s) -> p t s", t=4)
        mkT = view(16, 1024).rearrange("p (t s) -> p t s", t=4)
        mv = view(20, 1024).rearrange("p (j c) -> p j c", j=2)
        prob = [view(24, 384), view(25.5, 384), view(34, 384)]
        probT = [view(27, 384), view(28.5, 384)]
        sq = view(30, 512)
        rt = view(32, 512).rearrange("p (a n) -> p a n", a=4)
        qkg = sb("qkg", [P, 4, 64], F32, s1)
        posi = sb("posi", [P, 2], I32, s1)
        rope = sb("rope", [P, 6, 2, 8], F32, s1)
        q_m = [dma(qkg[:, :, :], A["qkg"], s_att), dma(posi[:, :], A["posi"], s_att)][-1]

        posf, ang, trn = rope[:, 0, :, 0], rope[:, 1, :, :], rope[:, 2, :, :]
        rsin, rcos, tmp8 = rope[:, 3, :, :], rope[:, 4, :, :], rope[:, 5, :, :]
        invf = const("invf", 8)
        tabs = {}

        def rope_tables():
            q = dve(lambda: V.tensor_copy(posf, posi[:, :]), q_m)
            qa = [dve(lambda j=j: V.tensor_scalar(ang[:, j, :], invf, posf[:, j:j + 1], None, ALU.mult), q, q_tab) for j in range(2)]
            q = dve(lambda: V.tensor_scalar(trn, ang, float(1 / (2 * np.pi)), MAGIC, ALU.mult, ALU.add), qa)
            yield
            q = dve(lambda: V.tensor_scalar(trn, trn, MAGIC, None, ALU.subtract), q)
            q2 = dve(lambda: V.scalar_tensor_tensor(ang, trn, -6.28125, ang, ALU.mult, ALU.add), q)
            q = dve(lambda: V.scalar_tensor_tensor(ang, trn, -float(2 * np.pi - 6.28125), ang, ALU.mult, ALU.add), q2)
            yield
            q = dve(lambda: V.tensor_scalar(ang, ang, 3.1415925, -3.1415925, ALU.min, ALU.max), q)
            q2 = dve(lambda: V.scalar_tensor_tensor(tmp8, ang, -1.0, ang, ALU.mult, ALU.max), q)
            q2 = dve(lambda: V.tensor_scalar(tmp8, tmp8, -1.0, float(np.pi / 2), ALU.mult, ALU.add), q2)
            yield
            q = act(lambda: nc.scalar.activation(rsin, ang, ACT.Sin), q)
            tabs["rope"] = act(lambda: nc.scalar.activation(rcos, tmp8, ACT.Sin), q2)
            tabs["gain"] = dve(lambda: V.tensor_scalar(qkg[:, 0:3:2, :], qkg[:, 0:3:2, :], 0.125, None, ALU.mult), q_m)

        background.append(rope_tables())

        def heads(ap, n):
            return ap.rearrange("p (h d) -> p h d", h=n)

        def wide(ap, n):
            return ap.unsqueeze(2).to_broadcast([ap.shape[0], ap.shape[1], n])

        def take_heads(banks, toks, dst, c0, ss, scratch):
            out_t = []
            for j in range(2):
                b = banks[j]
                q1 = normed(dst[:, j, c0:c0 + 512], b.t[:, :], ACT.Copy, j, toks[j])
                b.free = [q1]
                q2 = act(lambda j=j: nc.scalar.activation(scratch, dst[:, j, c0:c0 + 512], ACT.Square), q1, out_t)
                out_t = [dve(lambda j=j: V.tensor_reduce(ss[j], heads(scratch, 8), AX, ALU.add), q2)]
            return out_t

        def norm_heads(dst, j, n, r, g, *waits):
            d = heads(dst[:, j, :], n)
            q1 = dve(lambda: V.tensor_tensor(d, d, wide(r, 64), ALU.mult), *waits)
            if g is None:
                return q1
            gb = g.unsqueeze(1).to_broadcast([P, n, 64])
            return dve(lambda: V.tensor_tensor(d, d, gb, ALU.mult), q1)

        def to_heads_T(src, dst, nt_, ready, gain=None, wait=None, kbs=None):
            toks = []
            for kb in kbs or range(nt_ // 2):
                b = bank()
                for sub in range(2):
                    for j in range(2):
                        t = transpose(b.t[:, sub * S + j * P:sub * S + (j + 1) * P],
                                      src[:, j, (2 * kb + sub) * P:(2 * kb + sub + 1) * P], P,
                                      part(ready[j], kb), b.free, q_con, sig=(sub == 1 and j == 1))
                o3 = b.t[:, :].rearrange("p (k s) -> p k s", k=2)
                d = dst[:, 2 * kb:2 * kb + 2, :]
                if gain is None:
                    b.free = [act(lambda d=d, o3=o3: nc.scalar.activation(d, o3, ACT.Copy), t)]
                else:
                    b.free = [act(lambda d=d, o3=o3: nc.scalar.activation(d, o3, ACT.Copy, scale=gain), t, wait)]
                toks.append(b.free[0])
            return toks

        class Head:
            pass

        def scores(h_, qT, kT, ready, prob_, free, sm, cq=None, ck=None):
            hd = Head()
            p0, t = 64 * (h_ % 2), h_ // 2
            b = bank()
            for j in range(2):
                nk_ = P * (j + 1)
                o = b.t[:, 0:P] if j == 0 else b.t[:, P:3 * P]
                qs, ks = qT[p0:p0 + 64, t, j * P:(j + 1) * P], kT[p0:p0 + 64, t, 0:nk_]
                pe(lambda o=o, qs=qs, ks=ks: T.matmul(o, qs, ks, start=True, stop=False), ready, b.free, sig=False)
                if ck is not None:
                    l, r = ck(h_, nk_)
                    pe(lambda o=o, l=l, r=r: T.matmul(o, l, r, start=False, stop=False), sig=False)
                causal = maskb[:, 2 - j:3, :].rearrange("p a s -> p (a s)")
                q = pe(lambda o=o, causal=causal: T.matmul(o, maskb[:, 0, :], causal, start=False, stop=True), q_tab)
            mx, nb, rs = sm
            q1 = dve(lambda: V.tensor_reduce(mx[:, 0:1], b.t[:, 0:P], AX, ALU.max), q)
            q2 = dve(lambda: V.tensor_reduce(mx[:, 1:2], b.t[:, P:3 * P], AX, ALU.max), q)
            if cq is None:
                q3 = dve(lambda: V.tensor_scalar(nb, mx, -1.0, None, ALU.mult), q1, q2, free)
            else:
                q3 = dve(lambda: V.tensor_tensor(mx, mx, cq, ALU.add), q1, q2)
                q3 = dve(lambda: V.scalar_tensor_tensor(nb, mx, -1.0, cq, ALU.mult, ALU.add), q3, free)
            act(lambda: nc.scalar.activation(prob_[:, 0:P], b.t[:, 0:P], ACT.Exp, bias=nb[:, 0:1], accum_out=rs[:, 0:1]), q3, free)
            hd.exp = act(lambda: nc.scalar.activation(prob_[:, P:3 * P], b.t[:, P:3 * P], ACT.Exp, bias=nb[:, 1:2], accum_out=rs[:, 1:2]))
            b.free = [hd.exp]
            return hd

        def across(hd, prob_, probT_, free):
            b = bank()
            for i in range(3):
                q = transpose(b.t[:, i * P:(i + 1) * P], prob_[:, i * P:(i + 1) * P], P, hd.exp, b.free, sig=(i == 2))
            hd.trans = q
            hd.probs = dve(lambda: V.tensor_copy(probT_, b.t[:, 0:3 * P]), q, free)
            b.free = [hd.probs]

        def values(h_, hd, probT_, vt, vready, ob, obfree):
            c = (h_ % 4) * 64
            vv = [vt[:, kb, h_ * 64:(h_ + 1) * 64] for kb in range(2)]
            pe(lambda: T.matmul(ob.t[:, c:c + 64], probT_[:, 0:P], vv[0], start=True, stop=True), hd.probs, vready, obfree, sig=False)
            pe(lambda: T.matmul(ob.t[:, S + c:S + c + 64], probT_[:, P:2 * P], vv[0], start=True, stop=False), sig=False)
            hd.done = pe(lambda: T.matmul(ob.t[:, S + c:S + c + 64], probT_[:, 2 * P:3 * P], vv[1], start=False, stop=True))

        def attention(nh, qT, kT, vt, qkready, vready, dst, prob_, probT_, mx, nb, rs, step, cq=None, ck=None, toks=None):
            hds = []
            ob = None
            toks = [] if toks is None else toks
            for h_ in range(nh + 3):
                if h_ < nh:
                    i = h_ % 3
                    free = [hds[h_ - 3].trans] if h_ >= 3 else []
                    sm = (mx[:, i, :], nb[:, i, :], rs[:, :, h_])
                    hds.append(scores(h_, qT, kT, qkready, prob_[i], free, sm, cq and cq(h_), ck))
                g = h_ - 3
                if g >= 0:
                    if g % 4 == 0:
                        ob = bank()
                        ob.held = True
                        obfree = ob.free
                    values(g, hds[g], probT_[g % 2], vt, vready, ob, obfree)
                    if g % 4 == 3:
                        r4 = rs[:, :, g - 3:g + 1]
                        q1 = dve(lambda r4=r4: V.reciprocal(r4, r4), hds[g].exp)
                        o4 = ob.t[:, :].rearrange("p (j h d) -> p j h d", j=2, h=4)
                        d4 = dst[:, :, (g - 3) * 64:(g + 1) * 64].rearrange("p j (h d) -> p j h d", h=4)
                        for j in range(2):
                            q2 = dve(lambda j=j, r4=r4, o4=o4, d4=d4: V.tensor_tensor(
                                d4[:, j], o4[:, j], wide(r4[:, j, :], 64), ALU.mult), hds[g].done, q1)
                        ob.free = [q2]
                        ob.held = False
                        toks.append(q2)
                step()
                if 2 <= h_ <= nh + 1:
                    g = h_ - 2
                    across(hds[g], prob_[g % 3], probT_[g % 2], [hds[g - 2].done] if g >= 2 else [])
                step()
            return toks

        mss = st[:, 8:40].rearrange("p (i j h) -> p i j h", i=2, j=2)
        mrs = sb("mrs", [P, 32], F32, s1)
        rr = mrs[:, :].rearrange("p (i j h) -> p i j h", i=2, j=2)
        tk = []
        for i, (nm, dst) in enumerate((("mq", mq), ("mk", mk))):
            banks, toks = whole(stream(nm, 8, main))
            tk += take_heads(banks, toks, dst, 0, [mss[:, i, 0, :], mss[:, i, 1, :]], sq)
        q_rot = {}

        def rotate():
            q_r = rsqrt(mrs[:, :], st[:, 8:40], 32, 1.0 / 64, 1e-6, tk)
            yield
            for i, dst in enumerate((mq, mk)):
                for j in range(2):
                    q = norm_heads(dst, j, 8, rr[:, i, j, :], qkg[:, i, :], q_r, tabs["gain"])
                    hv = heads(dst[:, j, :], 8)
                    x1, x2 = hv[:, :, 0:8], hv[:, :, 8:16]
                    cb = rcos[:, j, :].unsqueeze(1).to_broadcast([P, 8, 8])
                    sb_ = rsin[:, j, :].unsqueeze(1).to_broadcast([P, 8, 8])
                    r4 = [rt[:, a, 64 * j:64 * j + 64].rearrange("p (h d) -> p h d", h=8) for a in range(4)]
                    prev = q_rot.get((0, j))
                    for a, (u, c) in enumerate(((x1, cb), (x2, sb_), (x2, cb), (x1, sb_))):
                        qm = pool(lambda a=a, u=u, c=c, r4=r4: G.tensor_tensor(r4[a], u, c, ALU.mult), q, tabs["rope"], prev)
                    pool(lambda x1=x1, r4=r4: G.tensor_tensor(x1, r4[0], r4[1], ALU.subtract), qm)
                    q_rot[i, j] = pool(lambda x2=x2, r4=r4: G.tensor_tensor(x2, r4[2], r4[3], ALU.add), qm)
                    yield

        background.append(rotate())
        banks, toks = whole(stream("mv", 8, main))
        q_mv = []
        for j in range(2):
            q_mv.append(normed(mv[:, j, :], banks[j].t[:, :], ACT.Copy, j, toks[j]))
            banks[j].free = [q_mv[-1]]
        settle()

        zr, zk, zv = (view(52 + 4 * i, 1024).rearrange("p (t s) -> p t s", t=4) for i in range(3))
        lor = view(64, 768).rearrange("p (t s) -> p t s", t=3)
        zt = view(67, 1024).rearrange("p (j c) -> p j c", j=2)
        zb = [view(71, 514).rearrange("p (k s) -> p k s", k=2), view(73.25, 514).rearrange("p (k s) -> p k s", k=2)]
        q_zb = [pool(lambda i=i: G.memset(zb[i][:, :, 0:1], 0.0)) for i in range(2)]
        z_tok = {}
        zb_free = [[], []]
        zt_free = [[]]

        def evacuate(banks, toks, w):
            qz = []
            for j in range(2):
                qz.append(normed(zt[:, j, 0:w], banks[j].t[:, 0:w], ACT.Copy, j, toks[j], zt_free[0]))
                banks[j].free = [qz[-1]]
            return qz

        def take_z(nm, qz, dst, w, mu0):
            tiles = [(i, min(P, w - i * P)) for i in range((w + P - 1) // P)]
            out_t = []
            for kb in range(0, len(tiles), 2):
                grp = tiles[kb:kb + 2]
                b = bank()
                for sub, (i, rows) in enumerate(grp):
                    for j in range(2):
                        q = transpose(b.t[0:rows, sub * S + j * P:sub * S + (j + 1) * P], zt[:, j, i * P:i * P + rows], P,
                                      qz, b.free, q_con, sig=(j == 1))
                ib = (kb // 2) % 2
                z_ = zb[ib]
                n, rows = len(grp), grp[-1][1]
                o3 = b.t[0:rows, 0:n * S].rearrange("p (k s) -> p k s", k=n)
                q = act(lambda z_=z_, o3=o3, n=n, rows=rows: nc.scalar.activation(z_[0:rows, 0:n, 1:S + 1], o3, ACT.Copy), q, zb_free[ib], q_zb)
                b.free = [q]
                d = dst[0:rows, kb:kb + n, :]
                q1 = dve(lambda z_=z_, d=d, n=n, rows=rows: V.tensor_tensor(d, z_[0:rows, 0:n, 0:S], z_[0:rows, 0:n, 1:S + 1], ALU.subtract), q)
                zb_free[ib] = []
                for sub in range(n):
                    mu = vcol("rwkv_mu", mu0 + kb + sub, rows)
                    q2 = dve(lambda z_=z_, d=d, sub=sub, mu=mu, rows=rows: V.scalar_tensor_tensor(
                        d[:, sub, :], d[:, sub, :], mu, z_[0:rows, sub, 1:S + 1], ALU.mult, ALU.add), q1, q_con)
                    zb_free[ib].append(q2)
                    out_t.append(q2)
                yield
            zt_free[0] = [q]
            z_tok[nm] = out_t

        def v48(kb, n=1024):
            return view(kb, n).rearrange("p (t s) -> p t s", t=4)

        AR = view(20, 2048).rearrange("p (t c a s) -> p t c a s", t=4, c=2, a=2)
        btl, ktl = (view(kb, 1024).rearrange("p (t c s) -> p t c s", t=4, c=2) for kb in (28, 32))
        Vt = view(36, 1024).rearrange("p (c n) -> p c n", c=2)
        Bt, Kt = view(40, 512), view(42, 512)
        bon, gg = v48(44), v48(48)
        cs = view(76, 1032).rearrange("p (n s) -> p n s", n=8)
        Wp = view(80.25, 1032).rearrange("p (n s) -> p n s", n=8)
        Wn = view(84.5, 1024).rearrange("p (n s) -> p n s", n=8)
        av, kk, tm = v48(88.5), v48(92.5), v48(96.5)
        wlo_sb = view(36, 1024)
        wg2 = view(40, 512)[0:32, :]
        r8 = sb("r8", [8, S], F32, s1)
        fac = sb("fac", [P, 2, 4], F32, s1)
        q_wl = dma(wlo_sb, A["wlora"], s_lora)
        q_wl = dma(wg2, A["wg2"], s_lora)
        wda, wgu = wlo_sb[:, 0:512], wlo_sb[:, 512:1024]

        def head_sums(src, ready):
            b = bank()
            for t in range(4):
                l, i = const("hsel", 32)[:, 8 * t:8 * t + 8], src[:, t, :]
                q = pe(lambda l=l, i=i, t=t: T.matmul(b.t[0:8, 0:S], l, i, start=(t == 0), stop=(t == 3)), ready, b.free, q_tab)
            return b, q

        def head_spread(ready):
            res = []
            for kb in range(2):
                b = bank()
                for sub in range(2):
                    o, l = b.t[:, sub * S:(sub + 1) * S], const("hspread", 512)[0:8, (2 * kb + sub) * P:(2 * kb + sub + 1) * P]
                    q = pe(lambda o=o, l=l: T.matmul(o, l, r8[:, :], start=True, stop=True), ready, b.free, q_tab)
                res.append((b, q))
            return res

        def per_head_sums(src, ready):
            res = []
            for kb in range(2):
                b = bank()
                for sub in range(2):
                    o, i = b.t[:, sub * S:(sub + 1) * S], src[:, 2 * kb + sub, :]
                    q = pe(lambda o=o, i=i: T.matmul(o, bones, i, start=True, stop=True), ready, b.free, q_tab)
                res.append((b, q))
            return res

        pre = {}
        q_dec, q_a, q_g, q_bon, q_vt = [], [], [], [], []

        def decay_prep():
            qt = z_tok["wl"]
            q_th = act(lambda: nc.scalar.activation(lor[0:64, 0, :], lor[0:64, 0, :], ACT.Tanh), qt)
            q_sg = act(lambda: nc.scalar.activation(lor[:, 1, :], lor[:, 1, :], ACT.Sigmoid), qt)
            q_sg = act(lambda: nc.scalar.activation(lor[0:32, 2, :], lor[0:32, 2, :], ACT.Sigmoid), qt)
            for kb in range(2):
                bs, qp = [bank(), bank(), bank()], [None] * 3
                for sub in range(2):
                    t = 2 * kb + sub
                    for what in range(2):
                        r = slice(64 * what, 64 * what + 64)
                        o, w, z_ = bs[what].t[:, sub * S:(sub + 1) * S], wda[r, t * P:(t + 1) * P], lor[r, 0, :]
                        qp[what] = pe(lambda o=o, w=w, z_=z_: T.matmul(o, w, z_, start=True, stop=True), q_th, qt, q_wl, bs[what].free)
                for sub in range(2):
                    t = 2 * kb + sub
                    o, w, w2 = bs[2].t[:, sub * S:(sub + 1) * S], wgu[:, t * P:(t + 1) * P], wg2[:, t * P:(t + 1) * P]
                    pe(lambda o=o, w=w: T.matmul(o, w, lor[:, 1, :], start=True, stop=False), q_sg, q_wl, bs[2].free, sig=False)
                    qp[2] = pe(lambda o=o, w2=w2: T.matmul(o, w2, lor[0:32, 2, :], start=False, stop=True))
                for what in range(3):
                    for sub in range(2):
                        t = 2 * kb + sub
                        o = bs[what].t[:, sub * S:(sub + 1) * S]
                        if what == 0:
                            f = act(lambda t=t, o=o: nc.scalar.activation(tm[:, t, :], o, ACT.Sigmoid, bias=vcol("decay_bias", t)), qp[0])
                            q_dec.append(f)
                        elif what == 1:
                            f = act(lambda t=t, o=o: nc.scalar.activation(av[:, t, :], o, ACT.Sigmoid, bias=vcol("aaa_bias", t)), qp[1])
                            q_a.append(f)
                        else:
                            f = act(lambda t=t, o=o: nc.scalar.activation(gg[:, t, :], o, ACT.Copy), qp[2])
                            q_g.append(f)
                    bs[what].free = [f]
            yield
            q0 = dve(lambda: V.memset(cs[:, :, 0:1], 0.0), z_tok["wl"])
            qs = []
            one = eps[:, 2:3].to_broadcast([P, P])
            for t in range(4):
                for c in range(2):
                    qs.append(dve(lambda t=t, c=c: V.tensor_tensor_scan(
                        cs[:, 2 * t + c, 1:P + 1], one, tm[:, t, c * P:(c + 1) * P], 0.0, ALU.mult, ALU.add), q_dec, q_eps))
            yield
            q = dve(lambda: V.tensor_tensor(Wp[:, :, :], cs[:, :, :], cs[:, :, 64:65].to_broadcast([P, 8, P + 1]), ALU.subtract), qs, q0)
            q_wn = act(lambda: nc.scalar.activation(Wn[:, :, :], Wp[:, :, 1:P + 1], ACT.Exp, scale=E05), q)
            q_wp = act(lambda: nc.scalar.activation(Wp[:, :, :], Wp[:, :, :], ACT.Exp, scale=-E05), q, q_wn)
            pre["cs"], pre["wn"], pre["wp"] = qs, q_wn, q_wp
            q = dve(lambda: V.reciprocal(fac[:, 0, :], Wp[:, 1:8:2, 0]), q_wp)
            pre["fac"] = dve(lambda: V.tensor_tensor(fac[:, 1, :], fac[:, 0, :], Wp[:, 0:8:2, P], ALU.mult), q)
            yield

        def key_prep():
            q_sq = [act(lambda t=t: nc.scalar.activation(tm[:, t, :], zk[:, t, :], ACT.Square, scale=vcol("k_k", t)), z_tok["wk"], pre["cs"]) for t in range(4)]
            q_k = [pool(lambda t=t: G.tensor_scalar(kk[:, t, :], zk[:, t, :], vcol("k_k", t), None, ALU.mult), z_tok["wk"]) for t in range(4)]
            yield
            b, q = head_sums(tm, q_sq)
            f = act(lambda: nc.scalar.activation(r8[:, :], b.t[0:8, 0:S], ACT.Sqrt), q)
            b.free = [f]
            f = dve(lambda: V.tensor_scalar(r8[:, :], r8[:, :], 1e-12, None, ALU.max), f)
            f = dve(lambda: V.reciprocal(r8[:, :], r8[:, :]), f)
            q1 = [pool(lambda t=t: G.tensor_scalar(tm[:, t, :], av[:, t, :], 1.0, vcol("k_a", t), ALU.subtract, ALU.mult), q_a, q) for t in range(4)]
            yield
            q_kk = []
            for kb, (b2, qb) in enumerate(head_spread(f)):
                o3 = b2.t[:, :].rearrange("p (k s) -> p k s", k=2)
                k2 = kk[:, 2 * kb:2 * kb + 2, :]
                q_kk.append(dve(lambda k2=k2, o3=o3: V.tensor_tensor(k2, k2, o3, ALU.mult), qb, q_k))
                b2.free = [q_kk[-1]]
            pre["kk"] = q_kk
            yield
            pre["k2"] = dve(lambda: V.scalar_tensor_tensor(zk, tm, 1.0, zk, ALU.add, ALU.mult), q1, q_k)
            pre["ka"] = pool(lambda: G.tensor_tensor(av, kk, av, ALU.mult), q_kk, q1)
            yield

        def bonus_prep():
            q1 = [dve(lambda t=t: V.scalar_tensor_tensor(tm[:, t, :], zr[:, t, :], vcol("r_k", t), zk[:, t, :], ALU.mult, ALU.mult),
                      pre["k2"], z_tok["wr"]) for t in range(4)]
            for c in range(2):
                q_vt.append(tokens_on_partitions(lambda t, c=c: zv[:, t, c * P:(c + 1) * P], Vt[:, c, :], [z_tok["wv"], q_g]))
            yield
            for kb, (b, qb) in enumerate(per_head_sums(tm, q1)):
                o3 = b.t[:, :].rearrange("p (k s) -> p k s", k=2)
                f = dve(lambda o3=o3, kb=kb: V.tensor_tensor(bon[:, 2 * kb:2 * kb + 2, :], o3, zv[:, 2 * kb:2 * kb + 2, :], ALU.mult), qb, z_tok["wv"])
                b.free = [f]
                q_bon.append(f)
            yield

        def tokens_on_partitions(src, dst, ready):
            b = bank()
            for t in range(4):
                q = transpose(b.t[:, t * P:(t + 1) * P], src(t), P, ready, b.free, sig=(t == 3))
            b.free = [act(lambda: nc.scalar.activation(dst, b.t[:, :], ACT.Copy), q)]
            return b.free[0]

        def rwkv_inputs():
            jobs = []

            def work():
                while jobs and next(jobs[0], jobs) is jobs:
                    jobs.pop(0)

            for nm, dst, w, m0, then in (("wl", lor, 288, 12, decay_prep), ("wk", zk, 512, 4, key_prep),
                                         ("wr", zr, 512, 0, None), ("wv", zv, 512, 8, bonus_prep)):
                g = stream(nm, 8, main)
                for _ in range(4):
                    next(g)
                    work()
                    yield "slab"
                banks, toks = whole(g)
                while last_z and last_z[0] not in z_tok:
                    work()
                    yield "work"
                last_z[:] = [nm]
                jobs.append(take_z(nm, evacuate(banks, toks, w), dst, w, m0))
                if then is not None:
                    jobs.append(then())
            while jobs:
                work()
                yield "work"

        last_z = []
        projections = rwkv_inputs()
        fillers.append(projections)
        fill(2)
        qk_t = to_heads_T(mq, mqT, 4, [q_rot[0, j] for j in range(2)])
        fill(2)
        qk_t += to_heads_T(mk, mkT, 4, [q_rot[1, j] for j in range(2)])
        mmx = sb("mmx", [P, 3, 2], F32, s1)
        mnb = sb("mnb", [P, 3, 2], F32, s1)
        msum = sb("msum", [P, 2, 8], F32, s1)
        q_yb = attention(8, mqT, mkT, mv, qk_t, q_mv, yb, prob, probT, mmx, mnb, msum, fill)

        q_gates = {}

        def gate_groups():
            for g in range(4):
                banks, toks = yield from stream(f"g{g}", 8, main)
                for j in range(2):
                    o = gates[:, j, g * 512:(g + 1) * 512]
                    q = normed(o, banks[j].t[:, :], ACT.Sigmoid, j, toks[j])
                    banks[j].free = [q]
                    q_gates[g, j] = q
                q_gates["pe"] = toks[1]
                yield

        gate_slabs = gate_groups()
        fillers.clear()
        for what in projections:
            if what == "work":
                next(gate_slabs)
        fillers.append(gate_slabs)

        wp1 = Wp[:, :, 1:P + 1].rearrange("p (t c) s -> p t c s", t=4)
        wp0 = Wp[:, :, 0:P].rearrange("p (t c) s -> p t c s", t=4)
        wn = Wn[:, :, :].rearrange("p (t c) s -> p t c s", t=4)

        def tcs(ap):
            return ap.rearrange("p t (c s) -> p t c s", c=2)

        q_ar, q_bk = [], []
        q_k2, q_fac = pre["k2"], pre["fac"]
        for t in range(4):
            q_bk.append(dve(lambda t=t: V.tensor_tensor(btl[:, t], tcs(av)[:, t], wn[:, t], ALU.mult), pre["ka"], pre["wn"], q_yb))
            q_bk.append(pool(lambda t=t: G.tensor_tensor(ktl[:, t], tcs(zk)[:, t], wn[:, t], ALU.mult), q_k2, pre["wn"], q_yb))
            q_ar.append(dve(lambda t=t: V.scalar_tensor_tensor(AR[:, t, :, 0, :], tcs(kk)[:, t], -1.0, wp0[:, t], ALU.mult, ALU.mult), pre["kk"], pre["wp"], q_yb))
            q_ar.append(dve(lambda t=t: V.tensor_tensor(AR[:, t, :, 1, :], tcs(zr)[:, t], wp1[:, t], ALU.mult), z_tok["wr"], pre["wp"], q_yb))
        fill(1)
        q_bt = tokens_on_partitions(lambda t: btl[:, t, 0, :], Bt, q_bk)
        q_kt = tokens_on_partitions(lambda t: ktl[:, t, 0, :], Kt, q_bk)
        early_done = [q_ar, q_bk, q_fac, q_bon, q_vt, q_k2, q_g]

        Sm = view(52, 4096).rearrange("p (h a s) -> p h a s", h=8, a=4)
        Ti = view(68, 1024).rearrange("p (h s) -> p h s", h=8)
        TT = view(72, 1024).rearrange("p (h s) -> p h s", h=8)
        M1 = view(76, 1024).rearrange("p (h s) -> p h s", h=8)
        Ao = [view(80, 512).rearrange("p (h s) -> p h s", h=4), view(82, 512).rearrange("p (h s) -> p h s", h=4)]
        RU, U = view(84, 512), view(86, 512)
        S0 = view(88, 256).rearrange("p (t v) -> p t v", t=4)
        Y = v48(89)
        Y2, Y3 = v48(93), v48(97)
        mask2 = const("mask2", 256)
        lev0 = const("lev0", P)
        levs = const("levs", 768).rearrange("p (l s) -> p l s", l=6)

        def both(ap):
            return ap.unsqueeze(1).to_broadcast([P, 4, P])

        q_y = []
        q_s0 = None
        prevU = []
        for c in range(2):
            q_sm = []
            for t in range(4):
                bs = [bank(), bank()]
                qp = {}
                for n_, keys in enumerate((btl, ktl)):
                    for u in range(2):
                        p0 = 64 * u
                        o, l = bs[u].t[:, 256 * n_:256 * n_ + 256], keys[p0:p0 + 64, t, c, :]
                        ar = AR[p0:p0 + 64, t, c, :, :].rearrange("p a s -> p (a s)")
                        qp[u] = pe(lambda o=o, l=l, ar=ar: T.matmul(o, l, ar, start=True, stop=True), q_ar, q_bk, bs[u].free)
                for u in range(2):
                    d = Sm[:, 2 * t + u].rearrange("p (w a) s -> p w (a s)", w=2)
                    o3 = bs[u].t[:, :].rearrange("p (w n) -> p w n", w=2)
                    q_sm.append(dve(lambda d=d, o3=o3: V.tensor_tensor(d, o3, mask2.unsqueeze(1).to_broadcast([P, 2, 256]), ALU.mult),
                                    qp[u], early_done, prevU))
                    bs[u].free = [q_sm[-1]]
            q_T, q_TT = [None, None], [None, None]
            q_ao = [[], []]
            for g in range(2):
                hs = slice(4 * g, 4 * g + 4)
                on, eng = ((dve, V), (pool, G))[g]
                q = on(lambda hs=hs, eng=eng: eng.tensor_tensor(TT[:, hs, :], Sm[:, hs, 0, :], both(lev0), ALU.mult), q_sm[4 * g:4 * g + 4], prevU)
                q_TT[g] = on(lambda hs=hs, eng=eng: eng.tensor_tensor(TT[:, hs, :], TT[:, hs, :], both(ident), ALU.add), q)
            fill(2)
            for g in range(2):
                b = bank()
                for i in range(4):
                    q = transpose(b.t[:, i * P:(i + 1) * P], TT[:, 4 * g + i, :], P, q_TT[g], b.free, sig=(i == 3))
                o3 = b.t[:, :].rearrange("p (h s) -> p h s", h=4)
                q_T[g] = act(lambda g=g, o3=o3: nc.scalar.activation(Ti[:, 4 * g:4 * g + 4, :], o3, ACT.Copy), q)
                b.free = [q_T[g]]
            q_m1pe = [None, None]
            for l in range(6):
                q_m1 = [None, None]
                for g in range(2):
                    hs = slice(4 * g, 4 * g + 4)
                    q = pool(lambda g=g, hs=hs, l=l: G.tensor_tensor(Ao[g], Sm[:, hs, 0, :], both(levs[:, l, :]), ALU.mult),
                             q_sm[4 * g:4 * g + 4], q_m1pe[g], early_done)
                    b = bank()
                    for i in range(4):
                        q2 = pe(lambda b=b, g=g, i=i: T.matmul(b.t[:, i * P:(i + 1) * P], Ao[g][:, i, :], Ti[:, 4 * g + i, :],
                                                               start=True, stop=True), q, q_T[g], b.free, sig=(i == 3))
                    q_m1pe[g] = q2
                    o3 = b.t[:, :].rearrange("p (h s) -> p h s", h=4)
                    q_m1[g] = act(lambda hs=hs, o3=o3: nc.scalar.activation(M1[:, hs, :], o3, ACT.Copy), q2)
                    b.free = [q_m1[g]]
                if l not in (1, 3):
                    fill(1)
                for g in range(2):
                    hs = slice(4 * g, 4 * g + 4)
                    if l < 5:
                        b = bank()
                        for i in range(4):
                            q2 = pe(lambda b=b, g=g, i=i: T.matmul(b.t[:, i * P:(i + 1) * P], TT[:, 4 * g + i, :], M1[:, 4 * g + i, :],
                                                                   start=True, stop=True), q_m1[g], q_TT[g], b.free, sig=(i == 3))
                        o3 = b.t[:, :].rearrange("p (h s) -> p h s", h=4)
                        q_T[g] = dve(lambda hs=hs, o3=o3: V.tensor_tensor(Ti[:, hs, :], Ti[:, hs, :], o3, ALU.add), q2)
                        b.free = [q_T[g]]
                    b = bank()
                    for i in range(4):
                        q2 = pe(lambda b=b, g=g, i=i: T.matmul(b.t[:, i * P:(i + 1) * P], M1[:, 4 * g + i, :], TT[:, 4 * g + i, :],
                                                               start=True, stop=True), q_m1[g], q_TT[g], b.free, sig=(i == 3))
                    o3 = b.t[:, :].rearrange("p (h s) -> p h s", h=4)
                    q_TT[g] = dve(lambda hs=hs, o3=o3: V.tensor_tensor(TT[:, hs, :], TT[:, hs, :], o3, ALU.add), q2)
                    b.free = [q_TT[g]]
            q_ru = []
            for par in range(2):
                b = bank()
                p0 = 64 * par
                for t in range(4):
                    hh = 2 * t + par
                    o = b.t[:, t * 64:(t + 1) * 64]
                    v_ = Vt[:, c, hh * 64:(hh + 1) * 64]
                    q = pe(lambda o=o, hh=hh, v_=v_, c=c: T.matmul(o, Sm[:, hh, 2, :], v_, start=True, stop=(c == 0)), q_sm, q_vt, b.free)
                    if c == 1:
                        q = pe(lambda o=o, t=t, p0=p0: T.matmul(o, AR[p0:p0 + 64, t, 1, 0, :], S0[p0:p0 + 64, t, :], start=False, stop=True), q_s0)
                d = RU.rearrange("p (t a v) -> p t a v", t=4, a=2)[:, :, par, :]
                o3 = b.t[:, 0:256].rearrange("p (t v) -> p t v", t=4)
                q_ru.append(act(lambda d=d, o3=o3: nc.scalar.activation(d, o3, ACT.Copy), q, early_done))
                b.free = [q_ru[-1]]
            fill(1)
            b = bank()
            for hh in range(8):
                o = b.t[:, hh * 64:(hh + 1) * 64]
                q = pe(lambda o=o, hh=hh: T.matmul(o, TT[:, hh, :], RU[:, hh * 64:(hh + 1) * 64], start=True, stop=True), q_ru, q_TT, b.free)
            q_u = act(lambda b=b: nc.scalar.activation(U, b.t[:, :], ACT.Copy), q)
            b.free = [q_u]
            fill(1)
            if c == 0:
                b = bank()
                for hh in range(8):
                    p0, t = 64 * (hh % 2), hh // 2
                    o = b.t[p0:p0 + 64, t * 64:(t + 1) * 64]
                    hd = slice(hh * 64, hh * 64 + 64)
                    pe(lambda o=o, hd=hd: T.matmul(o, Bt[:, hd], U[:, hd], start=True, stop=False), q_u, q_bt, b.free, sig=False)
                    q = pe(lambda o=o, hd=hd: T.matmul(o, Kt[:, hd], Vt[:, 0, hd], start=False, stop=True), q_kt, q_vt)
                o3 = b.t[:, 0:256].rearrange("p (t v) -> p t v", t=4)
                q_s0 = dve(lambda o3=o3: V.tensor_tensor(S0, o3, wide(fac[:, 1, :], 64), ALU.mult), q, q_fac)
                b.free = [q_s0]
            b = bank()
            for hh in range(8):
                p0, t = 64 * (hh % 2), hh // 2
                o = b.t[p0:p0 + 64, t * P:(t + 1) * P]
                hd = slice(hh * 64, hh * 64 + 64)
                pe(lambda o=o, hd=hd, hh=hh, c=c: T.matmul(o, Vt[:, c, hd], Sm[:, hh, 3, :], start=True, stop=False), q_u, b.free, sig=False)
                if c == 1:
                    pe(lambda o=o, t=t, p0=p0: T.matmul(o, S0[p0:p0 + 64, t, :], AR[p0:p0 + 64, t, 1, 1, :], start=False, stop=False), sig=False)
                q = pe(lambda o=o, hd=hd, hh=hh: T.matmul(o, U[:, hd], Sm[:, hh, 1, :], start=False, stop=True))
            prevU = [q]
            o3 = b.t[:, :].rearrange("p (t s) -> p t s", t=4)
            q_y.append(act(lambda b=b, o3=o3, c=c: nc.scalar.activation(Y[:, :, c * P:(c + 1) * P], o3, ACT.Copy), q, early_done))
            b.free = [q_y[-1]]

        q_gain, q_bias = [[], []], [[], []]
        for t in range(4):
            f = dve(lambda t=t: V.scalar_tensor_tensor(bon[:, t, :], bon[:, t, :], vcol("ln_b", t), gg[:, t, :], ALU.add, ALU.mult), q_bon, q_g)
            q_bias[t // 2].append(f)
            q_gain[t // 2].append(dve(lambda t=t: V.tensor_scalar(gg[:, t, :], gg[:, t, :], vcol("ln_g", t), None, ALU.mult), f))
        finish()
        ya = Acts(a_hi[:, 4:8, :], a_lo[:, 4:8, :])
        ybA = Acts(a_hi[:, 0:4, :], a_lo[:, 0:4, :])
        to_acts(yb, [q_yb, q_yb], ybA, 4, wait_free=(q_gates["pe"],))
        q_h = [Halves(), Halves()]
        q_b = {}

        def branch_b():
            for c in range(2):
                bb, tb = yield from stream(f"bb{c}", 4, ybA)
                for j in range(2):
                    d, gb = h[:, j, c * 512:(c + 1) * 512], gates[:, j, 1024 + c * 512:1024 + (c + 1) * 512]
                    q_b[c, j] = dve(lambda d=d, gb=gb, b=bb[j]: V.tensor_tensor(d, b.t[:, :], gb, ALU.mult), tb[j], q_gates[2 + c, j])
                    bb[j].free = [q_b[c, j]]

        fillers.append(branch_b())
        q_c = []
        for kb, (b, qb) in enumerate(per_head_sums(Y, q_y)):
            o3 = b.t[:, :].rearrange("p (k s) -> p k s", k=2)
            f = dve(lambda o3=o3, kb=kb: V.scalar_tensor_tensor(Y[:, 2 * kb:2 * kb + 2, :], o3, -1.0 / 64, Y[:, 2 * kb:2 * kb + 2, :], ALU.mult, ALU.add), qb)
            b.free = [f]
            q_c.append(f)
        q = [act(lambda kb=kb: nc.scalar.activation(Y2[:, 2 * kb:2 * kb + 2, :], Y[:, 2 * kb:2 * kb + 2, :], ACT.Square), q_c[kb]) for kb in range(2)]
        q_yg = []
        for kb in range(2):
            k2 = slice(2 * kb, 2 * kb + 2)
            q_yg.append(pool(lambda k2=k2: G.tensor_tensor(Y[:, k2, :], Y[:, k2, :], gg[:, k2, :], ALU.mult), q[kb], q_gain[kb]))
        fill(1)
        b, q = head_sums(Y2, q)
        f = act(lambda b=b: nc.scalar.activation(r8[:, :], b.t[0:8, 0:S], ACT.Sqrt, bias=eps[0:8, 1:2], scale=1.0 / 64), q, q_eps)
        b.free = [f]
        f = dve(lambda: V.reciprocal(r8[:, :], r8[:, :]), f)
        fill(1)
        q_n = []
        for kb, (b, qb) in enumerate(list(head_spread(f))):
            o3 = b.t[:, :].rearrange("p (k s) -> p k s", k=2)
            y2, k2 = Y[:, 2 * kb:2 * kb + 2, :], slice(2 * kb, 2 * kb + 2)
            q = dve(lambda y2=y2, o3=o3: V.tensor_tensor(y2, y2, o3, ALU.mult), qb, q_yg[kb])
            b.free = [q]
            q = dve(lambda y2=y2, k2=k2: V.tensor_tensor(y2, y2, bon[:, k2, :], ALU.add), q, q_bias[kb])
            hi = ya.hi[:, k2, :]
            q_n.append(act(lambda y2=y2, hi=hi: nc.scalar.activation(hi, y2, ACT.Copy), q, q_gates["pe"]))
        for kb in range(2):
            y2, k2 = Y[:, 2 * kb:2 * kb + 2, :], slice(2 * kb, 2 * kb + 2)
            hi, lo = ya.hi[:, k2, :], ya.lo[:, k2, :]
            ya.tok[2 * kb] = ya.tok[2 * kb + 1] = dve(
                lambda y2=y2, hi=hi, lo=lo: V.tensor_tensor(lo, y2, hi.bitcast(F32), ALU.subtract), q_n[kb])
        finish()

        for c in range(2):
            ba, ta = whole(stream(f"ba{c}", 4, ya))
            for j in range(2):
                d, t2 = h[:, j, c * 512:(c + 1) * 512], view(52 + 2 * (2 * c + j), 512)
                ga = gates[:, j, c * 512:(c + 1) * 512]
                f = dve(lambda t2=t2, ga=ga, b=ba[j]: V.tensor_tensor(t2, b.t[:, :], ga, ALU.mult), ta[j], q_gates[c, j])
                ba[j].free = [f]
                q_h[j].append([dve(lambda d=d, t2=t2: V.tensor_tensor(d, d, t2, ALU.add), f, q_b[c, j])])
        to_acts(h, q_h, main, 8)

        def residual(names, nk, acts, q_x, first, between=None):
            def add(c, j, banks, toks):
                xs = x[:, j, c * 512:(c + 1) * 512]
                f = dve(lambda: V.tensor_tensor(xs, xs, banks[j].t[:, :], ALU.add), toks[j])
                banks[j].free = [f]
                q_x[j].append([f])

            banks, toks = whole(stream(names[0], nk, acts))
            for j in range(2):
                add(0, j, banks, toks)
            if between is not None:
                pending.append(between)
            whole(stream(names[1], nk, acts, {(0, NS - 1): lambda b_, t_: add(1, 0, b_, t_), (1, 1): lambda b_, t_: first(),
                                              (1, NS - 1): lambda b_, t_: add(1, 1, b_, t_)}))
            split_next()
            split_next()

        q_x1 = [Halves(), Halves()]
        first, second = turnover(q_x1, "norm2_g", 0)
        residual(["wo0", "wo1"], 8, main, q_x1, first)
        s1.close()

        s3 = ExitStack()

        def hidden(name, stack):
            return Acts(sb(name + "_hi", [P, 22, S], F32R, stack)[:, :, :], sb(name + "_lo", [P, 22, S], F32R, stack)[:, :, :])

        ffn = hidden("f0", s3)
        at_ = [sb(f"at{i}", [P, 2, 512], F32, s3) for i in range(2)]
        aT = [sb(f"aT{i}", [P, 2, S], F32, s3) for i in range(2)]
        cv = [sb(f"cv{i}", [P, 2, S], F32, s3) for i in range(2)]
        at_free = [[], []]
        cv_free = [[], []]
        aT_free = [[], []]

        def take(banks, toks, dst, free):
            qs = []
            for j in range(2):
                q = normed(dst[:, j, :], banks[j].t[:, :], ACT.Copy, j, toks[j], free)
                banks[j].free = [q]
                qs.append(q)
            return qs

        def conv_tiles(k0, na, a_src, qa, ca, b_src, qb, cb):
            n = na // 2
            bk, q_a, q_b, q_cv, q_ge, q_pr, q_hi = ({} for _ in range(7))

            def across(u):
                bk[u] = (bank(), bank())
                for b, src, rdy, c0, res in ((bk[u][0], a_src, qa, ca, q_a), (bk[u][1], b_src, qb, cb, q_b)):
                    b.held = True
                    for sub in range(2):
                        for j in range(2):
                            q = transpose(b.t[:, sub * S + j * P:sub * S + (j + 1) * P],
                                          src[:, j, c0 + (2 * u + sub) * P:c0 + (2 * u + sub + 1) * P], P,
                                          rdy[j], b.free, sig=(sub == 1 and j == 1))
                    res[u] = q
                if u == n - 1:
                    at_free[0] = at_free[1] = [q_a[u], q_b[u]]

            def copy_a(u):
                b = bk[u][0]
                a3 = b.t[:, :].rearrange("p (k s) -> p k s", k=2)
                q_a[u] = act(lambda: nc.scalar.activation(aT[u][:, :, :], a3, ACT.Copy), q_a[u], aT_free[u])
                b.free, b.held = [q_a[u]], False

            def convolve(u):
                q_cv[u] = []
                for sub in range(2):
                    k = k0 + 2 * u + sub
                    a_, c_ = aT[u][:, sub, :], cv[u][:, sub, :]
                    w0, w1, w2, bi = (vcol(n_, k) for n_ in ("conv_w0", "conv_w1", "conv_w2", "conv_b"))
                    f = dve(lambda a_=a_, c_=c_, w2=w2, bi=bi: V.tensor_scalar(c_, a_, w2, bi, ALU.mult, ALU.add), q_a[u], cv_free[u])
                    f = dve(lambda a_=a_, c_=c_, w1=w1: V.scalar_tensor_tensor(
                        c_[:, 1:S], a_[:, 0:S - 1], w1, c_[:, 1:S], ALU.mult, ALU.add), f)
                    q_cv[u].append(dve(lambda a_=a_, c_=c_, w0=w0: V.scalar_tensor_tensor(
                        c_[:, 2:S], a_[:, 0:S - 2], w0, c_[:, 2:S], ALU.mult, ALU.add), f))
                aT_free[u] = q_cv[u]

            def gelu(u):
                q_ge[u] = act(lambda: nc.scalar.activation(cv[u][:, :, :], cv[u][:, :, :], ACT.Gelu), q_cv[u])

            def gate(u):
                b = bk[u][1]
                b3 = b.t[:, :].rearrange("p (k s) -> p k s", k=2)
                q_pr[u] = dve(lambda: V.tensor_tensor(cv[u][:, :, :], cv[u][:, :, :], b3, ALU.mult), q_ge[u], q_b[u])
                b.free, b.held = [q_pr[u]], False

            def part_hi(u):
                hi = ffn.hi[:, k0 + 2 * u:k0 + 2 * u + 2, :]
                q_hi[u] = act(lambda: nc.scalar.activation(hi, cv[u][:, :, :], ACT.Copy), q_pr[u])

            def part_lo(u):
                k = k0 + 2 * u
                hi, lo = ffn.hi[:, k:k + 2, :], ffn.lo[:, k:k + 2, :]
                f = dve(lambda: V.tensor_tensor(lo, cv[u][:, :, :], hi.bitcast(F32), ALU.subtract), q_hi[u])
                cv_free[u] = [f]
                ffn.tok[k] = ffn.tok[k + 1] = f

            stages = [across, copy_a, convolve, gelu, gate, part_hi, part_lo]
            for step in range(len(stages) + n - 1):
                for u in range(n):
                    if 0 <= step - u < len(stages):
                        stages[step - u](u)
                yield

        for i in range(5):
            banks, toks = whole(stream(f"ua{i}", 8, main, {(0, 0): lambda b_, t_, f=second: f()} if i == 0 else None))
            qa = take(banks, toks, at_[0], at_free[0])
            banks, toks = whole(stream(f"ub{i}", 8, main))
            settle()
            qb = take(banks, toks, at_[1], at_free[1])
            background.append(conv_tiles(4 * i, 4, at_[0], qa, 0, at_[1], qb, 0))
        banks, toks = whole(stream("ut", 8, main))
        qa = take(banks, toks, at_[0], at_free[0])
        settle()
        background.append(conv_tiles(20, 2, at_[0], qa, 0, at_[0], qa, 256))
        q_x2 = [Halves(), Halves()]
        first, second = turnover(q_x2, "mix_pre", 0, early=(0, 1))
        residual(["dn0", "dn1"], 22, ffn, q_x2, first,
                 lambda: to_acts(x, q_x2, main, 8, gain=lambda k: vcol("mix_pre", k), kbs=[0, 1]))
        s3.close()

        gain = [sb("gain0", [P, D])]
        ngain = [0]

        def load_gain(free):
            i = ngain[0]
            ngain[0] += 1
            g = gain[0]
            return g, dma(g[:, :], A["post"][i:i + 1, :].to_broadcast([P, D]), s_gain, free)

        gfree = [[]]
        sq_last = []

        def postnorm(names, nk, acts, xready, then=None, begun=None):
            g, qg = load_gain(gfree[0])
            ss, qt_ = [[], []], [[], []]
            done = [Halves(), Halves()]

            def take_in(c, j, banks, toks, between=None):
                cols = slice(c * 512, (c + 1) * 512)
                b = banks[j]

                def square(*waits):
                    f = act(lambda: nc.scalar.activation(sqj[:, :], b.t[:, :], ACT.Square,
                                                         accum_out=st[:, 40 + 2 * j + c:41 + 2 * j + c]), toks[j], sq_last, *waits)
                    sq_last[:] = [f]
                    ss[j].append(f)
                    return f

                def times(*waits):
                    f = dve(lambda: V.tensor_tensor(h[:, j, cols], b.t[:, :], g[:, cols], ALU.mult), toks[j], qg, *waits)
                    qt_[j].append(f)
                    return f

                if between is None:
                    b.free = [times(square())]
                else:
                    f = times()
                    between()
                    b.free = [square(f)]

            def close(j):
                a, r = st[:, 44 + j:45 + j], st[:, 46 + j:47 + j]
                q = dve(lambda: V.tensor_tensor(a, st[:, 40 + 2 * j:41 + 2 * j], st[:, 41 + 2 * j:42 + 2 * j], ALU.add), ss[j])
                q = rsqrt(r, a, 1, 1.0 / D, 1e-6, q)
                if j == 1:
                    split_next()
                for c in range(2):
                    hs, xs = h[:, j, c * 512:(c + 1) * 512], x[:, j, c * 512:(c + 1) * 512]
                    done[j].append([dve(lambda hs=hs, xs=xs: V.scalar_tensor_tensor(xs, hs, r, xs, ALU.mult, ALU.add), q, qt_[j], xready)])

            def half_way(banks, toks):
                take_in(1, 0, banks, toks)
                close(0)

            banks, toks = whole(begun or stream(names[0], nk, acts))
            for j in range(2):
                take_in(0, j, banks, toks)
            first, second = turnover(done, *then) if then is not None else (lambda: None, None)
            banks, toks = whole(stream(names[1], nk, acts, {(0, NS - 1): half_way, (1, 2): lambda b_, t_: split_next(pool)}))
            take_in(1, 1, banks, toks, first)
            close(1)
            gfree[0] = [qt_]
            norm["h"] = [done]
            return done, second

        sqj = sb("sqj", [P, 512])

        def swiglu(l, second, then=None):
            s5 = ExitStack()
            ffn = hidden(f"f{l + 1}", s5)
            sg = [h[:, :, i * 512:(i + 1) * 512] for i in range(2)]
            sg_free = [[], []]

            def groups(i, qp):
                to_acts_at(sg[i % 2], qp, 4, 4 * i)

            def to_acts_at(src, qp, nk_, k0):
                to_acts(src, qp, ffn, nk_, k0=k0)
                sg_free[(k0 // 4) % 2] = [ffn.tok[k0 + nk_ - 1]]

            for i in range(5):
                banks, toks = whole(stream(f"{l}ug{i}", 8, main, {(0, 2): lambda b_, t_: second()} if i == 0 else None))
                s_ = sg[i % 2]
                qs = []
                for j in range(2):
                    q = normed(s_[:, j, :], banks[j].t[:, :], ACT.Silu, j, toks[j], sg_free[i % 2])
                    banks[j].free = [q]
                    qs.append(q)
                banks, toks = whole(stream(f"{l}uu{i}", 8, main))
                qp = []
                for j in range(2):
                    q = dve(lambda j=j, b=banks[j], s_=s_: V.scalar_tensor_tensor(s_[:, j, :], b.t[:, :], norm["r"][j], s_[:, j, :], ALU.mult, ALU.mult), toks[j], qs[j])
                    banks[j].free = [q]
                    qp.append(q)
                pending.append(lambda i=i, qp=qp: groups(i, qp))
            banks, toks = whole(stream(f"{l}ut", 8, main))
            s_ = sg[1]
            qp = []
            for j in range(2):
                q = normed(s_[:, j, 0:256], banks[j].t[:, 0:256], ACT.Silu, j, toks[j], sg_free[1])
                q = dve(lambda j=j, b=banks[j]: V.scalar_tensor_tensor(
                    s_[:, j, 0:256], b.t[:, 256:512], norm["r"][j], s_[:, j, 0:256], ALU.mult, ALU.mult), q)
                banks[j].free = [q]
                qp.append(q)
            to_acts(s_, qp, ffn, 2, k0=20)
            res = postnorm([f"{l}dn0", f"{l}dn1"], 22, ffn, [], then)
            s5.close()
            return res

        s4_ = ExitStack()
        fq, fk = sb("fq", [P, 2, D], F32, s4_), sb("fk", [P, 2, D], F32, s4_)
        fv = sb("fv", [P, 2, D], F32, s4_)
        fgt = sb("fgt", [P, 2, D], F32, s4_)
        fo = fq
        wf = sb("wf", [P, 8, 16], F32, s4_)
        fprob = [sb(f"fprob{i}", [P, 384], F32, s4_) for i in range(3)]
        fprobT = [sb(f"fprobT{i}", [P, 384], F32, s4_) for i in range(2)]
        fc = sb("fc", [16, 4, S], F32, s4_)
        cqt = sb("cqt", [P, 2, 16], F32, s4_)
        frs = sb("frs", [P, 2, 16], F32, s4_)
        fmx = sb("fmx", [P, 3, 2], F32, s4_)
        fnb = sb("fnb", [P, 3, 2], F32, s4_)
        fgq = sb("fgq", [P, 1], F32, s4_)
        q_wf = dma(wf[:, :, :], A["wf"], s_wf, q_x2)
        q_fgq = dve(lambda: V.tensor_scalar(fgq[:, :], vcol("fox_g", 0), 0.125, None, ALU.mult), q_x2)

        tabs = {}

        def forget_gates():
            for _ in range(4):
                yield
            b = bank()
            for j in range(2):
                o = b.t[:, 16 * j:16 * j + 16]
                for k in range(8):
                    for n_, a_ in enumerate((main.hi, main.lo)):
                        l = a_[:, k, j * P:(j + 1) * P].bitcast(F32)
                        q = pe(lambda k=k, l=l, n_=n_, o=o: T.matmul(o, l, wf[:, k, :], start=(k == 0 and n_ == 0), stop=(k == 7 and n_ == 1)),
                               main.tok[k], q_wf, b.free, sig=(k == 7 and n_ == 1))
            while norm["tok"] is None:
                yield
            q = [normed(cqt[:, j, :], b.t[:, 16 * j:16 * j + 16], ACT.Copy, j, q) for j in range(2)]
            b.free = [q]
            b = bank()
            for j in range(2):
                q2 = transpose(b.t[0:16, j * P:(j + 1) * P], cqt[:, j, :], P, q, b.free, sig=True)
            yield
            q = act(lambda b=b: nc.scalar.activation(f0, b.t[0:16, 0:S], ACT.Identity, bias=vcol("b_f", 0, 16)), q2)
            b.free = [q]
            q1 = dve(lambda: V.scalar_tensor_tensor(f1, f0, -1.0, f0, ALU.mult, ALU.max), q)
            yield
            q1 = act(lambda: nc.scalar.activation(f1, f1, ACT.Exp, scale=-1.0), q1)
            yield
            q1 = act(lambda: nc.scalar.activation(f1, f1, ACT.Ln, bias=eps[0:16, 2:3]), q1, q_eps)
            q2 = dve(lambda: V.tensor_scalar(f0, f0, 0.0, None, ALU.min), q)
            yield
            q2 = dve(lambda: V.tensor_tensor(f0, f0, f1, ALU.subtract), q1, q2)
            yield
            q_c = dve(lambda: V.tensor_tensor_scan(f2, eps[0:16, 2:3].to_broadcast([16, S]), f0, 0.0, ALU.mult, ALU.add), q2)
            q = dve(lambda: V.tensor_scalar(f3, f2, -1.0, None, ALU.mult), q_c)
            for n_ in range(3):
                c_ = cparts[32 * n_:32 * n_ + 16, :]
                q1 = dve(lambda c_=c_: V.tensor_copy(c_, f3), q, q_cp)
                yield
                if n_ < 2:
                    q = dve(lambda c_=c_: V.tensor_tensor(f3, f3, c_, ALU.subtract), q1)
            tabs["nc"] = q1
            tabs["c"] = q_c

        f0, f1, f2, f3 = (fc[:, i, :] for i in range(4))
        cparts = sb("cparts", [P, S], BF16, s4_)
        chead = sb("chead", [P, 16], BF16, s4_)
        cone = sb("cone", [P, 16], F32, s4_)
        q_cp = [pool(lambda: G.memset(cparts[:, :], 0.0), q_x2)]
        q = pool(lambda: G.tensor_tensor(cone[:, :], ident[:, 0:16], ident[:, 32:48], ALU.add), q_x2)
        q_cp.append(pool(lambda: G.tensor_tensor(chead[:, :], cone[:, :], ident[:, 64:80], ALU.add), q))
        background.append(forget_gates())
        fss = sb("fss", [P, 64], F32, s4_)
        frr = sb("frr", [P, 64], F32, s4_)
        fs4 = fss[:, :].rearrange("p (i j h) -> p i j h", i=2, j=2)
        fr4 = frr[:, :].rearrange("p (i j h) -> p i j h", i=2, j=2)
        tk = []
        for i, (nm, dst) in enumerate((("fq", fq), ("fk", fk))):
            for c in range(2):
                banks, toks = whole(stream(f"{nm}{c}", 8, main, {(0, 0): lambda b_, t_, f=second: f()} if nm == "fq" and c == 0 else None))
                tk += take_heads(banks, toks, dst, c * 512, [fs4[:, i, j, 8 * c:8 * c + 8] for j in range(2)], sqj[:, :])
        settle()
        q_c, q_nc = tabs["c"], tabs["nc"]
        b = bank()
        for j in range(2):
            q = transpose(b.t[:, 16 * j:16 * j + 16], f2[:, j * P:(j + 1) * P], 16, q_c, b.free, sig=(j == 1))
        q_cq = act(lambda b=b: nc.scalar.activation(cqt[:, :, :], b.t[:, 0:32].rearrange("p (j h) -> p j h", j=2), ACT.Copy), q)
        b.free = [q_cq]
        q_n = {}

        fqT, fkT = sb("fqT", [P, 8, S], F32, s4_), sb("fkT", [P, 8, S], F32, s4_)
        qk_t = []

        def fox_norms():
            yield
            q_r = rsqrt(frr[:, :], fss[:, :], 64, 1.0 / 64, 1e-6, tk)
            for j in range(2):
                q_n[0, j] = norm_heads(fq, j, 16, fr4[:, 0, j, :], None, q_r)
                yield
            for j in range(2):
                q_n[1, j] = norm_heads(fk, j, 16, fr4[:, 1, j, :], None, q_r)
                for kb in (2 * j, 2 * j + 1):
                    qk_t.extend(to_heads_T(fq, fqT, 8, [q_n[0, j] for j in range(2)], gain=fgq[:, 0:1], wait=q_fgq, kbs=[kb]))
                yield
            for kb in range(4):
                qk_t.extend(to_heads_T(fk, fkT, 8, [q_n[1, j] for j in range(2)], gain=vcol("fox_g", 1), kbs=[kb]))
                if kb % 2:
                    yield

        background.append(fox_norms())
        q_fv = []
        for c in range(2):
            banks, toks = whole(stream(f"fv{c}", 8, main))
            for j in range(2):
                q = normed(fv[:, j, c * 512:(c + 1) * 512], banks[j].t[:, :], ACT.Copy, j, toks[j])
                banks[j].free = [q]
                q_fv.append(q)
        settle()
        q_fgt = {}

        def fox_gates():
            for c in range(2):
                banks, toks = yield from stream(f"fg{c}", 8, main)
                for j in range(2):
                    o = fgt[:, j, c * 512:(c + 1) * 512]
                    q = normed(o, banks[j].t[:, :], ACT.Sigmoid, j, toks[j])
                    banks[j].free = [q]
                    q_fgt[c, j] = q
                yield

        q_o = []
        way_out = stream("fo0", 8, main)

        q_og = {}

        def gated_heads(kb):
            q_og[kb] = []
            for j in range(2):
                o, gt = fo[:, j, kb * 256:(kb + 1) * 256], fgt[:, j, kb * 256:(kb + 1) * 256]
                q_og[kb].append(dve(lambda o=o, gt=gt: V.tensor_tensor(o, o, gt, ALU.mult), q_o[kb], q_fgt[kb // 2, j]))

        def fox_out():
            gated_heads(0)
            gated_heads(1)
            yield
            to_acts(fo, q_og[0], main, 8, kbs=[0])
            yield
            to_acts(fo, q_og[1], main, 8, kbs=[1])
            gated_heads(2)
            yield
            next(way_out)
            yield
            to_acts(fo, q_og[2], main, 8, kbs=[2])
            yield
            next(way_out)
            yield

        fillers.append(fox_gates())
        fillers.append(fox_out())
        half = [0]

        def step4():
            half[0] += 1
            if (half[0] % 3 == 0 and half[0] > 9) or half[0] > 25:
                fill()

        attention(16, fqT, fkT, fv, qk_t + [q_cq, q_nc, q_cp], q_fv, fo, [p[:, :] for p in fprob], [p[:, :] for p in fprobT],
                        fmx, fnb, frs, step4, cq=lambda h_: cqt[:, :, h_],
                        ck=lambda h_, n_: (chead[0:96, h_:h_ + 1].to_broadcast([96, P]), cparts[0:96, 0:n_]), toks=q_o)
        gated_heads(3)
        finish()
        next(way_out)
        to_acts(fo, q_og[3], main, 8, kbs=[3])
        s4_.close()
        q_x3, second = postnorm(["fo0", "fo1"], 8, main, [], ("ffn_pre", 0), way_out)
        s6 = ExitStack()
        ct = sb("ct", [P, 32, P], F32, s6)
        stb = sb("stb", [P, 32, P], F32, s6)
        pr = sb("pr", [P, 16, 32], F32, s6)
        bz = sb("bz", [P, 8, 2, P], F32, s6)
        cz = sb("cz", [P, 32, 4, 32], F32, s6)
        q_bz = dma(bz[:, :, :, :], A["bz"], s_bz, q_x3)
        q_cz = dma(cz[:, :, 0:2, :], A["cz"], s_cz, q_x3)
        dt, mag, th, tr, are, aim, den, zre, zim, t1, t2, nre, i_re, i_im, th2, t3 = (pr[:, i, :] for i in range(16))
        tab = {}

        def s5_tables():
            two_pi = float(2 * np.pi)
            lre, lim = vcols("lam_re", 32), vcols("lam_im", 32)
            iota = const("iota", P)
            q = act(lambda: nc.scalar.activation(dt, vcols("log_dt", 32), ACT.Exp), q_con, q_x3)
            q1 = dve(lambda: V.tensor_tensor(t1, lre, dt, ALU.mult), q)
            tab["mag"] = q_mag = act(lambda: nc.scalar.activation(mag, t1, ACT.Exp), q1)
            yield
            q1 = dve(lambda: V.tensor_tensor(th, lim, dt, ALU.mult), q)
            q1 = dve(lambda: V.tensor_scalar(t2, th, 1 / two_pi, MAGIC, ALU.mult, ALU.add), q1, q_mag)
            q1 = dve(lambda: V.tensor_scalar(t2, t2, MAGIC, None, ALU.subtract), q1)
            q1 = dve(lambda: V.scalar_tensor_tensor(th, t2, -6.28125, th, ALU.mult, ALU.add), q1)
            q1 = dve(lambda: V.scalar_tensor_tensor(th, t2, -(two_pi - 6.28125), th, ALU.mult, ALU.add), q1)
            q_tr = dve(lambda: V.tensor_scalar(tr, th, 1 / two_pi, None, ALU.mult), q1)
            yield
            sines = []
            for g in range(4):
                c, s = ct[:, 8 * g:8 * g + 8, :], stb[:, 8 * g:8 * g + 8, :]
                q = pool(lambda g=g, s=s: G.tensor_tensor(s, wide(tr[:, 8 * g:8 * g + 8], P), iota.unsqueeze(1).to_broadcast([P, 8, P]), ALU.mult), q_tr)
                yield
                q1 = dve(lambda c=c, s=s: V.tensor_scalar(c, s, MAGIC, MAGIC, ALU.add, ALU.subtract), q)
                q = pool(lambda c=c, s=s: G.tensor_tensor(s, s, c, ALU.subtract), q1)
                yield
                yield
                q1 = dve(lambda c=c, s=s: V.scalar_tensor_tensor(c, s, -1.0, s, ALU.mult, ALU.max), q)
                yield
                q1 = dve(lambda c=c: V.tensor_scalar(c, c, -two_pi, two_pi / 4, ALU.mult, ALU.add), q1)
                yield
                q2 = dve(lambda s=s: V.tensor_scalar(s, s, two_pi, 3.1415925, ALU.mult, ALU.min), q, q1)
                yield
                q2 = dve(lambda s=s: V.tensor_scalar(s, s, -3.1415925, None, ALU.max), q2)
                yield
                sines.append((c, s, q1, q2))
            q = dve(lambda: V.tensor_scalar(t1, tr, 128.0, None, ALU.mult), q_tr, q_mag)
            q1 = dve(lambda: V.tensor_scalar(t2, t1, MAGIC, MAGIC, ALU.add, ALU.subtract), q)
            q = dve(lambda: V.tensor_tensor(t1, t1, t2, ALU.subtract), q1)
            q1 = dve(lambda: V.scalar_tensor_tensor(t2, t1, -1.0, t1, ALU.mult, ALU.max), q)
            q1 = dve(lambda: V.tensor_scalar(t2, t2, -two_pi, two_pi / 4, ALU.mult, ALU.add), q1)
            q2 = dve(lambda: V.tensor_scalar(t1, t1, two_pi, 3.1415925, ALU.mult, ALU.min), q1)
            q2 = dve(lambda: V.tensor_scalar(t1, t1, -3.1415925, None, ALU.max), q2)
            yield
            while at["use"] < sine_slab:
                yield
            q_h = [act(lambda: nc.scalar.activation(th2, t2, ACT.Sin), q1), act(lambda: nc.scalar.activation(t3, t1, ACT.Sin), q2)]
            tab["half"] = q_h
            for c, s, q1, q2 in sines:
                q_ct = act(lambda c=c: nc.scalar.activation(c, c, ACT.Sin), q1)
                q_st = act(lambda s=s: nc.scalar.activation(s, s, ACT.Sin), q2)
                yield
                yield
            tab["ct"], tab["st"] = q_ct, q_st
            q = dve(lambda: V.tensor_tensor(are, mag, ct[:, :, 1], ALU.mult), q_ct, q_mag)
            q2 = dve(lambda: V.tensor_tensor(aim, mag, stb[:, :, 1], ALU.mult), q_st, q_mag)
            q = dve(lambda: V.tensor_scalar(nre, are, 1.0, None, ALU.subtract), q)
            q3 = dve(lambda: V.tensor_tensor(t1, lre, lre, ALU.mult), q_h)
            q4 = dve(lambda: V.tensor_tensor(t2, lim, lim, ALU.mult), q_h)
            q3 = dve(lambda: V.tensor_tensor(den, t1, t2, ALU.add), q3, q4)
            q3 = dve(lambda: V.reciprocal(den, den), q3)
            yield
            q4 = dve(lambda: V.tensor_tensor(t1, nre, lre, ALU.mult), q, q3)
            q5 = dve(lambda: V.tensor_tensor(t2, aim, lim, ALU.mult), q2, q3)
            q4 = dve(lambda: V.tensor_tensor(t1, t1, t2, ALU.add), q4, q5)
            q_zr = dve(lambda: V.tensor_tensor(zre, t1, den, ALU.mult), q4, q3)
            q4 = dve(lambda: V.tensor_tensor(t1, aim, lre, ALU.mult), q_zr)
            q5 = dve(lambda: V.tensor_tensor(t2, nre, lim, ALU.mult), q_zr)
            q4 = dve(lambda: V.tensor_tensor(t1, t1, t2, ALU.subtract), q4, q5)
            q_zi = dve(lambda: V.tensor_tensor(zim, t1, den, ALU.mult), q4)
            yield
            cre, cim, c2, c3 = (cz[:, :, i, :] for i in range(4))
            q = dve(lambda: V.tensor_tensor(c2, cre, wide(zre, 32), ALU.mult), q_cz, q_zr)
            yield
            q1 = dve(lambda: V.tensor_tensor(c3, cre, wide(zim, 32), ALU.mult), q_zi, q_cz)
            yield
            q2 = dve(lambda: V.tensor_tensor(cre, cim, wide(zim, 32), ALU.mult), q, q1, q_zi)
            yield
            q = dve(lambda: V.tensor_tensor(c2, c2, cre, ALU.subtract), q, q2)
            yield
            q2 = dve(lambda: V.tensor_tensor(cim, cim, wide(zre, 32), ALU.mult), q2, q_zr)
            yield
            q1 = dve(lambda: V.scalar_tensor_tensor(c3, c3, -1.0, cim, ALU.mult, ALU.subtract), q1, q2)
            yield
            q_c0 = dve(lambda: V.tensor_scalar(cre, c2, -1.0, None, ALU.mult), q)
            tab["cz"] = [q, q1, q_c0]

        sine_slab = at["use"] + 46
        background.append(s5_tables())
        q_x4, second = swiglu(0, second, ("mix_pre", 8))
        settle()
        q_mag, q_h, q_ct, q_st, q_cz = (tab[n] for n in ("mag", "half", "ct", "st", "cz"))

        uT = sb("uT", [P, 8, S], F32, s6)
        us = h
        q_us, q_ut = [Halves(), Halves()], []
        for c in range(2):
            banks, toks = whole(stream(f"si{c}", 8, main, {(0, 2): lambda b_, t_, f=second: f()} if c == 0 else None))
            for j in range(2):
                q = normed(us[:, j, c * 512:(c + 1) * 512], banks[j].t[:, :], ACT.Copy, j, toks[j])
                banks[j].free = [q]
                q_us[j].append([q])
            if c == 0:
                pending.append(lambda: q_ut.extend(to_heads_T(us, uT, 8, q_us, kbs=[0, 1])))
        q_ut.extend(to_heads_T(us, uT, 8, q_us, kbs=[2, 3]))
        s8 = ExitStack()
        ra = [sb(f"ra{i}", [P, 2, 2, P], F32, s8) for i in range(NT)]
        rb = [sb(f"rb{i}", [P, 2, 2, P], F32, s8) for i in range(NT)]
        rz = [sb(f"rz{i}", [P, 2, 2, P], F32, s8) for i in range(2)]
        rd = [sb(f"rd{i}", [P, 2, 2, P], F32, s8) for i in range(2)]
        q_rd = [pool(lambda i=i: G.memset(rd[i][:, :, :, 0:1], 0.0), q_x4) for i in range(2)]
        last = sb("last", [P, 2, 32], F32, s8)
        ybuf = uT
        free_r = [[] for _ in range(NT)]
        free_z = [[], []]
        q_last = []
        q_y5, q_ge5, q_ini, gathered = {}, {}, {}, {}
        bu, turned, prod = {}, {}, {}

        def half_of(n):
            return slice(n // 16 * P, n // 16 * P + P)

        def pair_of(n):
            m_, q_ = n % 16 // 4, n % 4
            pair = (8 * m_ + q_, 8 * m_ + 4 + q_)
            tt = slice(pair[0], pair[1] + 1, 4)
            c4 = ct[:, tt, :].unsqueeze(2).to_broadcast([P, 2, 2, P])
            n4 = stb[:, tt, :].unsqueeze(2).to_broadcast([P, 2, 2, P])
            return pair, tt, c4, n4, ra[n % NT], rb[n % NT], rz[n % 2]

        def drive(ns):
            for n in ns:
                bu[n] = [bank(), None]
            for u_ in range(2):
                for ri in range(2):
                    for n in ns:
                        b, t = bu[n][0], pair_of(n)[0][u_]
                        p0, kt = 32 * (t % 4), t // 4
                        o = b.t[:, (2 * u_ + ri) * P:(2 * u_ + ri + 1) * P]
                        l, r = bz[p0:p0 + 32, kt, ri, :], uT[p0:p0 + 32, kt, half_of(n)]
                        bu[n][1] = pe(lambda o=o, l=l, r=r, p0=p0: T.matmul(o, l, r, start=True, stop=True, tile_position=(p0, 0)),
                                      q_ut[kt // 2], q_bz, b.free, sig=(u_ == 1 and ri == 1))

        def turn(n):
            pair, tt, c4, n4, A_, B_, Z_ = pair_of(n)
            b, q = bu.pop(n)
            b4 = b.t[:, :].rearrange("p (t r s) -> p t r s", t=2, r=2)
            q1 = dve(lambda: V.tensor_tensor(A_[:, :, :, :], b4, c4, ALU.mult), q, q_ct, free_r[n % NT])
            q2 = dve(lambda: V.tensor_tensor(B_[:, :, :, :], b4, n4, ALU.mult), q, q_st, free_r[n % NT])
            b.free = [q2]
            turned[n] = [pool(lambda: G.tensor_tensor(A_[:, :, 0, :], A_[:, :, 0, :], B_[:, :, 1, :], ALU.add), q1, q2),
                         pool(lambda: G.tensor_tensor(A_[:, :, 1, :], A_[:, :, 1, :], B_[:, :, 0, :], ALU.subtract), q1, q2)]

        def run(n):
            pair, tt, c4, n4, A_, B_, Z_ = pair_of(n)
            q3 = turned.pop(n)
            if n >= 16:
                q3 = q3 + [dve(lambda ri=ri, ini=ini: V.tensor_tensor(A_[:, :, ri, 0], A_[:, :, ri, 0], ini[:, tt], ALU.add), q3, q_ini[n % 16 // 8])
                           for ri, ini in enumerate((i_re, i_im))]
            D_ = rd[n % 2]
            m4 = mag[:, tt].unsqueeze(2).unsqueeze(3).to_broadcast([P, 2, 2, P - 1])
            qd = act(lambda: nc.scalar.activation(D_[:, :, :, 1:P], m4, ACT.Copy), q_mag, free_z[n % 2])

            def flat3(a):
                return a[:, :, :, :].rearrange("p t r s -> p (t r s)")

            q4 = dve(lambda: V.tensor_tensor_scan(flat3(Z_), flat3(D_), flat3(A_), 0.0, ALU.mult, ALU.add), q3, qd, q_rd, free_z[n % 2])
            if n < 16:
                q_last.append(act(lambda: nc.scalar.activation(last[:, :, tt], Z_[:, :, :, P - 1].rearrange("p t r -> p r t"), ACT.Copy), q4))
            q5 = dve(lambda: V.tensor_tensor(A_[:, :, :, :], Z_[:, :, :, :], c4, ALU.mult), q4)
            q6 = pool(lambda: G.tensor_tensor(B_[:, :, :, :], Z_[:, :, :, :], n4, ALU.mult), q4, q_st)
            free_z[n % 2] = [q5, q6, q_last[-1]]
            prod[n] = [q5, q6]

        def gather(ns):
            for u_ in range(2):
                for n_ in range(4):
                    for n in ns:
                        pair, tt, c4, n4, A_, B_, Z_ = pair_of(n)
                        t = pair[u_]
                        p0, kt = 32 * (t % 4), t // 4
                        yb_ = wps[n // 8]
                        o = yb_.t[p0:p0 + 32, (kt % 4) * P:(kt % 4 + 1) * P]
                        w, m = ((2, A_[:, u_, 0, :]), (0, B_[:, u_, 1, :]), (3, B_[:, u_, 0, :]), (3, A_[:, u_, 1, :]))[n_]
                        q = pe(lambda o=o, w=w, m=m, t=t, n_=n_, p0=p0: T.matmul(o, cz[:, t, w, :], m, start=(n_ == 0), stop=(n_ == 3),
                                                                                 tile_position=(0, p0)),
                               prod[n], q_cz, yb_.free, sig=(n_ == 3))
                        if n_ == 3:
                            free_r[n % NT] = gathered[n] = [q]
        def outputs(g):
            for k4 in range(4):
                kt = 4 * (g % 2) + k4
                o = wps[g].t[:, k4 * P:(k4 + 1) * P]
                q_y5[g, k4] = dve(lambda o=o, kt=kt, cols=half_of(8 * g): V.scalar_tensor_tensor(
                    ybuf[:, kt, cols], uT[:, kt, cols], vcol("d_skip", kt), o, ALU.mult, ALU.add), gathered[8 * g + 7])
            wps[g].free = [q_y5[g, 3]]
            if g >= 2:
                for kb in (2 * g - 4, 2 * g - 3):
                    y2 = ybuf[:, 2 * kb:2 * kb + 2, :]
                    q_ge5[kb] = act(lambda y2=y2: nc.scalar.activation(y2, y2, ACT.Gelu_apprx_tanh),
                                    [q_y5[g_, k4] for g_ in (g - 2, g) for k4 in range(4)])

        def parts(g):
            for kb in (2 * g - 4, 2 * g - 3):
                y2 = ybuf[:, 2 * kb:2 * kb + 2, :]
                hi, lo = main.hi[:, 2 * kb:2 * kb + 2, :], main.lo[:, 2 * kb:2 * kb + 2, :]
                q = act(lambda y2=y2, hi=hi: nc.scalar.activation(hi, y2, ACT.Copy), q_ge5[kb], q_ut)
                q = dve(lambda y2=y2, hi=hi, lo=lo: V.tensor_tensor(lo, y2, hi.bitcast(F32), ALU.subtract), q)
                main.tok[2 * kb] = main.tok[2 * kb + 1] = q

        def start(g):
            tt = slice(16 * g, 16 * g + 16)
            a, b = t1[:, tt], t2[:, tt]
            c_, s_ = th2[:, tt], t3[:, tt]
            ql = q_last[8 * g:8 * g + 8]
            q = dve(lambda: V.tensor_tensor(a, last[:, 0, tt], c_, ALU.mult), ql, q_h)
            q1 = dve(lambda: V.tensor_tensor(b, last[:, 1, tt], s_, ALU.mult), ql, q_h)
            q = dve(lambda: V.tensor_tensor(a, a, b, ALU.subtract), q, q1)
            q_i1 = dve(lambda: V.tensor_tensor(i_re[:, tt], a, mag[:, tt], ALU.mult), q)
            q = dve(lambda: V.tensor_tensor(a, last[:, 0, tt], s_, ALU.mult), q_i1)
            q1 = dve(lambda: V.tensor_tensor(b, last[:, 1, tt], c_, ALU.mult), q_i1)
            q = dve(lambda: V.tensor_tensor(a, a, b, ALU.add), q, q1)
            q_ini[g] = [q_i1, dve(lambda: V.tensor_tensor(i_im[:, tt], a, mag[:, tt], ALU.mult), q)]

        while at["split"] < at["use"] + NS:
            split_next()
        sg = []
        drive((0, 1))
        drive((2, 3))
        turn(0)
        for n in range(32):
            if n % 2 == 1 and n + 3 < 32:
                drive((n + 3, n + 4))
            if n + 1 < 32:
                turn(n + 1)
            run(n)
            if n in (12, 20, 26):
                outputs((n - 10) // 8)
            if n in (13, 21):
                start(n // 16)
            if n == 27:
                parts(2)
            if n in (29, 31):
                wpair[0] = 0
                b2 = [bank() for _ in range(2)] if n == 31 else None
                for b in b2 or ():
                    b.held = True
                sg.append(stream(f"sg{len(sg)}", 8, main, banks=b2))
                next(sg[-1])
                if n == 29:
                    next(sg[-1])
            if n % 2 == 1:
                gather([g for g in (n - 2, n - 1) if g >= 0])
        gather([31])
        outputs(3)
        parts(3)
        next(sg[1])
        q_sg = [Halves(), Halves()]

        def sigmoids(c, banks, toks):
            for j in range(2):
                o = h[:, j, c * 512:(c + 1) * 512]
                q = act(lambda o=o, b=banks[j]: nc.scalar.activation(o, b.t[:, :], ACT.Sigmoid), toks[j])
                banks[j].free = [q]
                banks[j].held = False
                q_sg[j].append([q])

        def gated(kb):
            b = bank()
            for sub in range(2):
                for j in range(2):
                    q = transpose(b.t[:, sub * S + j * P:sub * S + (j + 1) * P], h[:, j, (2 * kb + sub) * P:(2 * kb + sub + 1) * P], P,
                                  part(q_sg[j], kb), b.free, sig=(sub == 1 and j == 1))
            y2 = ybuf[:, 2 * kb:2 * kb + 2, :]
            hi, lo = main.hi[:, 2 * kb:2 * kb + 2, :], main.lo[:, 2 * kb:2 * kb + 2, :]
            o3 = b.t[:, :].rearrange("p (k s) -> p k s", k=2)
            q = dve(lambda: V.tensor_tensor(y2, y2, o3, ALU.mult), q)
            b.free = [q]
            q = act(lambda: nc.scalar.activation(hi, y2, ACT.Copy), q)
            main.tok[2 * kb] = main.tok[2 * kb + 1] = [q, dve(lambda: V.tensor_tensor(lo, y2, hi.bitcast(F32), ALU.subtract), q)]

        sigmoids(0, *whole(sg[0]))
        next(sg[1])
        gated(0)
        gated(1)
        sigmoids(1, *whole(sg[1]))
        soon.append(lambda: (gated(2), gated(3)))
        post = postnorm(["so0", "so1"], 8, main, [], ("ffn_pre", 8))
        s8.close()
        s6.close()
        q_x5, second = post
        q_x6, _ = swiglu(1, second)
        for c in range(2):
            for j in range(2):
                cols = slice(c * 512, (c + 1) * 512)
                dma(out[j * P:(j + 1) * P, cols], x[:, j, cols], s_out, q_x6[j][c])

        block = ctx.enter_context(nc.Block())

        @block.sync
        def _(eng):
            seen = {}
            for fn, waits, s in sp_items:
                for sm, v in waits:
                    if seen.get(id(sm), 0) < v:
                        eng.wait_ge(sm, v)
                        seen[id(sm)] = v
                fn().then_inc(s, 16)
            eng.wait_ge(s_out, dma_sems[s_out])

        @block.scalar
        def _(eng):
            act.play(eng)

        @block.vector
        def _(eng):
            dve.play(eng)

        @block.gpsimd
        def _(eng):
            pool.play(eng)

        @block.tensor
        def _(eng):
            pe.play(eng)


def constants():
    t = np.arange(P)
    con = np.zeros((P, NCON), np.float32)

    def put(name, a):
        con[:, CON_AT[name]:CON_AT[name] + a.shape[1]] = a

    def level(n):
        same = (t[:, None] // (2 * n)) == (t[None, :] // (2 * n))
        return (same & (t[:, None] % (2 * n) < n) & (t[None, :] % (2 * n) >= n)).astype(np.float32)

    put("ident", np.eye(P, dtype=np.float32))
    put("bones", np.kron(np.eye(2), np.ones((64, 64))).astype(np.float32))
    put("lev0", level(1))
    put("levs", np.concatenate([level(2 << l) for l in range(6)], 1))
    strict = (t[:, None] < t[None, :]).astype(np.float32)
    incl = (t[:, None] <= t[None, :]).astype(np.float32)
    put("mask2", np.concatenate([strict, incl], 1))
    head = (np.arange(512) // 64 == np.arange(8)[:, None]).astype(np.float32)
    put("hsel", head.T.reshape(4, P, 8).transpose(1, 0, 2).reshape(P, 32))
    put("hspread", np.concatenate([head, np.zeros((P - 8, 512), np.float32)], 0))
    put("iota", np.broadcast_to(t.astype(np.float32), (P, P)))
    half = 8
    inv = np.float32(500000.0) ** (-np.arange(half, dtype=np.float32) / np.float32(half))
    put("invf", np.broadcast_to(inv.astype(np.float32), (P, half)))
    words = np.concatenate([np.eye(P), np.zeros((P, P)), np.where(t[None, :] > t[:, None], -1e30, 0.0)], 1).astype(np.float32)
    return con, (words.view(np.uint32) >> 16).astype(np.uint16).view(np.int16)


def arrays_of(inputs):
    I = {k: np.asarray(v) for k, v in inputs.items()}
    out = {"x": np.ascontiguousarray(I["x"][0])}
    con, out["mask"] = constants()
    out["ident"], out["con"] = con[:, 0:P], con[:, P:]

    def cols(a, n):
        a = a.reshape(-1)
        if a.size < n * P:
            a = np.concatenate([a, np.zeros(n * P - a.size, a.dtype)])
        return a.reshape(n, P).T

    cw = I["ffn_conv_w"][0]
    parts = {
        "norm1_g": I["norm1_g"], "rwkv_mu": I["rwkv_mu"], "decay_bias": I["decay_bias"], "aaa_bias": I["aaa_bias"],
        "k_k": I["rwkv_k_k"], "k_a": I["rwkv_k_a"], "r_k": I["rwkv_r_k"], "ln_g": I["rwkv_ln_g"], "ln_b": I["rwkv_ln_b"],
        "norm2_g": I["norm2_g"], "conv_w0": cw[0], "conv_w1": cw[1], "conv_w2": cw[2], "conv_b": I["ffn_conv_b"],
        "b_f": I["fox_b_f_2"], "log_dt": np.repeat(I["s5_log_dt_2"].reshape(-1), 64), "lam_re": I["s5_lam_re_2"],
        "lam_im": I["s5_lam_im_2"], "d_skip": I["s5_d_2"], "mix_pre": I["mix_pre_gain_2"], "ffn_pre": I["ffn_pre_gain_2"],
        "fox_g": np.concatenate([I[n].reshape(-1) for n in ("fox_q_gain_2", "fox_q_gain_2", "fox_k_gain_2", "fox_k_gain_2")]),
    }
    out["vec"] = np.concatenate([cols(parts[n], k) for n, k in VEC_TILES], 1)
    rows = lambda a: np.broadcast_to(a.reshape(1, -1), (P, a.size))
    out["qkg"] = np.stack([rows(I["q_norm_g"]), rows(I["k_norm_g"]), rows(I["q_norm_g"]), rows(I["k_norm_g"])], 1)
    out["posi"] = I["positions"].reshape(2, P).T
    out["wlora"] = np.concatenate([np.concatenate([I["w_decay_up"][0], I["w_aaa_up"][0]], 0), I["w_gate_up"][0][:P]], 1)
    out["wg2"] = I["w_gate_up"][0][P:]
    fw = I["fox_w_in_2"][0]
    out["wf"] = fw[:, 4096:].reshape(8, P, 16).transpose(1, 0, 2)
    mp, fp = I["mix_post_gain_2"], I["ffn_post_gain_2"]
    out["post"] = np.stack([mp[0], fp[0], mp[1], fp[1]])
    bz = np.zeros((8, 4, 2, 16, 2, 2, 64), np.float32)
    cz = np.zeros((32, 2, 2, 64, 2, 16), np.float32)
    for ri, (bn, cn) in enumerate((("s5_b_re_2", "s5_c_re_2"), ("s5_b_im_2", "s5_c_im_2"))):
        b = I[bn][0].reshape(8, 4, 2, 64, 16).transpose(0, 1, 2, 4, 3)
        c = I[cn][0].reshape(32, 2, 16, 64).transpose(0, 1, 3, 2)
        for g in range(2):
            bz[:, :, g, :, ri, g, :] = b[:, :, g]
            cz[:, ri, g, :, g, :] = c[:, g]
    out["bz"] = bz.reshape(8, P, 2, P).transpose(1, 0, 2, 3)
    out["cz"] = cz.reshape(32, 2, P, 32).transpose(2, 0, 1, 3)

    wi = I["w_in"][0]
    r0, m0 = 0, 1824
    g0 = m0 + 1536
    src = {}
    for i, n in enumerate(("mq", "mk", "mv")):
        src[n] = wi[:, m0 + 512 * i:m0 + 512 * (i + 1)]
    for i, n in enumerate(("wr", "wk", "wv")):
        src[n] = wi[:, 512 * i:512 * (i + 1)]
    src["wl"] = wi[:, 1536:1824]
    for i in range(4):
        src[f"g{i}"] = wi[:, g0 + 512 * i:g0 + 512 * (i + 1)]

    def halves(n, a):
        for i in range(2):
            src[f"{n}{i}"] = a[:, 512 * i:512 * (i + 1)]

    def updown(pa, pb, pt, a, b):
        for i in range(5):
            src[f"{pa}{i}"] = a[:, 512 * i:512 * (i + 1)]
            src[f"{pb}{i}"] = b[:, 512 * i:512 * (i + 1)]
        src[pt] = np.concatenate([a[:, 2560:], b[:, 2560:]], 1)

    halves("ba", I["w_branch_a"][0])
    halves("bb", I["w_branch_b"][0])
    halves("wo", I["w_out"][0])
    up = I["w_ffn_up"][0]
    updown("ua", "ub", "ut", up[:, :FF], up[:, FF:])
    halves("dn", I["w_ffn_down"][0])
    for i, n in enumerate(("fq", "fk", "fv", "fg")):
        halves(n, fw[:, 1024 * i:1024 * (i + 1)])
    halves("fo", I["fox_w_out_2"][0])
    halves("si", I["s5_w_in_2"][0])
    halves("sg", I["s5_w_glu_2"][0])
    halves("so", I["s5_w_out_2"][0])
    for l in range(2):
        updown(f"{l}ug", f"{l}uu", f"{l}ut", I["ffn_w_gate_2"][l], I["ffn_w_up_2"][l])
        halves(f"{l}dn", I["ffn_w_down_2"][l])
    for name, nk, w in stream_plan():
        a = src[name]
        assert a.shape == (nk * P, w), (name, a.shape)
        out["w_" + name] = a.reshape(nk // 2, 2, P, w).transpose(0, 2, 1, 3).reshape(nk // 2, P, 2 * w)
    return {k: np.ascontiguousarray(v) for k, v in out.items()}


def kernel(**inputs):
    import concourse.bacc as bacc
    from concourse.bass_utils import run_bass_kernel_spmd

    arrays = arrays_of(inputs)
    nc = bacc.Bacc("TRN2", target_bir_lowering=False, num_devices=1)
    A = {k: nc.dram_tensor("in_" + k, a.shape, mybir.dt.from_np(a.dtype), kind="ExternalInput").ap() for k, a in arrays.items()}
    out = nc.dram_tensor("out_x", (S, D), F32, kind="ExternalOutput").ap()
    program(nc, A, out)
    r = run_bass_kernel_spmd(nc, [{"in_" + k: a for k, a in arrays.items()}], core_ids=[0])
    return r.results[0]["out_x"].reshape(1, S, D)
```
